# Optimizing a Trainium2 kernel written in Bass

```python
import math
import jax, jax.numpy as jnp
from jax import lax
import numpy as np

D_MODEL = 1024
BATCH = 1
SEQ = 512
DEPTH = 2

HEAD_DIM = 64
SB_HEADS = 4
MLA_HEADS = 4
RWKV_HEADS = 8
SB_WIDTH = SB_HEADS * HEAD_DIM
MLA_WIDTH = MLA_HEADS * HEAD_DIM
RWKV_WIDTH = RWKV_HEADS * HEAD_DIM
MIX_WIDTH = SB_WIDTH + MLA_WIDTH + RWKV_WIDTH

MLA_Q_LORA = 192
MLA_KV_LORA = 128
MLA_NOPE_DIM = 64
MLA_ROPE_DIM = 32
MLA_V_DIM = HEAD_DIM
ROPE_THETA = 10000.0

RWKV_DECAY_LORA = 64
RWKV_AAA_LORA = 64
RWKV_GATE_LORA = 128
RWKV_GN_EPS = 64e-5

SB_COLS = 3 * SB_WIDTH
MLA_COLS = MLA_Q_LORA + MLA_KV_LORA + MLA_ROPE_DIM
RWKV_COLS = 3 * RWKV_WIDTH + RWKV_DECAY_LORA + RWKV_AAA_LORA + RWKV_GATE_LORA
IN_COLS = SB_COLS + MLA_COLS + RWKV_COLS

D_FF = 2816
CONV_WIDTH = 3

Q_BLOCK = 128
LN_EPS = 1e-5
RMS_EPS = 1e-6
DEEPNORM_ALPHA = (2 * DEPTH) ** 0.25
DEEPNORM_BETA = (8 * DEPTH) ** -0.25


def layer_norm(x, g, b):
    xf = x.astype(jnp.float32)
    mu = jnp.mean(xf, axis=-1, keepdims=True)
    var = jnp.mean(jnp.square(xf - mu), axis=-1, keepdims=True)
    return ((xf - mu) * lax.rsqrt(var + LN_EPS) * g + b).astype(x.dtype)

def rms_norm(x, g):
    xf = x.astype(jnp.float32)
    return (xf * lax.rsqrt(jnp.mean(jnp.square(xf), axis=-1, keepdims=True) + RMS_EPS) * g).astype(x.dtype)

def split_heads(t, n_heads):
    b, s, _ = t.shape
    return t.reshape(b, s, n_heads, -1).transpose(0, 2, 1, 3)

def merge_heads(t):
    b, h, s, d = t.shape
    return t.transpose(0, 2, 1, 3).reshape(b, s, h * d)

def query_block_map(block_fn, q):
    b, h, s, d = q.shape
    nb = s // Q_BLOCK
    qb = q.reshape(b, h, nb, Q_BLOCK, d).transpose(2, 0, 1, 3, 4)
    starts = jnp.arange(nb, dtype=jnp.int32) * Q_BLOCK
    out = lax.map(lambda a: block_fn(a[0], a[1]), (qb, starts))
    return out.transpose(1, 2, 0, 3, 4).reshape(b, h, s, -1)

def stick_breaking_attention(q, k, v):
    s_len = k.shape[2]
    scale = q.shape[-1] ** -0.5
    kpos = jnp.arange(s_len, dtype=jnp.int32)

    def block(qb, start):
        z = jnp.einsum('bhqd,bhkd->bhqk', qb, k).astype(jnp.float32) * scale
        qpos = start + jnp.arange(Q_BLOCK, dtype=jnp.int32)
        past = kpos[None, :] < qpos[:, None]
        log_keep = jnp.where(past, jax.nn.log_sigmoid(-z), 0.0)
        log_later = lax.cumsum(log_keep, axis=3, reverse=True) - log_keep
        w = jnp.where(past, jnp.exp(jax.nn.log_sigmoid(z) + log_later), 0.0)
        return jnp.einsum('bhqk,bhkd->bhqd', w.astype(v.dtype), v)

    return query_block_map(block, q)

def causal_softmax_attention(q, k, v, scale):
    s_len = k.shape[2]
    kpos = jnp.arange(s_len, dtype=jnp.int32)
    neg = jnp.finfo(jnp.float32).min

    def block(qb, start):
        s = jnp.einsum('bhqd,bhkd->bhqk', qb, k).astype(jnp.float32) * scale
        qpos = start + jnp.arange(Q_BLOCK, dtype=jnp.int32)
        s = jnp.where(kpos[None, :] <= qpos[:, None], s, neg)
        p = jax.nn.softmax(s, axis=-1)
        return jnp.einsum('bhqk,bhkd->bhqd', p.astype(v.dtype), v)

    return query_block_map(block, q)

def rope_tables(s_len, dim):
    inv_freq = 1.0 / (ROPE_THETA ** (jnp.arange(0, dim, 2, dtype=jnp.float32) / dim))
    ang = jnp.arange(s_len, dtype=jnp.float32)[:, None] * inv_freq[None, :]
    return jnp.cos(ang), jnp.sin(ang)

def apply_rope(t, cos, sin):
    t1, t2 = jnp.split(t, 2, axis=-1)
    cos = cos.astype(t.dtype)
    sin = sin.astype(t.dtype)
    return jnp.concatenate([t1 * cos - t2 * sin, t2 * cos + t1 * sin], axis=-1)

def mla_mixer(cols, q_norm, w_uq, kv_norm, w_ukv):
    c_q, c_kv, k_rope = jnp.split(cols, [MLA_Q_LORA, MLA_Q_LORA + MLA_KV_LORA], axis=-1)
    q = split_heads(rms_norm(c_q, q_norm) @ w_uq, MLA_HEADS)
    kv = split_heads(rms_norm(c_kv, kv_norm) @ w_ukv, MLA_HEADS)
    q_nope, q_rope = jnp.split(q, [MLA_NOPE_DIM], axis=-1)
    k_nope, v = jnp.split(kv, [MLA_NOPE_DIM], axis=-1)
    cos, sin = rope_tables(cols.shape[1], MLA_ROPE_DIM)
    q_rope = apply_rope(q_rope, cos, sin)
    k_rope = apply_rope(k_rope[:, None], cos, sin)
    q = jnp.concatenate([q_nope, q_rope], axis=-1)
    k = jnp.concatenate([k_nope, jnp.broadcast_to(k_rope, k_nope.shape[:-1] + (MLA_ROPE_DIM,))], axis=-1)
    out = causal_softmax_attention(q, k, v, (MLA_NOPE_DIM + MLA_ROPE_DIM) ** -0.5)
    return merge_heads(out)

def token_shift_mix(p, mu):
    prev = jnp.pad(p, ((0, 0), (1, 0), (0, 0)))[:, :-1]
    return p + (prev - p) * mu

def rwkv7_mixer(cols, mu, w0, w2, a0, a2, g2, k_k, k_a, r_k, gn_g, gn_b):
    b, s, _ = cols.shape
    p = token_shift_mix(cols, mu)
    idx = [RWKV_WIDTH, 2 * RWKV_WIDTH, 3 * RWKV_WIDTH,
           3 * RWKV_WIDTH + RWKV_DECAY_LORA, 3 * RWKV_WIDTH + RWKV_DECAY_LORA + RWKV_AAA_LORA]
    r, k, v, wd, ad, gd = jnp.split(p, idx, axis=-1)
    w = -jax.nn.softplus(-(w0 + jnp.tanh(wd) @ w2)) - 0.5
    decay = jnp.exp(-jnp.exp(w.astype(jnp.float32)))
    a = jax.nn.sigmoid(a0 + ad @ a2)
    g = jax.nn.sigmoid(gd) @ g2
    kk = (k * k_k).reshape(b, s, RWKV_HEADS, HEAD_DIM).astype(jnp.float32)
    kk = kk * lax.rsqrt(jnp.maximum(jnp.sum(jnp.square(kk), axis=-1, keepdims=True), 1e-12))
    k = k * (1.0 + (a - 1.0) * k_a)

    def heads(t):
        return t.reshape(b, s, RWKV_HEADS, HEAD_DIM).astype(jnp.float32)

    rh, kh, vh, ah, wh = heads(r), heads(k), heads(v), heads(a), heads(decay)
    tm = lambda t: jnp.swapaxes(t, 0, 1)

    def step(state, inp):
        r_t, w_t, k_t, v_t, kk_t, a_t = inp
        sa = jnp.einsum('bhvk,bhk->bhv', state, -kk_t)
        state = (state * w_t[:, :, None, :] + sa[..., None] * (kk_t * a_t)[:, :, None, :]
                 + v_t[..., None] * k_t[:, :, None, :])
        return state, jnp.einsum('bhvk,bhk->bhv', state, r_t)

    init = jnp.zeros((b, RWKV_HEADS, HEAD_DIM, HEAD_DIM), jnp.float32)
    _, ys = lax.scan(step, init, (tm(rh), tm(wh), tm(kh), tm(vh), tm(kk), tm(ah)))
    y = jnp.swapaxes(ys, 0, 1)
    mu_y = jnp.mean(y, axis=-1, keepdims=True)
    var_y = jnp.mean(jnp.square(y - mu_y), axis=-1, keepdims=True)
    y = ((y - mu_y) * lax.rsqrt(var_y + RWKV_GN_EPS)).reshape(b, s, RWKV_WIDTH) * gn_g + gn_b
    bonus = jnp.sum(rh * kh * r_k, axis=-1, keepdims=True) * vh
    y = (y + bonus.reshape(b, s, RWKV_WIDTH)) * g
    return y.astype(cols.dtype)

def causal_depthwise_conv(u, w, bias):
    out = lax.conv_general_dilated(u, w[:, None, :], window_strides=(1,),
                                   padding=[(CONV_WIDTH - 1, 0)],
                                   dimension_numbers=('NWC', 'WIO', 'NWC'),
                                   feature_group_count=u.shape[-1])
    return out + bias

def hybrid_layer(x, w_in, mla_q_norm, mla_w_uq, mla_kv_norm, mla_w_ukv,
                 rwkv_mu, rwkv_w0, rwkv_w2, rwkv_a0, rwkv_a2, rwkv_g2, rwkv_k_k, rwkv_k_a, rwkv_r_k,
                 rwkv_gn_g, rwkv_gn_b, w_o, ln1_g, ln1_b,
                 ffn_w_up, ffn_conv_w, ffn_conv_b, ffn_w_down, ln2_g, ln2_b):
    h = x @ w_in
    sb_cols, mla_cols, rwkv_cols = jnp.split(h, [SB_COLS, SB_COLS + MLA_COLS], axis=-1)
    q, k, v = (split_heads(t, SB_HEADS) for t in jnp.split(sb_cols, 3, axis=-1))
    o_sb = merge_heads(stick_breaking_attention(q, k, v))
    o_mla = mla_mixer(mla_cols, mla_q_norm, mla_w_uq, mla_kv_norm, mla_w_ukv)
    o_rwkv = rwkv7_mixer(rwkv_cols, rwkv_mu, rwkv_w0, rwkv_w2, rwkv_a0, rwkv_a2, rwkv_g2,
                         rwkv_k_k, rwkv_k_a, rwkv_r_k, rwkv_gn_g, rwkv_gn_b)
    mix = jnp.concatenate([o_sb, o_mla, o_rwkv], axis=-1) @ w_o
    x = layer_norm(DEEPNORM_ALPHA * x + mix, ln1_g, ln1_b)
    u_act, u_gate = jnp.split(x @ ffn_w_up, 2, axis=-1)
    hid = jax.nn.gelu(causal_depthwise_conv(u_act, ffn_conv_w, ffn_conv_b), approximate=False) * u_gate
    x = layer_norm(DEEPNORM_ALPHA * x + hid @ ffn_w_down, ln2_g, ln2_b)
    return x

def first_inputs(seed: int = 0) -> dict:
    key = jax.random.key(seed)
    ks = iter(jax.random.split(key, 32))
    L = DEPTH

    def nrm(shape, scale):
        return jax.random.normal(next(ks), shape, jnp.float32) * scale

    def unif(shape, lo, hi):
        return jax.random.uniform(next(ks), shape, jnp.float32, lo, hi)

    return {
        "x": nrm((BATCH, SEQ, D_MODEL), 1.0),
        "w_in": nrm((L, D_MODEL, IN_COLS), D_MODEL ** -0.5),
        "mla_q_norm": 1.0 + nrm((L, MLA_Q_LORA), 0.02),
        "mla_w_uq": nrm((L, MLA_Q_LORA, MLA_HEADS * (MLA_NOPE_DIM + MLA_ROPE_DIM)), MLA_Q_LORA ** -0.5),
        "mla_kv_norm": 1.0 + nrm((L, MLA_KV_LORA), 0.02),
        "mla_w_ukv": nrm((L, MLA_KV_LORA, MLA_HEADS * (MLA_NOPE_DIM + MLA_V_DIM)), MLA_KV_LORA ** -0.5),
        "rwkv_mu": unif((L, RWKV_COLS), 0.0, 1.0),
        "rwkv_w0": unif((L, RWKV_WIDTH), -6.5, -1.5),
        "rwkv_w2": nrm((L, RWKV_DECAY_LORA, RWKV_WIDTH), 0.1),
        "rwkv_a0": nrm((L, RWKV_WIDTH), 0.1),
        "rwkv_a2": nrm((L, RWKV_AAA_LORA, RWKV_WIDTH), RWKV_AAA_LORA ** -0.5),
        "rwkv_g2": nrm((L, RWKV_GATE_LORA, RWKV_WIDTH), RWKV_GATE_LORA ** -0.5),
        "rwkv_k_k": 0.85 + nrm((L, RWKV_WIDTH), 0.05),
        "rwkv_k_a": 1.0 + nrm((L, RWKV_WIDTH), 0.05),
        "rwkv_r_k": nrm((L, RWKV_HEADS, HEAD_DIM), 0.1),
        "rwkv_gn_g": 1.0 + nrm((L, RWKV_WIDTH), 0.02),
        "rwkv_gn_b": nrm((L, RWKV_WIDTH), 0.02),
        "w_o": nrm((L, MIX_WIDTH, D_MODEL), MIX_WIDTH ** -0.5 * DEEPNORM_BETA),
        "ln1_g": 1.0 + nrm((L, D_MODEL), 0.02),
        "ln1_b": nrm((L, D_MODEL), 0.02),
        "ffn_w_up": nrm((L, D_MODEL, 2 * D_FF), D_MODEL ** -0.5),
        "ffn_conv_w": nrm((L, CONV_WIDTH, D_FF), CONV_WIDTH ** -0.5),
        "ffn_conv_b": nrm((L, D_FF), 0.02),
        "ffn_w_down": nrm((L, D_FF, D_MODEL), D_FF ** -0.5 * DEEPNORM_BETA),
        "ln2_g": 1.0 + nrm((L, D_MODEL), 0.02),
        "ln2_b": nrm((L, D_MODEL), 0.02),
    }

def first_block(x, w_in, mla_q_norm, mla_w_uq, mla_kv_norm, mla_w_ukv,
              rwkv_mu, rwkv_w0, rwkv_w2, rwkv_a0, rwkv_a2, rwkv_g2, rwkv_k_k, rwkv_k_a, rwkv_r_k,
              rwkv_gn_g, rwkv_gn_b, w_o, ln1_g, ln1_b,
              ffn_w_up, ffn_conv_w, ffn_conv_b, ffn_w_down, ln2_g, ln2_b):
    for l in range(DEPTH):
        x = hybrid_layer(x, w_in[l], mla_q_norm[l], mla_w_uq[l], mla_kv_norm[l], mla_w_ukv[l],
                         rwkv_mu[l], rwkv_w0[l], rwkv_w2[l], rwkv_a0[l], rwkv_a2[l], rwkv_g2[l],
                         rwkv_k_k[l], rwkv_k_a[l], rwkv_r_k[l], rwkv_gn_g[l], rwkv_gn_b[l],
                         w_o[l], ln1_g[l], ln1_b[l],
                         ffn_w_up[l], ffn_conv_w[l], ffn_conv_b[l], ffn_w_down[l], ln2_g[l], ln2_b[l])
    return x


N_MIXERS = 2
N_LAYERS_A = (DEPTH + N_MIXERS - 1) // N_MIXERS
N_LAYERS_B = DEPTH // N_MIXERS
LRU_WIDTH = D_MODEL
LRU_HEADS = 4
LRU_HEAD_DIM = LRU_WIDTH // LRU_HEADS
CONV_WIDTH_2 = 4
LRU_C = 8.0
MIN_RAD = 0.9
MAX_RAD = 0.999
POOL_WINDOWS = (2, 4, 8, 16)
POOL_GROUPS = len(POOL_WINDOWS)
POOL_GROUP_DIM = D_MODEL // POOL_GROUPS
D_FF_2 = 4 * D_MODEL
N_MOD = 6
EPS = 1e-6


def rms_norm_2(x, g):
    xf = x.astype(jnp.float32)
    y = xf * lax.rsqrt(jnp.mean(xf * xf, axis=-1, keepdims=True) + EPS)
    return (y * g.astype(jnp.float32)).astype(x.dtype)

def modulate(h, shift, scale):
    return h * (1.0 + scale[:, None, :]) + shift[:, None, :]

def causal_depthwise_conv_2(x, w, b):
    s = x.shape[1]
    xp = jnp.pad(x, ((0, 0), (CONV_WIDTH_2 - 1, 0), (0, 0)))
    y = xp[:, 0:s] * w[0]
    for k in range(1, CONV_WIDTH_2):
        y = y + xp[:, k:k + s] * w[k]
    return y + b

def _lru_combine(left, right):
    a1, b1 = left
    a2, b2 = right
    return a1 * a2, a2 * b1 + b2

def block_diag_linear(x, w, b):
    bsz, s, _ = x.shape
    xh = x.reshape(bsz, s, LRU_HEADS, LRU_HEAD_DIM)
    y = jnp.einsum("bshi,hij->bshj", xh, w) + b
    return y.reshape(bsz, s, LRU_WIDTH)

def rg_lru(x, w_a, b_a, w_x, b_x, lam):
    gate_r = jax.nn.sigmoid(block_diag_linear(x, w_a, b_a)).astype(jnp.float32)
    gate_i = jax.nn.sigmoid(block_diag_linear(x, w_x, b_x)).astype(jnp.float32)
    log_a = LRU_C * gate_r * jax.nn.log_sigmoid(lam.astype(jnp.float32))
    a = jnp.exp(log_a)
    mult = jnp.sqrt(-jnp.expm1(2.0 * log_a))
    u = mult * (gate_i * x.astype(jnp.float32))
    _, h = lax.associative_scan(_lru_combine, (a, u), axis=1)
    return h.astype(x.dtype)

def recurrent_mixer(h, w_y, b_y, w_in, b_in, conv_w, conv_b, w_a, b_a, w_x, b_x, lam, w_out, b_out):
    gate_branch = jax.nn.gelu(jnp.einsum("bsd,dw->bsw", h, w_y) + b_y)
    xr = jnp.einsum("bsd,dw->bsw", h, w_in) + b_in
    xr = causal_depthwise_conv_2(xr, conv_w, conv_b)
    xr = rg_lru(xr, w_a, b_a, w_x, b_x, lam)
    return jnp.einsum("bsw,wd->bsd", xr * gate_branch, w_out) + b_out

def pool_mixer(h, w_pool, pool_scale):
    bsz, s, _ = h.shape
    hf = h.astype(jnp.float32)
    counts = jnp.arange(1, s + 1, dtype=jnp.float32)
    outs = []
    for g, win in enumerate(POOL_WINDOWS):
        xg = hf[..., g * POOL_GROUP_DIM:(g + 1) * POOL_GROUP_DIM]
        cs = jnp.cumsum(xg, axis=1)
        cs_lag = jnp.pad(cs, ((0, 0), (win, 0), (0, 0)))[:, :s]
        mean = (cs - cs_lag) / jnp.minimum(counts, float(win))[None, :, None]
        outs.append(mean - xg)
    pooled = jnp.stack(outs, axis=2).astype(h.dtype)
    mixed = jnp.einsum("bsgi,gij->bsgj", pooled, w_pool).reshape(bsz, s, D_MODEL)
    return mixed * pool_scale

def sq_relu_mlp(h, w1, w2):
    u = jax.nn.relu(jnp.einsum("bsd,df->bsf", h, w1))
    return jnp.einsum("bsf,fd->bsd", u * u, w2)

def second_inputs(seed: int = 0) -> dict:
    key = jax.random.key(seed)
    ks = jax.random.split(key, 26)
    f32 = jnp.float32
    nrm = lambda k, shape, s: (jax.random.normal(k, shape, f32) * s)
    d, w, hd, na, nb = D_MODEL, LRU_WIDTH, LRU_HEAD_DIM, N_LAYERS_A, N_LAYERS_B
    rad = jnp.sqrt(jax.random.uniform(ks[15], (na, w), f32, MIN_RAD ** 2, MAX_RAD ** 2))
    return {
        "x": nrm(ks[0], (BATCH, SEQ, d), 1.0),
        "c": nrm(ks[1], (BATCH, d), 1.0),
        "w_mod": nrm(ks[2], (DEPTH, d, N_MOD * d), 0.5 * d ** -0.5),
        "b_mod": nrm(ks[3], (DEPTH, N_MOD * d), 0.02),
        "norm_mix_g": 1.0 + nrm(ks[4], (DEPTH, d), 0.05),
        "norm_ffn_g": 1.0 + nrm(ks[5], (DEPTH, d), 0.05),
        "lru_w_y": nrm(ks[6], (na, d, w), d ** -0.5),
        "lru_b_y": nrm(ks[7], (na, w), 0.02),
        "lru_w_in": nrm(ks[8], (na, d, w), d ** -0.5),
        "lru_b_in": nrm(ks[9], (na, w), 0.02),
        "lru_conv_w": nrm(ks[10], (na, CONV_WIDTH_2, w), CONV_WIDTH_2 ** -0.5),
        "lru_conv_b": nrm(ks[11], (na, w), 0.02),
        "lru_w_a": nrm(ks[12], (na, LRU_HEADS, hd, hd), hd ** -0.5),
        "lru_b_a": nrm(ks[13], (na, LRU_HEADS, hd), 0.02),
        "lru_w_x": nrm(ks[14], (na, LRU_HEADS, hd, hd), hd ** -0.5),
        "lru_b_x": nrm(ks[16], (na, LRU_HEADS, hd), 0.02),
        "lru_lambda": jnp.log(rad) - jnp.log1p(-rad),
        "lru_w_out": nrm(ks[17], (na, w, d), w ** -0.5),
        "lru_b_out": nrm(ks[18], (na, d), 0.02),
        "pool_w": nrm(ks[19], (nb, POOL_GROUPS, POOL_GROUP_DIM, POOL_GROUP_DIM), POOL_GROUP_DIM ** -0.5),
        "pool_scale": 1.0 + nrm(ks[20], (nb, d), 0.1),
        "ffn_w1": nrm(ks[21], (DEPTH, d, D_FF_2), d ** -0.5),
        "ffn_w2": nrm(ks[22], (DEPTH, D_FF_2, d), D_FF_2 ** -0.5),
        "final_norm_g": 1.0 + nrm(ks[23], (d,), 0.05),
    }

def second_block(x, c, w_mod, b_mod, norm_mix_g, norm_ffn_g, lru_w_y, lru_b_y, lru_w_in, lru_b_in,
              lru_conv_w, lru_conv_b, lru_w_a, lru_b_a, lru_w_x, lru_b_x, lru_lambda, lru_w_out,
              lru_b_out, pool_w, pool_scale, ffn_w1, ffn_w2, final_norm_g):
    cond = jax.nn.silu(c)
    for i in range(DEPTH):
        mod = jnp.einsum("bd,de->be", cond, w_mod[i]) + b_mod[i]
        sh_m, sc_m, gt_m, sh_f, sc_f, gt_f = jnp.split(mod, N_MOD, axis=-1)
        h = modulate(rms_norm_2(x, norm_mix_g[i]), sh_m, sc_m)
        j = i // N_MIXERS
        if i % N_MIXERS == 0:
            y = recurrent_mixer(h, lru_w_y[j], lru_b_y[j], lru_w_in[j], lru_b_in[j],
                                lru_conv_w[j], lru_conv_b[j], lru_w_a[j], lru_b_a[j],
                                lru_w_x[j], lru_b_x[j], lru_lambda[j], lru_w_out[j], lru_b_out[j])
        else:
            y = pool_mixer(h, pool_w[j], pool_scale[j])
        x = x + gt_m[:, None, :] * y
        h = modulate(rms_norm_2(x, norm_ffn_g[i]), sh_f, sc_f)
        x = x + gt_f[:, None, :] * sq_relu_mlp(h, ffn_w1[i], ffn_w2[i])
    return rms_norm_2(x, final_norm_g)


def setup_inputs(seed=0):
    out = dict(first_inputs(seed))
    for name, value in second_inputs(seed + 1).items():
        if name != "x":
            out[name + "_2"] = value
    return out


def reference(
    x, w_in, mla_q_norm, mla_w_uq, mla_kv_norm, mla_w_ukv, rwkv_mu, rwkv_w0, rwkv_w2, rwkv_a0,
    rwkv_a2, rwkv_g2, rwkv_k_k, rwkv_k_a, rwkv_r_k, rwkv_gn_g, rwkv_gn_b, w_o, ln1_g, ln1_b,
    ffn_w_up, ffn_conv_w, ffn_conv_b, ffn_w_down, ln2_g, ln2_b, c_2, w_mod_2, b_mod_2,
    norm_mix_g_2, norm_ffn_g_2, lru_w_y_2, lru_b_y_2, lru_w_in_2, lru_b_in_2, lru_conv_w_2,
    lru_conv_b_2, lru_w_a_2, lru_b_a_2, lru_w_x_2, lru_b_x_2, lru_lambda_2, lru_w_out_2,
    lru_b_out_2, pool_w_2, pool_scale_2, ffn_w1_2, ffn_w2_2, final_norm_g_2,
):
    x = first_block(
        x, w_in, mla_q_norm, mla_w_uq, mla_kv_norm, mla_w_ukv, rwkv_mu, rwkv_w0, rwkv_w2,
        rwkv_a0, rwkv_a2, rwkv_g2, rwkv_k_k, rwkv_k_a, rwkv_r_k, rwkv_gn_g, rwkv_gn_b, w_o,
        ln1_g, ln1_b, ffn_w_up, ffn_conv_w, ffn_conv_b, ffn_w_down, ln2_g, ln2_b,
    )
    return second_block(
        x, c_2, w_mod_2, b_mod_2, norm_mix_g_2, norm_ffn_g_2, lru_w_y_2, lru_b_y_2, lru_w_in_2,
        lru_b_in_2, lru_conv_w_2, lru_conv_b_2, lru_w_a_2, lru_b_a_2, lru_w_x_2, lru_b_x_2,
        lru_lambda_2, lru_w_out_2, lru_b_out_2, pool_w_2, pool_scale_2, ffn_w1_2, ffn_w2_2,
        final_norm_g_2,
    )


_drawn_inputs = setup_inputs


def setup_inputs(seed=0):
    import zlib

    import numpy as np

    out = dict(_drawn_inputs(seed))
    spreads = {}
    factors = {'mla_q_norm': 8.0,
     'mla_kv_norm': 8.0,
     'rwkv_w2': 8.0,
     'rwkv_a0': 7.211,
     'rwkv_k_k': 5.611,
     'rwkv_k_a': 4.78,
     'rwkv_gn_g': 8.0,
     'rwkv_gn_b': 8.0,
     'ffn_conv_b': 8.0,
     'norm_mix_g_2': 3.414,
     'lru_b_y_2': 8.0,
     'lru_b_in_2': 5.911,
     'lru_conv_b_2': 5.516,
     'lru_b_a_2': 8.0,
     'lru_b_x_2': 8.0,
     'lru_b_out_2': 22.199,
     'norm_ffn_g_2': 3.641,
     'pool_scale_2': 4.137}
    for name, (base, spread) in spreads.items():
        noise = np.random.default_rng([zlib.crc32(name.encode()), seed]).standard_normal(out[name].shape)
        drawn = base * np.exp(spread * noise) if base else spread * noise
        out[name] = __import__('jax').numpy.asarray(drawn.astype(out[name].dtype))
    for name, factor in factors.items():
        out[name] = (out[name] * factor).astype(out[name].dtype)
    return out
```

```python
from contextlib import ExitStack, contextmanager

import numpy as np

import concourse.bass as bass
from concourse import mybir

F32 = mybir.dt.float32
F32R = mybir.dt.float32r
I32 = mybir.dt.int32
ALU = mybir.AluOpType
ACT = mybir.ActivationFunctionType
AX_X = mybir.AxisListType.X

P = 128
S = 512
D = 1024
KT = D // P
CHUNK = KT * P
BLOCKS = S // P
DEPTH = 2
HD = 64
F1, F2 = 2816, 4096
GROUPS1 = (8, 8, 6)
GROUPS2 = F2 // P // 8
POOL_WINDOWS = (2, 4, 8, 16)
ALPHA = (2 * DEPTH) ** 0.25
SB_SCALE = HD ** -0.5
MLA_SCALE = (64 + 32) ** -0.5
DECAY = float(np.exp(-0.5))
LN_EPS, RMS_EPS, GN_EPS = 1e-5, 1e-6, 64e-5
NEG = -1e30
LEVELS = (1, 2, 4, 8, 16, 32)

C_WAG, C_KRV = 0, 2
C_SB, C_MLA = 14, 20
C_UP, C_LORA = 23, 25
C_WO = 26
C_FFN = []
_s = C_WO + KT
for _g in GROUPS1:
    C_FFN.append((_s, _s + 2 * _g))
    _s += 2 * _g + KT
LC = _s
SPECIAL1 = (C_UP, C_UP + 1, C_LORA)
C_Y, C_IN, C_AX, C_OUT, C_F0 = 0, 8, 16, 20, 28
C_POOL = C_F0 + 16 * GROUPS2
C_F1 = C_POOL + 2
LC2 = C_F1 + 16 * GROUPS2
SPECIAL2 = (16, 17, 18, 19, C_POOL, C_POOL + 1)
CHUNKS = DEPTH * LC + LC2


def uses_before(s, special):
    return sum(1 for c in range(s % 2, s, 2) if c not in special)


USES1 = [uses_before(LC + p, SPECIAL1) for p in range(2)]


class Place:

    def __init__(self, pair0, use0, special):
        self.pair0, self.use0, self.special = pair0, use0, special

    def chunk(self, s, i=0):
        return self.pair0 * 2 + s + i * 2

    def landed(self, s, i=0):
        return (self.pair0 + s // 2 + i + 1) * 16

    def use(self, s, i=0):
        return self.use0[s % 2] + uses_before(s, self.special) + i


def place1(layer):
    return Place(layer * (LC // 2), [layer * USES1[0], layer * USES1[1]], SPECIAL1)


PLACE2 = Place(DEPTH * LC // 2, [DEPTH * USES1[0], DEPTH * USES1[1]], SPECIAL2)

LAYER_VECS = [("mu", 14), ("w0", 4), ("a0", 4), ("k_k", 4), ("k_a", 4), ("r_k", 4), ("gn_g", 4),
              ("gn_b", 4), ("q_norm", 2), ("kv_norm", 1), ("ln1_g", 8), ("ln1_b", 8),
              ("conv0", 22), ("conv1", 22), ("conv2", 22), ("conv_b", 22), ("ln2_g", 8),
              ("ln2_b", 8)]
VECS2 = [("c", 8), ("b_mod", 96), ("mix_g", 16), ("ffn_g", 16), ("b_y", 8), ("b_in", 8),
         ("conv0", 8), ("conv1", 8), ("conv2", 8), ("conv3", 8), ("conv_b", 8), ("b_a", 8),
         ("b_x", 8), ("lam", 8), ("b_out", 8), ("pool_scale", 8), ("final_g", 8)]


def columns(vecs):
    at, out = 0, {}
    for name, n in vecs:
        out[name] = at
        at += n
    return out, at


V1, NV1 = columns(LAYER_VECS)
V2, NV2 = columns(VECS2)

CONSTS = [("ident", 128), ("neg_sb", 128), ("neg_mla", 128), ("upper", 128), ("lower", 128),
          ("upper_incl", 128), ("heads", 128), ("ones", 128), ("lev_x", 6 * 128),
          ("lev_xt", 6 * 128), ("rope", S), ("chunk_mask", S), ("pool_fix", 64)]
VC, NVC = columns(CONSTS)


def constants():
    c = np.zeros((P, NVC), np.float32)
    i, j = np.arange(P)[:, None], np.arange(P)[None, :]
    same = (i // HD) == (j // HD)

    def put(name, a, n=0):
        c[:, VC[name] + n:VC[name] + n + a.shape[1]] = a

    put("ident", (i == j))
    put("neg_sb", np.where(j >= i, NEG, 0.0))
    put("neg_mla", np.where(j > i, NEG, 0.0))
    put("upper", same & (i < j))
    put("lower", same & (j < i))
    put("upper_incl", same & (i <= j))
    put("heads", same)
    put("ones", np.ones((P, P)))
    for n, b in enumerate(LEVELS):
        low = (i // (2 * b) == j // (2 * b)) & (i // b % 2 == 1) & (j // b % 2 == 0)
        put("lev_x", low, n * P)
        put("lev_xt", low.T, n * P)
    inv = 1.0 / (np.float32(10000.0) ** (np.arange(0, 32, 2, dtype=np.float32) / np.float32(32)))
    ang = np.arange(S, dtype=np.float32)[:, None] * inv[None].astype(np.float32)
    cos, sin = np.cos(ang).T.astype(np.float32), np.sin(ang).T.astype(np.float32)
    rope = np.zeros((P, S), np.float32)
    rope[64:96] = np.concatenate([cos, cos])
    rope[96:128] = np.concatenate([-sin, sin])
    put("rope", rope)
    put("chunk_mask", np.broadcast_to((np.arange(S) % HD != 0), (P, S)))
    for g, win in enumerate(POOL_WINDOWS):
        t = np.arange(16)
        put("pool_fix", np.broadcast_to(win / np.minimum(t + 1.0, win), (P, 16)), 16 * g)
    return c


PER = {"layer": 126, "pool": 99}


class Chain:

    def __init__(self, eng, sem, apart=None):
        self.eng, self.sem, self.base, self.n, self.apart = eng, sem, 0, 0, apart

    def __call__(self, ins):
        ins.then_inc(self.sem, 1)
        self.n += 1
        wait = self.apart or type(self.eng).wait_ge
        wait(self.eng, self.sem, self.base + self.n)

    @contextmanager
    def loop(self, count, calls):
        base, n = self.base, self.n
        with self.eng.Fori(0, count) as i:
            self.base, self.n = base + n + i * calls, 0
            yield i
            assert self.n == calls, f"{self.n} calls in the loop's body, {calls} given"
        self.base, self.n = base, n + count * calls


def build(nc, x_in, stream, mod_stream, vecs1, vecs2, consts, out):
    ctx = ExitStack()
    with ctx:
        top = [nc.sbuf_usable_end - nc.sbuf_bytes_remaining + 63]
        top[0] -= top[0] % 64
        limit = nc.sbuf_usable_end

        def at(name, shape, offset, dt=F32):
            size = 4 * int(np.prod(shape[1:]))
            assert offset + size <= limit, (name, offset, size, limit)
            return nc.alloc_sbuf_tensor_at(name, shape, dt, offset=offset)

        def sb(name, shape, dt=F32):
            t = at(name, shape, top[0], dt)
            top[0] += (4 * int(np.prod(shape[1:])) + 31) // 32 * 32
            return t

        x = sb("x", [P, KT, S])
        xh = sb("xh", [P, KT, S], F32R)
        xl = sb("xl", [P, KT, S], F32R)
        raw = sb("raw", [P, 2, CHUNK])
        wh = sb("wh", [P, 2, KT, P], F32R)
        wl = sb("wl", [P, 2, KT, P], F32R)
        cst = sb("cst", [P, NVC])
        pv_next = sb("pv_next", [P, NV1])
        pv = sb("pv", [P, NV1])
        one_minus = sb("one_minus", [P, 14 + 4])
        pv2 = sb("pv2", [P, NV2])
        cond = sb("cond", [P, KT])
        mod = sb("mod", [P, DEPTH, 48])
        small = sb("small", [P, 16, 8])
        krv_at = top[0]
        krv = sb("krv", [P, 12, S])
        norm_sum = at("norm_sum", [P, S], krv_at)
        norm_sq = at("norm_sq", [P, S], krv_at + 2048)
        sq = at("sq", [P, 2, S], krv_at + 4096)
        rstd = at("rstd", [P, S], krv_at + 8192)
        shift = at("shift", [P, S], krv_at + 10240)
        nt = at("nt", [P, 2, S], krv_at + 12288)
        wag_at = top[0]
        wag = sb("wag", [P, 2, S])
        u0 = at("u0", [P, S], wag_at)
        uu = at("uu", [P, S], wag_at + 2048)
        r0 = top[0]

        class Region:
            def __init__(self, start):
                self.at = start

            def __call__(self, name, shape, dt=F32):
                t = at(name, shape, self.at, dt)
                self.at += (4 * int(np.prod(shape[1:])) + 31) // 32 * 32
                return t

        rg = Region(r0)
        sbq = rg("sbq", [P, 2, S])
        sbk = rg("sbk", [P, 2, S])
        cq = rg("cq", [P, 2, S])
        ckv = rg("ckv", [P, S])
        krot = rg("krot", [P, S])
        vsb = rg("vsb", [P, BLOCKS, 256])
        vmla = rg("vmla", [P, BLOCKS, 256])
        qh = rg("qh", [P, 4, S])
        kh = rg("kh", [P, 4, S])
        at0 = rg.at
        sbvT = rg("sbvT", [P, 2, S])
        csq = rg("csq", [P, 3, S])
        crs = rg("crs", [P, 2, S])
        rope_t = rg("rope_t", [P, 2, S])
        rg = Region(at0)
        keep = rg("keep", [P, 2, S])
        sig = rg("sig", [P, 2, S])
        later = rg("later", [P, 2, S])
        wts = rg("wts", [P, 2, S])
        wT = rg("wT", [P, 2, S])
        rg = Region(r0)
        aa = rg("aa", [P, 4, S])
        gg = rg("gg", [P, 4, S])
        kk = rg("kk", [P, 4, S])
        bv = rg("bv", [P, 4, S])
        dead0 = rg.at
        e1 = rg("e1", [P, 4, S])
        cum = rg("cum", [P, 4, S])
        tmp4 = rg("tmp4", [P, 4, S])
        cc = rg("cc", [P, 4, 8])
        state_at = rg.at
        rg = Region(dead0)
        mt = rg("mt", [P, 8, P])
        nT = rg("nT", [P, 8, P])
        lbT = rg("lbT", [P, 8, P])
        lkT = rg("lkT", [P, 8, P])
        xi = rg("xi", [P, 8, P])
        px = rg("px", [P, 8, P])
        assert rg.at <= state_at - 4 * 32
        rg = Region(state_at)
        xiT = rg("xiT", [P, 8, P])
        stage = rg("stage", [P, 5, 4, P])
        tok = rg("tok", [P, 3, 4 * P])
        st = rg("st", [P, 4, 4, P])
        mcc = rg("mcc", [P, 2, 4, P])
        yy = at("yy", [P, 4, S], krv_at)
        rg = Region(state_at)
        yc = rg("yc", [P, 2, S])
        ysq = rg("ysq", [P, 2, S])
        rg = Region(r0)
        hidh = rg("hidh", [P, 8, S], F32R)
        hidl = rg("hidl", [P, 8, S], F32R)
        hf = rg("hf", [P, 2, S])
        ua = rg("ua", [P, S + 4])
        cv = rg("cv", [P, S])
        gel = rg("gel", [P, S])
        mraw = rg("mraw", [P, 2, KT, P])
        mred = rg("mred", [P, 2, P])
        blk2_at = rg.at
        gate = rg("gate", [P, 8, S])
        rg2 = Region(krv_at + 16384)
        gx = rg2("gx", [P, 2, S])
        ga = rg2("ga", [P, 2, S])
        xc = rg("xc", [P, 8, S])
        rg = Region(blk2_at)
        hp = rg("hp", [P, S + 16])
        cs = rg("cs", [P, S + 16])

        dbank = [ctx.enter_context(nc.psum_tensor(f"dense{i}", [P, S], F32)) for i in range(2)]
        aux = [ctx.enter_context(nc.psum_tensor(f"aux{i}", [P, S], F32)) for i in range(6)]

        def sem(name):
            return ctx.enter_context(nc.semaphore(name))

        def const(name, rows=slice(0, P), n=None, off=0):
            n = n if n is not None else dict(CONSTS)[name]
            return cst[rows, VC[name] + off:VC[name] + off + n]

        def vec(name, t, rows=slice(0, P)):
            return pv[rows, bass.ds(V1[name] + t, 1)]

        def vec2(name, t):
            return pv2[:, bass.ds(V2[name] + t, 1)]

        in_landed = sem("in_landed")
        vecs_landed = sem("vecs_landed")
        vecs_ready = sem("vecs_ready")
        w_landed = [sem("w_landed0"), sem("w_landed1")]
        hi_done = sem("hi_done")
        lo_done = sem("lo_done")
        pe_chunk = sem("pe_chunk")
        bank_free = [sem("bank0_read"), sem("bank1_read")]
        mod_landed = [sem("mod_landed0"), sem("mod_landed1")]
        mod_mul, mod_red, mod_pe, mod_out = (sem("mod_mul"), sem("mod_red"), sem("mod_pe"),
                                             sem("mod_out"))
        cond_sig, cond_ready, vecs2_ready = sem("cond_sig"), sem("cond_ready"), sem("vecs2_ready")
        xh_ready, xl_ready = sem("xh_ready"), sem("xl_ready")
        dve_chain, act_chain, pool_chain = sem("dve_chain"), sem("act_chain"), sem("pool_chain")
        sq_ready, sums_tile, sums_pe = sem("sq_ready"), sem("sums_tile"), sem("sums_pe")
        mean_ready, var_ready, sd_ready = sem("mean_ready"), sem("var_ready"), sem("sd_ready")
        n_mul, n_aff = sem("n_mul"), sem("n_aff")
        shift_a, shift_d = sem("shift_a"), sem("shift_d")
        vtok_pe, vtok_ready = sem("vtok_pe"), sem("vtok_ready")
        csq_ready, c_ms, c_var, c_sd = sem("csq_ready"), sem("c_ms"), sem("c_var"), sem("c_sd")
        c_norm, ch_ready, cl_ready = sem("c_norm"), sem("ch_ready"), sem("cl_ready")
        up_pe, up_act, up_dve = sem("up_pe"), sem("up_act"), sem("up_dve")
        krot_ready, kh_rope = sem("krot_ready"), sem("kh_rope")
        z_ready, w_act, mx_ready, w_ready = (sem("z_ready"), sem("w_act"), sem("mx_ready"),
                                             sem("w_ready"))
        t_ready, wT_ready, av_done = sem("t_ready"), sem("wT_ready"), sem("av_done")
        mixh_ready, mixl_ready = sem("mixh_ready"), sem("mixl_ready")
        wag_ready, lh_ready, ll_ready = sem("wag_ready"), sem("lora_h"), sem("lora_l")
        lora_pe, lora_read = sem("lora_pe"), sem("lora_read")
        cum_ready, e_ready, kk0_ready, kksq_ready = (sem("cum_ready"), sem("e_ready"),
                                                     sem("kk0_ready"), sem("kksq_ready"))
        ss_pe, ss_max, kn_sd = sem("ss_pe"), sem("ss_max"), sem("kn_sd")
        rkk_ready, bonus_pe, hats_ready = sem("rkk_ready"), sem("bonus_pe"), sem("hats_ready")
        zero_ready, eye_ready, stage_ready, mcc_ready = (sem("zero_ready"), sem("eye_ready"),
                                                         sem("stage_ready"), sem("mcc_ready"))
        tok_pe, tok_ready, mm5_pe, mm5_read = (sem("tok_pe"), sem("tok_ready"), sem("mm5_pe"),
                                               sem("mm5_read"))
        p_pe, p_read, q_pe, q_read = sem("p_pe"), sem("p_read"), sem("q_pe"), sem("q_read")
        u0_pe, u0_read, u_pe, u_read = sem("u0_pe"), sem("u0_read"), sem("u_pe"), sem("u_read")
        s_pe, st_sum, state_ready = sem("s_pe"), sem("st_sum"), sem("state_ready")
        y_pe, y_read = sem("y_pe"), sem("y_read")
        gm_pe, yc_ready, ysq_ready, gv_pe, gvar_ready, gsd_ready = (
            sem("gm_pe"), sem("yc_ready"), sem("ysq_ready"), sem("gv_pe"), sem("gvar_ready"),
            sem("gsd_ready"))
        gn_mul, gn_aff, yf_ready = sem("gn_mul"), sem("gn_aff"), sem("yf_ready")
        ua_zero, ua_ready, conv_done, gel_ready = (sem("ua_zero"), sem("ua_ready"),
                                                   sem("conv_done"), sem("gel_ready"))
        hf_ready, hidh_ready, hidl_ready = sem("hf_ready"), sem("hidh_ready"), sem("hidl_ready")
        lam_a, lam_d, fold_ready = sem("lam_a"), sem("lam_d"), sem("fold_ready")
        xc_ready, ax_pe, ax_read, a_ready = (sem("xc_ready"), sem("ax_pe"), sem("ax_read"),
                                             sem("a_ready"))
        th_ready, m2_ready, m_ready, h_ready = (sem("th_ready"), sem("m2_ready"), sem("m_ready"),
                                                sem("h_ready"))
        y_add, relu_ready, pooled_ready, x_start = (sem("y_add"), sem("relu_ready"),
                                                    sem("pooled_ready"), sem("x_start"))
        out_tile, out_done = sem("out_tile"), sem("out_done")

        UNITS = [(kind, pair, i, e) for kind in ("sb", "mla") for pair in range(2)
                 for i in range(BLOCKS) for e in range(2)]
        NU = len(UNITS)
        MODS = 24
        HATS = {"A": kk, "B": aa, "K": krv[:, 0:4], "R": krv[:, 4:8], "V": krv[:, 8:12]}

        def heads4(a):
            return a.unsqueeze(1).to_broadcast([P, 4, P])

        def mask(name, n=0):
            return heads4(const(name, n=P, off=n * P))

        def bank4(b):
            return b[:].rearrange("q (h t) -> q h t", h=4)

        def wait_apart(eng, sem, value):
            eng.wait_ge(sem, value)
            eng.nop(nofuse=True)

        block = ctx.enter_context(nc.Block())

        @block.sync
        def _(sp):
            sp.dma_start(x[:], x_in).then_inc(in_landed, 16)
            sp.dma_start(raw[:, 0, :], stream[0]).then_inc(w_landed[0], 16)
            sp.dma_start(cst[:], consts).then_inc(in_landed, 16)
            sp.dma_start(pv2[:], vecs2).then_inc(in_landed, 16)
            sp.dma_start(pv_next[:], vecs1[0]).then_inc(vecs_landed, 16)
            sp.dma_start(raw[:, 1, :], stream[1]).then_inc(w_landed[1], 16)

            def load(n, slot):
                sp.wait_ge(lo_done, n - 1)
                sp.dma_start(raw[:, slot, :], stream[n]).then_inc(w_landed[slot], 16)

            def load_mod(m, slot):
                sp.wait_ge(mod_red, m + 1)
                sp.dma_start(mraw[:, slot], mod_stream[m]).then_inc(mod_landed[slot], 16)

            first = C_FFN[0][0]
            with sp.Fori(0, DEPTH) as layer:
                n0 = layer * LC + 2
                with sp.Fori(0, first // 2) as i:
                    for j in range(2):
                        load(n0 + i * 2 + j, j)
                wait_apart(sp, mixl_ready, layer * 8 + 8)
                with sp.Fori(0, MODS) as i:
                    for j in range(2):
                        load(n0 + first + i * 2 + j, j)
                        load_mod(layer * 2 * MODS + i * 2 + j, j)
                sp.wait_ge(vecs_ready, layer + 1)
                sp.dma_start(pv_next[:], vecs1[DEPTH - 1]).then_inc(vecs_landed, 16)
                with sp.Fori(0, (LC - first) // 2 - MODS) as i:
                    for j in range(2):
                        load(n0 + first + 2 * MODS + i * 2 + j, j)
            with sp.Fori(0, LC2 // 2 - 1) as i:
                for j in range(2):
                    load(DEPTH * LC + 2 + i * 2 + j, j)
            for m in range(KT):
                sp.wait_ge(out_tile, m + 1)
                sp.dma_start(out[m], x[:, m, :]).then_inc(out_done, 16)
            sp.wait_ge(out_done, 16 * KT)

        @block.tensor
        def _(pe):
            def split_product(o, w, w_rows, k_rhs, first, last):
                (slot, cols), (h, l) = w, k_rhs
                a = wh[w_rows, slot].rearrange("p k m -> p (k m)")[:, cols:cols + P]
                b = wl[w_rows, slot].rearrange("p k m -> p (k m)")[:, cols:cols + P]
                pe.matmul(o, a, h, start=first, stop=False)
                pe.matmul(o, a, l, start=False, stop=False)
                return pe.matmul(o, b, h, start=False, stop=last)

            def dense(pl, s, i, h, l, tiles=KT, tile_sem=None, tile_at=0):
                slot = s % 2
                pe.wait_ge(lo_done, pl.chunk(s, i) + 1)
                pe.wait_ge(bank_free[slot], pl.use(s, i))
                for k in range(tiles):
                    if tile_sem is not None:
                        pe.wait_ge(tile_sem, tile_at + k + 1)
                    m = split_product(dbank[slot][:], (slot, k * P), slice(0, P),
                                      (h[:, k, :], l[:, k, :]), k == 0, k == tiles - 1)
                m.then_inc(pe_chunk, 1)

            def section(pl, s, count, h, l, tiles=KT, tile_sem=None, tile_at=0, extra=None,
                        late=None):
                for j in range(2):
                    dense(pl, s + j, 0, h, l, tiles, tile_sem if j == 0 else None, tile_at)
                    if late:
                        late(j)
                if count > 2:
                    with pe.Fori(1, count // 2) as i:
                        for j in range(2):
                            dense(pl, s + j, i, h, l, tiles)
                            if extra:
                                extra(i - 1, j)
                return (lambda j: extra(count // 2 - 1, j)) if extra else None

            def norm_sums(k):
                pe.wait_ge(sums_tile, 8 * k + 10)
                pe.matmul(aux[4][:], const("ones"), norm_sum[:], start=True, stop=True)
                pe.matmul(aux[5][:], const("ones"), norm_sq[:], start=True, stop=True)\
                  .then_inc(sums_pe, 1)

            def latent(L, pl):
                pe.wait_ge(csq_ready, L + 1)
                pe.matmul(aux[0][:], const("ones"), csq[:, 0, :], start=True, stop=False)
                pe.matmul(aux[0][:], const("ones", slice(0, 64)), csq[0:64, 1, :],
                          start=False, stop=True)
                pe.matmul(aux[1][:], const("ones"), csq[:, 2, :], start=True, stop=True)\
                  .then_inc(c_ms, 1)
                for tb in range(BLOCKS):
                    for p in range(2):
                        o = aux[2 + tb // 2][:, 256 * (tb % 2) + P * p:256 * (tb % 2) + P * p + P]
                        m = pe.transpose(o, sbvT[:, p, tb * P:(tb + 1) * P], const("ident"))
                m.then_inc(vtok_pe, 1)
                pe.wait_ge(lo_done, pl.chunk(C_UP + 1) + 1)
                pe.wait_ge(cl_ready, L * 3 + 3)
                pe.wait_ge(vtok_ready, L * 2 + 2)
                s0, s1 = C_UP % 2, (C_UP + 1) % 2
                for h in range(4):
                    split_product(aux[h][:], (s0, h * P), slice(0, P), (xh[:, 4, :], xl[:, 4, :]),
                                  True, False)
                    split_product(aux[h][:], (s1, h * P), slice(0, 64),
                                  (xh[0:64, 5, :], xl[0:64, 5, :]), False, True)\
                        .then_inc(up_pe, 1)
                for p in range(2):
                    split_product(aux[4 + p][:], (s0, 512 + p * P), slice(0, P),
                                  (xh[:, 6, :], xl[:, 6, :]), True, True).then_inc(up_pe, 1)
                ukv_h = wh[:, s0].rearrange("p k m -> p (k m)")[:, 768:1024]
                ukv_l = wl[:, s0].rearrange("p k m -> p (k m)")[:, 768:1024]
                for tb in range(BLOCKS):
                    if tb % 2 == 0:
                        pe.wait_ge(up_act, L * 8 + 1 + tb // 2)
                        pe.wait_ge(up_dve, L * 4 + 1 + tb // 2)
                    o = aux[tb // 2][:, 256 * (tb % 2):256 * (tb % 2) + 256]
                    th, tl = xh[:, 6, tb * P:(tb + 1) * P], xl[:, 6, tb * P:(tb + 1) * P]
                    pe.matmul(o, th, ukv_h, start=True, stop=False)
                    pe.matmul(o, th, ukv_l, start=False, stop=False)
                    m = pe.matmul(o, tl, ukv_h, start=False, stop=True)
                m.then_inc(pe_chunk, 2)

            def attention(L):
                def scores(u):
                    kind, pair, i, e = UNITS[u]
                    n, q0, z = (i + 1) * P, i * P, aux[u % 2]
                    if u >= 2:
                        pe.wait_ge(w_act, L * NU + u - 1)
                    if kind == "sb":
                        r = slice(64 * e, 64 * e + 64)
                        pe.matmul(z[:, 0:n], sbq[r, pair, q0:q0 + P], sbk[r, pair, 0:n],
                                  start=True, stop=False)
                    else:
                        h = 2 * pair + e
                        pe.matmul(z[:, 0:n], qh[0:96, h, q0:q0 + P], kh[0:96, h, 0:n],
                                  start=True, stop=False)
                    neg = const("neg_sb" if kind == "sb" else "neg_mla")
                    pe.matmul(z[:, q0:q0 + P], const("ident"), neg, start=False, stop=True)\
                      .then_inc(z_ready, 1)

                def turn(u):
                    i = UNITS[u][2]
                    pe.wait_ge(w_ready, L * NU + u + 1)
                    if u >= 2:
                        pe.wait_ge(wT_ready, L * NU + u - 1)
                    for j in range(i + 1):
                        m = pe.transpose(aux[2 + u % 2][:, j * P:(j + 1) * P],
                                         wts[:, u % 2, j * P:(j + 1) * P], const("ident"))
                    m.then_inc(t_ready, 1)

                def values(u):
                    kind, pair, i, e = UNITS[u]
                    q = (2 if kind == "mla" else 0) + pair
                    pe.wait_ge(wT_ready, L * NU + u + 1)
                    if i == 0 and e == 0 and q >= 2:
                        pe.wait_ge(mixl_ready, L * 8 + q - 1)
                    v = vsb if kind == "sb" else vmla
                    o = aux[4 + q % 2][64 * e:64 * e + 64, i * P:(i + 1) * P]
                    for j in range(i + 1):
                        m = pe.matmul(o, v[:, j, 128 * pair + 64 * e:128 * pair + 64 * e + 64],
                                      wT[:, u % 2, j * P:(j + 1) * P],
                                      start=(j == 0), stop=(j == i))
                    m.then_inc(av_done, 1)

                pe.wait_ge(vtok_ready, L * 2 + 2)
                pe.wait_ge(kh_rope, L + 1)
                pe.wait_ge(up_dve, L * 4 + 4)
                pe.wait_ge(up_act, L * 8 + 8)
                scores(0)
                for u in range(NU):
                    if u + 1 < NU:
                        scores(u + 1)
                    turn(u)
                    if u >= 1:
                        values(u - 1)
                values(NU - 1)

            def recurrence_inputs(L, pl):
                pe.wait_ge(lo_done, pl.chunk(C_LORA) + 1)
                pe.wait_ge(ll_ready, L * 2 + 2)
                pe.wait_ge(mixl_ready, L * 8 + 4)
                slot = C_LORA % 2
                for p in range(4):
                    if p >= 2:
                        pe.wait_ge(lora_read, L * 12 + 3 * (p - 1))
                    b = 3 * (p % 2)
                    split_product(aux[b][:], (slot, p * P), slice(0, 64),
                                  (xh[0:64, 4, :], xl[0:64, 4, :]), True, True)
                    split_product(aux[b + 1][:], (slot, p * P), slice(64, P),
                                  (xh[64:P, 4, :], xl[64:P, 4, :]), True, True)
                    m = split_product(aux[b + 2][:], (slot, 512 + p * P), slice(0, P),
                                      (xh[:, 5, :], xl[:, 5, :]), True, True)
                    if p < 3:
                        m.then_inc(lora_pe, 1)
                    else:
                        m.then_inc(pe_chunk, 1)
                pe.wait_ge(lora_read, L * 12 + 12)
                for p in range(4):
                    pe.wait_ge(kksq_ready, L * 4 + p + 1)
                    pe.matmul(aux[p][:], const("heads"), bv[:, p, :], start=True, stop=True)\
                      .then_inc(ss_pe, 1)
                for p in range(4):
                    pe.wait_ge(rkk_ready, L * 4 + p + 1)
                    pe.wait_ge(ss_max, L * 4 + p + 1)
                    pe.matmul(aux[p][:], const("heads"), bv[:, p, :], start=True, stop=True)\
                      .then_inc(bonus_pe, 1)

            def recurrence_block(B, b, half):
                A, Bh, K, R, V = (stage[:, n] for n in range(5))
                R_now = HATS["R"][:, :, bass.ts(b, P)]
                pe.wait_ge(stage_ready, B * 2 + 1)
                pe.wait_ge(state_ready, B * 2)
                for n, src in enumerate((Bh, K, V)):
                    for p in range(4):
                        m = pe.transpose(aux[n][:, p * P:(p + 1) * P], src[:, p, :],
                                         const("ident"))
                    m.then_inc(tok_pe, 1)
                pe.wait_ge(stage_ready, B * 2 + 2)
                pe.wait_ge(y_read, B * 2)
                q = 0
                for g in range(2):
                    for left, right in ((Bh, A), (A, Bh), (K, A), (Bh, R), (K, R)):
                        b = aux[(3 + q) % 6]
                        if 3 <= q < 6:
                            pe.wait_ge(tok_ready, B * 3 + q - 2)
                        if q >= 6:
                            pe.wait_ge(mm5_read, B * 10 + q - 5)
                        r = slice(64 * g, 64 * g + 64)
                        for p in range(4):
                            m = pe.matmul(b[:, p * P:(p + 1) * P], left[r, p, :],
                                          right[r, p, :], start=True, stop=True)
                        m.then_inc(mm5_pe, 1)
                        q += 1
                pe.wait_ge(mm5_read, B * 10 + 10)
                for n in range(1, 6):
                    for g in range(2):
                        if n > 1:
                            pe.wait_ge(q_read, B * 10 + 2 * (n - 2) + g + 1)
                        for h4 in range(4):
                            h = 4 * g + h4
                            m = pe.matmul(aux[g][:, h4 * P:(h4 + 1) * P], mt[:, h, :],
                                          xi[:, h, :], start=True, stop=True)
                        m.then_inc(p_pe, 1)
                    for g in range(2):
                        pe.wait_ge(p_read, B * 10 + 2 * (n - 1) + g + 1)
                        for h4 in range(4):
                            h = 4 * g + h4
                            if n < 5:
                                pe.matmul(aux[2 + g][:, h4 * P:(h4 + 1) * P], xiT[:, h, :],
                                          px[:, h, :], start=True, stop=True)
                            m = pe.matmul(aux[4 + g][:, h4 * P:(h4 + 1) * P], px[:, h, :],
                                          xiT[:, h, :], start=True, stop=True)
                        m.then_inc(q_pe, 1)
                pe.wait_ge(q_read, B * 10 + 10)
                tB, tK, tV = (tok[:, n, :] for n in range(3))
                for h in range(8):
                    pe.matmul(aux[0][:, h * 64:(h + 1) * 64], nT[:, 4 * (h % 2) + h // 2, :],
                              tV[:, h * 64:(h + 1) * 64], start=(h == 0), stop=False,
                              skip_group_check=True)
                for c in range(2):
                    s_in = st[:, (2 * half + c) % 4]
                    rows = slice(64 * c, 64 * c + 64)
                    pe.wait_ge(state_ready, B * 2 + c)
                    for p in range(4):
                        m = pe.matmul(aux[0][rows, p * P:(p + 1) * P], A[:, p, rows],
                                      s_in[:, p, :], start=False, stop=(p == 3),
                                      skip_group_check=True)
                    m.then_inc(u0_pe, 1)
                    for p in range(4):
                        cols = slice(p * P, (p + 1) * P)
                        pe.matmul(aux[2][:, cols], tK[rows, cols], tV[rows, cols],
                                  start=(p == 0), stop=False, skip_group_check=True)
                    wait_apart(pe, u0_read, B * 2 + c + 1)
                    for h in range(8):
                        m = pe.matmul(aux[1][rows, h * 64:(h + 1) * 64],
                                      xiT[rows, 4 * (h % 2) + h // 2, rows],
                                      u0[rows, h * 64:(h + 1) * 64], start=True, stop=True)
                    m.then_inc(u_pe, 1)
                    pe.wait_ge(u_read, B * 2 + c + 1)
                    for p in range(4):
                        cols = slice(p * P, (p + 1) * P)
                        m = pe.matmul(aux[2][:, cols], tB[rows, cols], uu[rows, cols],
                                      start=False, stop=(p == 3), skip_group_check=True)
                    m.then_inc(s_pe, 1)
                for p in range(4):
                    o = aux[3 + p // 2][:, (p % 2) * 256:(p % 2) * 256 + 256]\
                        .rearrange("q (g t) -> q g t", g=2)
                    cols = slice(p * P, (p + 1) * P)
                    pe.matmul(o, uu[:, cols], lbT[:, p:p + 5:4, :], start=(p % 2 == 0),
                              stop=False, skip_group_check=True)
                    pe.matmul(o, tV[:, cols], lkT[:, p:p + 5:4, :], start=False, stop=False,
                              skip_group_check=True)
                    for c in range(2):
                        t = slice(64 * c, 64 * c + 64)
                        m = pe.matmul(o[:, :, t], st[:, (2 * half + c) % 4, p, :],
                                      R_now[:, p, t].unsqueeze(1).to_broadcast([P, 2, 64]),
                                      start=False, stop=(p % 2 == 1 and c == 1),
                                      skip_group_check=True)
                    if p % 2:
                        m.then_inc(y_pe, 1)

            def group_norm(L):
                for q in range(2):
                    for r in range(2):
                        if q == 0:
                            pe.wait_ge(y_read, (L + 1) * 8)
                        pe.matmul(aux[r][:], const("heads"), yy[:, 2 * q + r, :], start=True,
                                  stop=True).then_inc(gm_pe, 1)
                    for r in range(2):
                        pe.wait_ge(ysq_ready, L * 4 + 2 * q + r + 1)
                        if q:
                            pe.wait_ge(gvar_ready, L * 4 + r + 1)
                        pe.matmul(aux[2 + r][:], const("heads"), ysq[:, r, :], start=True,
                                  stop=True).then_inc(gv_pe, 1)

            pe.wait_ge(in_landed, 48)
            with pe.Fori(0, DEPTH) as L:
                pl = place1(L)
                section(pl, 0, C_UP - 1, xh, xl, tile_sem=xl_ready, tile_at=L * 16)
                dense(pl, C_UP - 1, 0, xh, xl)
                latent(L, pl)
                attention(L)
                recurrence_inputs(L, pl)
                wait_apart(pe, zero_ready, L + 1)
                with pe.Fori(0, 2) as i:
                    for half in range(2):
                        recurrence_block(L * 4 + i * 2 + half, i * 2 + half, half)
                group_norm(L)
                section(pl, C_WO, KT, xh, xl, tile_sem=mixl_ready, tile_at=L * 8)
                norm_sums(L * 2)
                def mod_sum(m0):
                    def one(i, j):
                        m = m0 + i * 2 + j
                        pe.wait_ge(mod_red, L * 2 * MODS + m + 3)
                        pe.matmul(aux[0][:, bass.ds(m, 1)], mred[:, j, :], const("ones", n=1),
                                  start=True, stop=True).then_inc(mod_pe, 1)
                    return one

                late = None
                for g, tiles in enumerate(GROUPS1):
                    up, down = C_FFN[g]
                    late = section(pl, up, 2 * tiles, xh, xl,
                                   tile_sem=xl_ready if g == 0 else None, tile_at=L * 16 + 8,
                                   extra=mod_sum(g * MODS) if g < 2 else None, late=late)
                    late = section(pl, down, KT, hidh, hidl, tiles, tile_sem=hidl_ready,
                                   tile_at=L * 22 + 8 * g,
                                   extra=mod_sum(g * MODS + 16) if g < 2 else None, late=late)
                norm_sums(L * 2 + 1)

            pl = PLACE2
            H0 = DEPTH * 22
            norm_sums(4)
            section(pl, C_Y, 16, xh, xl, tile_sem=xl_ready, tile_at=40)
            for h in range(4):
                pe.wait_ge(lo_done, pl.chunk(C_AX + h) + 1)
                pe.wait_ge(hidl_ready, H0 + 2 * h + 2)
                if h:
                    pe.wait_ge(ax_read, 4 * h)
                for o in range(4):
                    for k in range(2):
                        m = split_product(aux[o][:], (h % 2, (2 * o + k) * P), slice(0, P),
                                          (hidh[:, 2 * h + k, :], hidl[:, 2 * h + k, :]),
                                          k == 0, k == 1)
                m.then_inc(pe_chunk, 1)
            section(pl, C_OUT, KT, xh, xl, tile_sem=xl_ready, tile_at=48)
            norm_sums(5)
            H1 = H0 + 8

            def ffn2(c0, xl_at, hid_at):
                section(pl, c0, 8, xh, xl, tile_sem=xl_ready, tile_at=xl_at)
                section(pl, c0 + 8, 8, hidh, hidl, tile_sem=hidl_ready, tile_at=hid_at)
                with pe.Fori(1, GROUPS2) as g:
                    pg = Place(pl.pair0 + g * 8, [pl.use0[0] + g * 8, pl.use0[1] + g * 8],
                               pl.special)
                    with pe.Fori(0, 4) as i:
                        for j in range(2):
                            dense(pg, c0 + j, i, xh, xl)
                    for j in range(2):
                        dense(pg, c0 + 8 + j, 0, hidh, hidl, 8,
                              hidl_ready if j == 0 else None, hid_at + g * 8)
                    with pe.Fori(1, 4) as i:
                        for j in range(2):
                            dense(pg, c0 + 8 + j, i, hidh, hidl)

            ffn2(C_F0, 56, H1)
            norm_sums(6)
            for c in range(2):
                pe.wait_ge(lo_done, pl.chunk(C_POOL + c) + 1)
                pe.wait_ge(xl_ready, 64 + 4 * c + 4)
                if c:
                    pe.wait_ge(y_add, 8 + 4)
                for o in range(4):
                    for k in range(2):
                        t = 4 * c + 2 * (o // 2) + k
                        m = split_product(aux[o][:], (c, (2 * o + k) * P), slice(0, P),
                                          (xh[:, t, :], xl[:, t, :]), k == 0, k == 1)
                m.then_inc(pe_chunk, 1)
            norm_sums(7)
            ffn2(C_F1, 72, H1 + 32)
            norm_sums(8)

        @block.scalar
        def _(act):
            chain = Chain(act, act_chain)

            def prepare(pl, s, i=0, lead=False):
                slot = s % 2
                act.wait_ge(w_landed[slot], pl.landed(s, i))
                if not lead:
                    act.wait_ge(pe_chunk, pl.chunk(s, i) - 1)
                act.activation(wh[:, slot].rearrange("p k m -> p (k m)"), raw[:, slot, :],
                               ACT.Copy).then_inc(hi_done, 1)

            def done(pl, s, i=0, more=True):
                if more:
                    prepare(pl, s + 2, i)
                else:
                    act.wait_ge(pe_chunk, pl.chunk(s, i) + 1)

            def squares(pl, k, s, m, i=0, j=0):
                act.wait_ge(bank_free[s % 2], pl.use(s, i) + 1)
                act.wait_ge(sums_tile, 8 * k + m + 1)
                act.activation(sq[:, j, :], x[:, m, :], ACT.Square).then_inc(sq_ready, 1)

            def norm_stats(k, centred):
                act.wait_ge(sums_pe, k + 1)
                if centred:
                    act.activation(shift[:], aux[4][:], ACT.Copy, scale=1.0 / D)\
                       .then_inc(mean_ready, 1)
                    act.activation(rstd[:], aux[4][:], ACT.Square, scale=1.0 / D)\
                       .then_inc(mean_ready, 1)
                act.wait_ge(var_ready, k + 1)
                act.activation(rstd[:], rstd[:], ACT.Ln).then_inc(sd_ready, 1)
                act.wait_ge(sd_ready, 2 * k + 1)
                act.activation(rstd[:], rstd[:], ACT.Exp, scale=-0.5).then_inc(sd_ready, 1)

            def split_hi(dst, src):
                act.activation(dst, src, ACT.Copy).then_inc(xh_ready, 1)

            def layer_norm(k, g, b, xk):
                norm_stats(k, True)
                for m in range(KT):
                    act.wait_ge(n_mul, 8 * k + m + 1)
                    act.activation(x[:, m, :], nt[:, m % 2, :], ACT.Identity,
                                   scale=vec(g, m), bias=vec(b, m)).then_inc(n_aff, 1)
                    act.wait_ge(n_aff, 8 * k + m + 1)
                    split_hi(xh[:, m, :], x[:, m, :])

            act.wait_ge(in_landed, 48)
            act.activation(cond[:], pv2[:, V2["c"]:V2["c"] + 8], ACT.Sigmoid)\
               .then_inc(cond_sig, 1)
            lam = pv2[:, V2["lam"]:V2["lam"] + 8]
            chain(act.activation(small[:, 0, :], lam, ACT.Abs))
            chain(act.activation(small[:, 0, :], small[:, 0, :], ACT.Exp, scale=-1.0))
            act.activation(small[:, 1, :], small[:, 0, :], ACT.Ln, bias=1.0).then_inc(lam_a, 1)
            for m in range(KT):
                split_hi(xh[:, m, :], x[:, m, :])
            for s in range(2):
                prepare(place1(0), s, 0, True)

            def projections(L, pl):
                act.wait_ge(vecs_ready, L + 1)

                def keep_own(s, i, dst, col):
                    done(pl, s, i)
                    act.activation(dst, dbank[s % 2][:], ACT.Copy,
                                   scale=one_minus[:, bass.ds(col, 1)]).then_inc(shift_a, 1)

                for j in range(2):
                    keep_own(C_WAG + j, 0, wag[:, j, :], j)
                with act.Fori(0, 6) as i:
                    for j in range(2):
                        keep_own(C_KRV + j, i, krv[:, i * 2 + j, :], i * 2 + j + 2)
                act.wait_ge(n_aff, L * 16)
                for s, dst in zip(range(C_SB, C_UP), (sbq[:, 0, :], sbq[:, 1, :], sbk[:, 0, :],
                                                      sbk[:, 1, :], sbvT[:, 0, :], sbvT[:, 1, :],
                                                      cq[:, 0, :], cq[:, 1, :], ckv[:])):
                    done(pl, s)
                    act.activation(dst, dbank[s % 2][:], ACT.Copy)\
                       .then_inc(bank_free[s % 2], 1)

            def latent(L, pl):
                for s in (C_UP - 1, C_UP - 2):
                    act.wait_ge(bank_free[s % 2], pl.use(s) + 1)
                act.activation(csq[:, 0, :], cq[:, 0, :], ACT.Square)
                act.activation(csq[0:64, 1, :], cq[0:64, 1, :], ACT.Square)
                act.activation(csq[:, 2, :], ckv[:], ACT.Square).then_inc(csq_ready, 1)
                act.wait_ge(c_var, L + 1)
                act.activation(crs[:], crs[:], ACT.Ln).then_inc(c_sd, 1)
                act.wait_ge(c_sd, L * 2 + 1)
                act.activation(crs[:], crs[:], ACT.Exp, scale=-0.5).then_inc(c_sd, 1)
                act.wait_ge(vtok_pe, L + 1)
                for t in range(2):
                    act.activation(vsb[:, 2 * t:2 * t + 2, :].rearrange("p a b -> p (a b)"),
                                   aux[2 + t][:], ACT.Copy).then_inc(vtok_ready, 1)
                for n, (dst, src) in enumerate(((xh[:, 4, :], cq[:, 0, :]),
                                                (xh[0:64, 5, :], cq[0:64, 1, :]),
                                                (xh[:, 6, :], ckv[:]))):
                    act.wait_ge(c_norm, L * 3 + n + 1)
                    act.activation(dst, src, ACT.Copy).then_inc(ch_ready, 1)
                for h in range(4):
                    act.wait_ge(up_pe, L * 6 + h + 1)
                    act.activation(qh[0:64, h, :], aux[h][0:64, :], ACT.Copy).then_inc(up_act, 1)
                for p in range(2):
                    act.wait_ge(up_pe, L * 6 + 5 + p)
                    act.activation(kh[0:64, 2 * p, :], aux[4 + p][0:64, :], ACT.Copy)
                    act.activation(kh[0:64, 2 * p + 1, :], aux[4 + p][64:P, :], ACT.Copy)\
                       .then_inc(up_act, 1)
                for s in (C_UP, C_UP + 1):
                    done(pl, s)
                for t in range(2):
                    act.activation(vmla[:, 2 * t:2 * t + 2, :].rearrange("p a b -> p (a b)"),
                                   aux[t][:], ACT.Copy).then_inc(up_act, 1)

            def attention(L):
                def weights(u):
                    kind, pair, i, e = UNITS[u]
                    n, z, b = (i + 1) * P, aux[u % 2], u % 2
                    act.wait_ge(z_ready, L * NU + u + 1)
                    if u >= 2:
                        act.wait_ge(w_ready, L * NU + u - 1)
                    if kind == "sb":
                        act.activation(keep[:, b, 0:n], z[:, 0:n], ACT.Sigmoid, scale=-SB_SCALE)
                        act.activation(sig[:, b, 0:n], z[:, 0:n], ACT.Sigmoid, scale=SB_SCALE)\
                           .then_inc(w_act, 1)
                    else:
                        act.wait_ge(mx_ready, L * (NU // 2) + u - NU // 2 + 1)
                        act.activation(keep[:, b, 0:n], z[:, 0:n], ACT.Exp, scale=MLA_SCALE,
                                       bias=small[:, 2, b:b + 1],
                                       accum_out=small[:, 3, b:b + 1]).then_inc(w_act, 1)

                def turned(u):
                    n = (UNITS[u][2] + 1) * P
                    act.wait_ge(t_ready, L * NU + u + 1)
                    if u >= 2:
                        act.wait_ge(av_done, L * NU + u - 1)
                    act.activation(wT[:, u % 2, 0:n], aux[2 + u % 2][:, 0:n], ACT.Copy)\
                       .then_inc(wT_ready, 1)

                def pair_out(q):
                    act.wait_ge(av_done, L * NU + 8 * q + 8)
                    act.activation(xh[:, q, :], aux[4 + q % 2][:], ACT.Copy)\
                       .then_inc(mixh_ready, 1)

                weights(0)
                for u in range(NU):
                    if u + 1 < NU:
                        weights(u + 1)
                    turned(u)
                    if u >= 8 and u % 8 == 1:
                        pair_out(u // 8 - 1)
                pair_out(3)

            def recurrence_inputs(L, pl):
                for j in range(2):
                    act.wait_ge(bank_free[j], pl.use(C_WAG + j) + 1)
                act.activation(wag[0:64, 0, :], wag[0:64, 0, :], ACT.Tanh)
                act.activation(wag[:, 1, :], wag[:, 1, :], ACT.Sigmoid).then_inc(wag_ready, 1)
                act.wait_ge(wag_ready, L + 1)
                for j in range(2):
                    act.activation(xh[:, 4 + j, :], wag[:, j, :], ACT.Copy).then_inc(lh_ready, 1)
                act.wait_ge(mixl_ready, L * 8 + 4)
                for p in range(4):
                    b = 3 * (p % 2)
                    if p < 3:
                        act.wait_ge(lora_pe, L * 3 + p + 1)
                    else:
                        act.wait_ge(pe_chunk, pl.chunk(C_LORA) + 1)
                    act.activation(tmp4[:, p, :], aux[b][:], ACT.Sigmoid, bias=vec("w0", p))\
                       .then_inc(lora_read, 1)
                    act.activation(aa[:, p, :], aux[b + 1][:], ACT.Sigmoid, bias=vec("a0", p))\
                       .then_inc(lora_read, 1)
                    act.activation(gg[:, p, :], aux[b + 2][:], ACT.Copy).then_inc(lora_read, 1)
                done(pl, C_LORA)
                act.wait_ge(cum_ready, L * 4 + 4)
                act.activation(e1[:], cum[:], ACT.Exp, scale=-DECAY)
                act.activation(cum[:], cum[:], ACT.Exp, scale=DECAY).then_inc(e_ready, 1)
                for p in range(4):
                    act.wait_ge(kk0_ready, L * 4 + p + 1)
                    act.activation(bv[:, p, :], kk[:, p, :], ACT.Square).then_inc(kksq_ready, 1)
                for p in range(4):
                    act.wait_ge(ss_max, L * 4 + p + 1)
                    act.activation(tmp4[:, p, :], tmp4[:, p, :], ACT.Ln).then_inc(kn_sd, 1)
                act.wait_ge(kn_sd, L * 5 + 4)
                act.activation(tmp4[:], tmp4[:], ACT.Exp, scale=-0.5).then_inc(kn_sd, 1)

            def stage_block(b, names):
                for name in names:
                    a = act.activation(stage[:, "ABKRV".index(name)],
                                       HATS[name][:, :, bass.ts(b, P)], ACT.Copy)
                a.then_inc(stage_ready, 1)

            def recurrence_block(B, b, last):
                for n in range(3):
                    act.wait_ge(tok_pe, B * 3 + n + 1)
                    act.activation(tok[:, n, :], aux[n][:], ACT.Copy).then_inc(tok_ready, 1)
                for n in range(1, 6):
                    for g in range(2):
                        k = B * 10 + 2 * (n - 1) + g
                        act.wait_ge(p_pe, k + 1)
                        if n > 1:
                            act.wait_ge(q_pe, k - 1)
                        act.activation(px[:, 4 * g:4 * g + 4, :], bank4(aux[g]), ACT.Copy)\
                           .then_inc(p_read, 1)
                if not last:
                    stage_block(b + 1, "BKRV")
                for c in range(2):
                    rows = slice(64 * c, 64 * c + 64)
                    act.wait_ge(u0_pe, B * 2 + c + 1)
                    act.activation(u0[rows, :], aux[0][rows, :], ACT.Copy).then_inc(u0_read, 1)
                if not last:
                    stage_block(b + 1, "A")
                for q in range(2):
                    act.wait_ge(y_pe, B * 2 + q + 1)
                    for g in range(2):
                        r = slice(64 * g, 64 * g + 64)
                        src = aux[3 + q][r, :].rearrange("q (p g t) -> q p g t", p=2, g=2)
                        a = act.activation(yy[r, 2 * q:2 * q + 2, bass.ts(b, P)],
                                           src[:, :, g, :], ACT.Copy)
                    a.then_inc(y_read, 1)

            def group_norm(L):
                for q in range(2):
                    for r in range(2):
                        k = L * 4 + 2 * q + r + 1
                        act.wait_ge(yc_ready, k)
                        act.activation(ysq[:, r, :], yc[:, r, :], ACT.Square)\
                           .then_inc(ysq_ready, 1)
                    for r in range(2):
                        k = L * 4 + 2 * q + r + 1
                        act.wait_ge(gvar_ready, k)
                        act.activation(ysq[:, r, :], ysq[:, r, :], ACT.Ln)\
                           .then_inc(gsd_ready, 1)
                    act.wait_ge(gsd_ready, L * 6 + 3 * q + 2)
                    act.activation(ysq[:], ysq[:], ACT.Exp, scale=-0.5).then_inc(gsd_ready, 1)
                    for r in range(2):
                        p = 2 * q + r
                        act.wait_ge(gn_mul, L * 4 + p + 1)
                        act.activation(yc[:, r, :], yc[:, r, :], ACT.Identity,
                                       scale=vec("gn_g", p), bias=vec("gn_b", p))\
                           .then_inc(gn_aff, 1)
                    for r in range(2):
                        p = 2 * q + r
                        act.wait_ge(yf_ready, L * 4 + p + 1)
                        act.activation(xh[:, 4 + p, :], yc[:, r, :], ACT.Copy)\
                           .then_inc(mixh_ready, 1)

            def hidden_hi(ready, value, slot_i, j):
                act.wait_ge(ready, value)
                act.activation(hidh[:, slot_i, :], hf[:, j, :], ACT.Copy).then_inc(hidh_ready, 1)

            with act.Fori(0, DEPTH) as L:
                pl = place1(L)
                projections(L, pl)
                latent(L, pl)
                attention(L)
                recurrence_inputs(L, pl)
                act.wait_ge(hats_ready, L + 1)
                stage_block(0, "BKRV")
                stage_block(0, "A")
                with act.Fori(0, BLOCKS - 1) as b:
                    recurrence_block(L * 4 + b, b, False)
                recurrence_block(L * 4 + BLOCKS - 1, BLOCKS - 1, True)
                group_norm(L)
                with act.Fori(0, KT // 2) as i:
                    for j in range(2):
                        done(pl, C_WO + j, i)
                        squares(pl, L * 2, C_WO + j, i * 2 + j, i, j)
                layer_norm(L * 2, "ln1_g", "ln1_b", 1)
                for g, tiles in enumerate(GROUPS1):
                    up, down = C_FFN[g]
                    with act.Fori(0, tiles) as i:
                        t = L * 22 + 8 * g + i
                        done(pl, up, i)
                        act.wait_ge(ua_zero, L + 1)
                        act.wait_ge(conv_done, t)
                        act.activation(ua[:, 2:S + 2], dbank[0][:], ACT.Copy)\
                           .then_inc(bank_free[0], 1)
                        act.wait_ge(conv_done, t + 1)
                        act.activation(gel[:], cv[:], ACT.Gelu, bias=vec("conv_b", 8 * g + i))\
                           .then_inc(gel_ready, 1)
                        done(pl, up + 1, i)
                        hidden_hi(bank_free[1], pl.use(up + 1, i) + 1, i, 0)
                    with act.Fori(0, KT // 2) as i:
                        for j in range(2):
                            done(pl, down + j, i)
                            if g == 2:
                                squares(pl, L * 2 + 1, down + j, i * 2 + j, i, j)
                layer_norm(L * 2 + 1, "ln2_g", "ln2_b", 2)

            pl = PLACE2
            H0 = DEPTH * 22
            act.wait_ge(n_aff, 32)

            def squares_now(k):
                for m in range(KT):
                    act.wait_ge(sums_tile, 8 * k + m + 1)
                    act.activation(sq[:, m % 2, :], x[:, m, :], ACT.Square).then_inc(sq_ready, 1)

            def modulated(k, scale, bias, hi=True):
                act.wait_ge(fold_ready, 1)
                norm_stats(k, False)
                for m in range(KT):
                    act.wait_ge(n_mul, 8 * k + m + 1)
                    act.activation(nt[:, m % 2, :], nt[:, m % 2, :], ACT.Identity,
                                   scale=scale(m), bias=bias(m)).then_inc(n_aff, 1)
                    if hi:
                        act.wait_ge(n_aff, 8 * k + m + 1)
                        split_hi(xh[:, m, :], nt[:, m % 2, :])

            squares_now(4)
            modulated(4, lambda m: small[:, 4, m:m + 1], lambda m: mod[:, 0, m:m + 1])
            with act.Fori(0, 4) as i:
                for j in range(2):
                    m = i * 2 + j
                    done(pl, C_Y + j, i)
                    act.activation(gate[:, m, :], dbank[j][:], ACT.Gelu_apprx_tanh,
                                   bias=vec2("b_y", m)).then_inc(bank_free[j], 1)
            with act.Fori(0, 4) as i:
                for j in range(2):
                    m = i * 2 + j
                    done(pl, C_IN + j, i)
                    act.wait_ge(xc_ready, m)
                    act.wait_ge(ua_zero, DEPTH + 1)
                    act.activation(ua[:, 3:S + 3], dbank[j][:], ACT.Identity,
                                   bias=vec2("b_in", m)).then_inc(bank_free[j], 1)
                    act.wait_ge(xc_ready, m + 1)
                    act.activation(hidh[:, m, :], xc[:, m, :], ACT.Copy).then_inc(hidh_ready, 1)
            for h in range(4):
                done(pl, C_AX + h)
                if h:
                    act.wait_ge(h_ready, 2 * h)
                for t in range(2):
                    act.activation(ga[:, t, :], aux[t][:], ACT.Sigmoid,
                                   bias=vec2("b_a", 2 * h + t)).then_inc(ax_read, 1)
                for t in range(2):
                    act.activation(gx[:, t, :], aux[2 + t][:], ACT.Sigmoid,
                                   bias=vec2("b_x", 2 * h + t)).then_inc(ax_read, 1)
                act.wait_ge(ax_read, 4 * h + 4)
                for t in range(2):
                    act.activation((gel if t == 0 else cv)[:], ga[:, t, :], ACT.Tanh,
                                   scale=small[:, 7, 2 * h + t:2 * h + t + 1])\
                       .then_inc(th_ready, 1)
                for t in range(2):
                    act.activation(ga[:, t, :], ga[:, t, :], ACT.Exp,
                                   scale=small[:, 6, 2 * h + t:2 * h + t + 1])\
                       .then_inc(a_ready, 1)
                for t in range(2):
                    act.wait_ge(m2_ready, 2 * h + t + 1)
                    b = (gel if t == 0 else cv)[:]
                    act.activation(b, b, ACT.Sqrt, scale=2.0).then_inc(m_ready, 1)
                for t in range(2):
                    act.wait_ge(h_ready, 2 * h + t + 1)
                    split_hi(xh[:, 2 * h + t, :], xc[:, 2 * h + t, :])

            def gated_add(s, i, m, j, scale, bias, k):
                done(pl, s, i)
                act.activation(nt[:, j, :], dbank[j][:], ACT.Identity, scale=scale(m),
                               bias=bias(m)).then_inc(bank_free[j], 1)

            with act.Fori(0, 4) as i:
                for j in range(2):
                    m = i * 2 + j
                    gated_add(C_OUT + j, i, m, j, lambda m: mod[:, 0, bass.ds(16 + m, 1)],
                              lambda m: small[:, 8, bass.ds(m, 1)], 5)
                    act.wait_ge(y_add, m + 1)
                    act.wait_ge(sums_tile, 8 * 5 + m + 1)
                    act.activation(sq[:, j, :], x[:, m, :], ACT.Square).then_inc(sq_ready, 1)

            def ffn2(c0, k, lay, hid0, last):
                modulated(k, lambda m: small[:, 5 if lay == 0 else 10, m:m + 1],
                          lambda m: mod[:, lay, 24 + m:25 + m])

                def group(pg, h0, stats, end):
                    with act.Fori(0, 4) as i:
                        for j in range(2):
                            done(pg, c0 + j, i)
                            t = h0 + i * 2 + j
                            act.wait_ge(hf_ready, t)
                            act.activation(gel[:], dbank[j][:], ACT.Relu)\
                               .then_inc(bank_free[j], 1)
                            hidden_hi(hf_ready, t + 1, i * 2 + j, j)

                    def down(i, more):
                        for j in range(2):
                            done(pg, c0 + 8 + j, i, more)
                            if stats:
                                squares(pg, k + 1, c0 + 8 + j, i * 2 + j, i, j)

                    with act.Fori(0, 3) as i:
                        down(i, True)
                    down(3, not end)

                with act.Fori(0, GROUPS2 - 1) as g:
                    group(Place(pl.pair0 + g * 8, [pl.use0[0] + g * 8, pl.use0[1] + g * 8],
                                pl.special), hid0 + g * 8, False, False)
                g = GROUPS2 - 1
                group(Place(pl.pair0 + g * 8, [u + g * 8 for u in pl.use0], pl.special),
                      hid0 + g * 8, True, last)

            ffn2(C_F0, 5, 0, 0, False)
            norm_stats(6, False)
            for m in range(KT):
                act.wait_ge(n_mul, 8 * 6 + m + 1)
                act.activation(nt[:, m % 2, :], nt[:, m % 2, :], ACT.Identity,
                               scale=small[:, 9, m:m + 1], bias=mod[:, 1, m:m + 1])\
                   .then_inc(n_aff, 1)
                act.wait_ge(pooled_ready, m + 1)
                split_hi(xh[:, m, :], hp[:, 0:S])
            for c in range(2):
                done(pl, C_POOL + c)
                for o in range(4):
                    m = 4 * c + o
                    if m >= 2:
                        act.wait_ge(y_add, 8 + m - 1)
                    act.activation(nt[:, o % 2, :], aux[o][:], ACT.Copy,
                                   scale=small[:, 11, m:m + 1]).then_inc(ax_read, 1)
                    act.wait_ge(y_add, 8 + m + 1)
                    act.wait_ge(sums_tile, 8 * 7 + m + 1)
                    act.activation(sq[:, o % 2, :], x[:, m, :], ACT.Square).then_inc(sq_ready, 1)
            ffn2(C_F1, 7, 1, 32, True)
            norm_stats(8, False)
            for m in range(KT):
                act.wait_ge(n_mul, 8 * 8 + m + 1)
                act.activation(x[:, m, :], nt[:, m % 2, :], ACT.Copy,
                               scale=vec2("final_g", m)).then_inc(out_tile, 1)

        @block.vector
        def _(dve):
            chain = Chain(dve, dve_chain)
            tt, stt, ts = dve.tensor_tensor, dve.scalar_tensor_tensor, dve.tensor_scalar
            MUL, ADD, SUB = ALU.mult, ALU.add, ALU.subtract

            def prepare(n, slot):
                dve.wait_ge(hi_done, n + 1)
                tt(wl[:, slot].rearrange("p k m -> p (k m)"), raw[:, slot, :],
                   wh[:, slot].rearrange("p k m -> p (k m)").bitcast(F32), SUB)\
                    .then_inc(lo_done, 1)

            def done(pl, s, i=0, more=True):
                n = pl.chunk(s, i)
                if more:
                    prepare(n + 2, s % 2)
                dve.wait_ge(pe_chunk, n + 1)

            def low(dst, src, hi, ready):
                tt(dst, src, hi.bitcast(F32), SUB).then_inc(ready, 1)

            def norm_scale(k, centred, eps):
                dve.wait_ge(sums_pe, k + 1)
                if centred:
                    dve.wait_ge(mean_ready, 2 * k + 2)
                    chain(stt(rstd[:], aux[5][:], 1.0 / D, rstd[:], MUL, SUB))
                    ts(rstd[:], rstd[:], 0.0, eps, ALU.max, ADD).then_inc(var_ready, 1)
                else:
                    ts(rstd[:], aux[5][:], 1.0 / D, eps, MUL, ADD).then_inc(var_ready, 1)
                dve.wait_ge(sd_ready, 2 * k + 2)
                if centred:
                    chain(stt(shift[:], shift[:], -1.0, rstd[:], MUL, MUL))

            def normal(m, centred):
                if centred:
                    chain(tt(nt[:, m % 2, :], x[:, m, :], rstd[:], MUL))
                    tt(nt[:, m % 2, :], nt[:, m % 2, :], shift[:], ADD).then_inc(n_mul, 1)
                else:
                    tt(nt[:, m % 2, :], x[:, m, :], rstd[:], MUL).then_inc(n_mul, 1)

            def norm_tiles(centred, xh_at, source):
                normal(0, centred)
                for m in range(KT):
                    if m + 1 < KT:
                        if m and not centred:
                            dve.wait_ge(xl_ready, xh_at + m)
                        normal(m + 1, centred)
                    dve.wait_ge(xh_ready, xh_at + m + 1)
                    low(xl[:, m, :], source(m), xh[:, m, :], xl_ready)

            dve.wait_ge(in_landed, 48)
            for m in range(KT):
                dve.wait_ge(xh_ready, m + 1)
                low(xl[:, m, :], x[:, m, :], xh[:, m, :], xl_ready)
            for n in range(2):
                prepare(n, n)
            dve.wait_ge(cond_sig, 1)
            tt(cond[:], cond[:], pv2[:, V2["c"]:V2["c"] + 8], MUL).then_inc(cond_ready, 1)
            dve.wait_ge(cond_ready, 1)
            dve.wait_ge(lam_a, 1)
            chain(stt(small[:, 6, :], pv2[:, V2["lam"]:V2["lam"] + 8], 0.0, small[:, 1, :],
                      ALU.min, SUB))
            chain(ts(small[:, 6, :], small[:, 6, :], 8.0, None, MUL))
            chain(ts(small[:, 7, :], small[:, 6, :], -1.0, None, MUL))

            def projections(L, pl):
                dve.wait_ge(vecs_ready, L + 1)

                def add_previous(s, i, dst, col, k):
                    prepare(pl.chunk(s, i) + 2, s % 2)
                    dve.wait_ge(shift_a, L * 14 + k + 1)
                    stt(dst[:, 1:S] if not callable(dst) else dst(), dbank[s % 2][:, 0:S - 1],
                        vec("mu", col), dst[:, 1:S] if not callable(dst) else dst(), MUL, ADD)\
                        .then_inc(bank_free[s % 2], 1)

                for j in range(2):
                    add_previous(C_WAG + j, 0, wag[:, j, :], j, j)
                with dve.Fori(0, 6) as i:
                    for j in range(2):
                        k = i * 2 + j + 2
                        add_previous(C_KRV + j, i, lambda: krv[:, i * 2 + j, 1:S], k, k)
                for s in range(C_SB, C_UP):
                    prepare(pl.chunk(s) + 2, s % 2)

            def rope(dst, swapped, plain, c):
                tt(rope_t[64:96, 0, :], swapped, const("rope", slice(96, 128)), MUL)
                c(tt(rope_t[64:96, 1, :], plain, const("rope", slice(64, 96)), MUL))
                return tt(dst, rope_t[64:96, 0, :], rope_t[64:96, 1, :], ADD)

            def latent(L, pl):
                for s in (C_UP - 1, C_UP - 2):
                    dve.wait_ge(bank_free[s % 2], pl.use(s) + 1)
                rope(krot[64:96, :], cq[96:128, 1, :], cq[64:96, 1, :], chain)\
                    .then_inc(krot_ready, 1)
                dve.wait_ge(c_ms, L + 1)
                ts(crs[:, 0, :], aux[0][:], 1.0 / 192, RMS_EPS, MUL, ADD)
                ts(crs[:, 1, :], aux[1][:], 1.0 / 128, RMS_EPS, MUL, ADD).then_inc(c_var, 1)
                dve.wait_ge(c_sd, L * 2 + 2)
                stt(cq[:, 0, :], cq[:, 0, :], vec("q_norm", 0), crs[:, 0, :], MUL, MUL)\
                    .then_inc(c_norm, 1)
                stt(cq[0:64, 1, :], cq[0:64, 1, :], vec("q_norm", 1, slice(0, 64)),
                    crs[0:64, 0, :], MUL, MUL).then_inc(c_norm, 1)
                stt(ckv[:], ckv[:], vec("kv_norm", 0), crs[:, 1, :], MUL, MUL)\
                    .then_inc(c_norm, 1)
                for n, (r, t, src) in enumerate(((slice(0, P), 4, cq[:, 0, :]),
                                                 (slice(0, 64), 5, cq[0:64, 1, :]),
                                                 (slice(0, P), 6, ckv[:]))):
                    dve.wait_ge(ch_ready, L * 3 + n + 1)
                    low(xl[r, t, :], src, xh[r, t, :], cl_ready)
                for h in range(4):
                    dve.wait_ge(up_pe, L * 6 + h + 1)
                    if h:
                        dve.wait_ge(up_dve, L * 4 + h)
                    rope(qh[64:96, h, :], aux[h][96:128, :], aux[h][64:96, :], chain)\
                        .then_inc(up_dve, 1)
                for s in (C_UP, C_UP + 1):
                    prepare(pl.chunk(s) + 2, s % 2)

            def attention(L):
                def row_max(u):
                    kind, pair, i, e = UNITS[u]
                    if kind == "sb":
                        return
                    b = u % 2
                    dve.wait_ge(z_ready, L * NU + u + 1)
                    dve.wait_ge(w_act, L * NU + u - 1)
                    chain(dve.reduce_max(small[:, 12, b:b + 1], aux[b][:, 0:(i + 1) * P], AX_X))
                    ts(small[:, 2, b:b + 1], small[:, 12, b:b + 1], -MLA_SCALE, None, MUL)\
                        .then_inc(mx_ready, 1)

                def weights(u):
                    kind, pair, i, e = UNITS[u]
                    n, b = (i + 1) * P, u % 2
                    dve.wait_ge(w_act, L * NU + u + 1)
                    if u >= 2:
                        dve.wait_ge(t_ready, L * NU + u - 1)
                    if kind == "sb":
                        k = keep[:, b, 1:n][:, ::-1]
                        chain(dve.tensor_tensor_scan(later[:, b, 0:n - 1][:, ::-1], k, k, 1.0,
                                                     MUL, ALU.min))
                        tt(wts[:, b, 0:n], later[:, b, 0:n], sig[:, b, 0:n], MUL)\
                            .then_inc(w_ready, 1)
                    else:
                        chain(dve.reciprocal(small[:, 13, b:b + 1], small[:, 3, b:b + 1]))
                        ts(wts[:, b, 0:n], keep[:, b, 0:n], small[:, 13, b:b + 1], None, MUL)\
                            .then_inc(w_ready, 1)

                def pair_out(q):
                    dve.wait_ge(mixh_ready, L * 8 + q + 1)
                    low(xl[:, q, :], aux[4 + q % 2][:], xh[:, q, :], mixl_ready)

                dve.wait_ge(up_act, L * 8 + 8)
                chain(dve.memset(later[:], 0.0))
                for u in range(NU):
                    if u + 1 < NU:
                        row_max(u + 1)
                    weights(u)
                    if u >= 8 and u % 8 == 1:
                        pair_out(u // 8 - 1)
                pair_out(3)

            def recurrence_inputs(L, pl):
                k, r, v = krv[:, 0:4, :], krv[:, 4:8, :], krv[:, 8:12, :]
                for j in range(2):
                    dve.wait_ge(lh_ready, L * 2 + j + 1)
                    low(xl[:, 4 + j, :], wag[:, j, :], xh[:, 4 + j, :], ll_ready)
                for p in range(4):
                    dve.wait_ge(lora_read, L * 12 + 3 * p + 1)
                    dve.tensor_tensor_scan(cum[:, p, :], const("chunk_mask"), tmp4[:, p, :], 0.0,
                                           MUL, ADD).then_inc(cum_ready, 1)
                for p in range(4):
                    ts(kk[:, p, :], k[:, p, :], vec("k_k", p), None, MUL).then_inc(kk0_ready, 1)
                prepare(pl.chunk(C_LORA) + 2, C_LORA % 2)
                for p in range(4):
                    dve.wait_ge(ss_pe, L * 4 + p + 1)
                    ts(tmp4[:, p, :], aux[p][:], 1e-12, None, ALU.max).then_inc(ss_max, 1)
                dve.wait_ge(kn_sd, L * 5 + 5)
                chain(tt(kk[:], kk[:], tmp4[:], MUL))
                dve.wait_ge(lora_read, L * 12 + 12)
                for p in range(4):
                    t = ts(tmp4[:, p, :], aa[:, p, :], vec("k_a", p),
                           one_minus[:, 14 + p:15 + p], MUL, ADD)
                chain(t)
                chain(tt(k, k, tmp4[:], MUL))
                for p in range(4):
                    stt(bv[:, p, :], r[:, p, :], vec("r_k", p), k[:, p, :], MUL, MUL)\
                        .then_inc(rkk_ready, 1)
                chain(tt(aa[:], kk[:], aa[:], MUL))
                dve.wait_ge(e_ready, L + 1)
                tt(aa[:], aa[:], cum[:], MUL)
                tt(k, k, cum[:], MUL)
                tt(r, r, e1[:], MUL)
                kc = kk[:].rearrange("q p (c t) -> q (p c) t", t=HD)
                ec = e1[:].rearrange("q p (c t) -> q (p c) t", t=HD)
                stt(kc[:, :, 1:HD], kc[:, :, 1:HD], -1.0, ec[:, :, 0:HD - 1], MUL, MUL)
                ts(kc[:, :, 0:1], kc[:, :, 0:1], -1.0, None, MUL)
                dve.tensor_copy(cc[:].rearrange("q p c -> q (p c)").unsqueeze(2),
                                ec[:, :, HD - 1:HD])
                for p in range(4):
                    dve.wait_ge(bonus_pe, L * 4 + p + 1)
                    t = tt(bv[:, p, :], aux[p][:], v[:, p, :], MUL)
                t.then_inc(hats_ready, 1)

            def recurrence_block(B, half):
                dve.wait_ge(eye_ready, B + 1)
                q = 0
                for g in range(2):
                    hs = slice(4 * g, 4 * g + 4)
                    for name in ("mt", "m", "n", "lb", "lk"):
                        b = bank4(aux[(3 + q) % 6])
                        wait_apart(dve, mm5_pe, B * 10 + q + 1)
                        if name == "mt":
                            dve.copy_predicated(xiT[:, hs, :], mask("lev_xt").bitcast(I32), b)
                            t = tt(mt[:, hs, :], b, mask("upper"), MUL)
                        elif name == "m":
                            t = dve.copy_predicated(xi[:, hs, :], mask("lev_x").bitcast(I32), b)
                        else:
                            dst = {"n": nT, "lb": lbT, "lk": lkT}[name]
                            t = tt(dst[:, hs, :], b, mask("upper" if name == "n"
                                                          else "upper_incl"), MUL)
                        t.then_inc(mm5_read, 1)
                        q += 1
                for n in range(1, 6):
                    for g in range(2):
                        hs = slice(4 * g, 4 * g + 4)
                        wait_apart(dve, q_pe, B * 10 + 2 * (n - 1) + g + 1)
                        if n < 5:
                            dve.copy_predicated(xi[:, hs, :], mask("lev_x", n).bitcast(I32),
                                                bank4(aux[2 + g]))
                        dve.copy_predicated(xiT[:, hs, :], mask("lev_xt", n).bitcast(I32),
                                            bank4(aux[4 + g])).then_inc(q_read, 1)
                for c in range(2):
                    rows = slice(64 * c, 64 * c + 64)
                    s_in, s_out = (2 * half + c) % 4, (2 * half + c + 1) % 4
                    dve.wait_ge(u_pe, B * 2 + c + 1)
                    dve.tensor_copy(uu[rows, :], aux[1][rows, :]).then_inc(u_read, 1)
                    dve.wait_ge(s_pe, B * 2 + c + 1)
                    dve.wait_ge(mcc_ready, B + 1)
                    dve.wait_ge(state_ready, B * 2 + c)
                    tt(st[:, s_out], bank4(aux[2]), st[:, s_in], ADD).then_inc(st_sum, 1)
                    dve.wait_ge(st_sum, B * 2 + c + 1)
                    tt(st[:, s_out], st[:, s_out], mcc[:, c], MUL).then_inc(state_ready, 1)

            def group_norm(L):
                for q in range(2):
                    for r in range(2):
                        p = 2 * q + r
                        dve.wait_ge(gm_pe, L * 4 + p + 1)
                        if q:
                            dve.wait_ge(mixl_ready, L * 8 + 4 + p - 1)
                        stt(yc[:, r, :], aux[r][:], -1.0 / HD, yy[:, p, :], MUL, ADD)\
                            .then_inc(yc_ready, 1)
                    for r in range(2):
                        dve.wait_ge(gv_pe, L * 4 + 2 * q + r + 1)
                        ts(ysq[:, r, :], aux[2 + r][:], 1.0 / HD, GN_EPS, MUL, ADD)\
                            .then_inc(gvar_ready, 1)
                    for r in range(2):
                        dve.wait_ge(gsd_ready, L * 6 + 3 * q + 3)
                        tt(yc[:, r, :], yc[:, r, :], ysq[:, r, :], MUL).then_inc(gn_mul, 1)
                    for r in range(2):
                        p = 2 * q + r
                        dve.wait_ge(gn_aff, L * 4 + p + 1)
                        chain(tt(yc[:, r, :], yc[:, r, :], bv[:, p, :], ADD))
                        tt(yc[:, r, :], yc[:, r, :], gg[:, p, :], MUL).then_inc(yf_ready, 1)
                    for r in range(2):
                        p = 2 * q + r
                        dve.wait_ge(mixh_ready, L * 8 + 4 + p + 1)
                        low(xl[:, 4 + p, :], yc[:, r, :], xh[:, 4 + p, :], mixl_ready)

            def residual(pl, s, i, m, alpha):
                if alpha:
                    stt(x[:, m, :], x[:, m, :], ALPHA, dbank[s % 2][:], MUL, ADD)\
                        .then_inc(bank_free[s % 2], 1)
                else:
                    tt(x[:, m, :], x[:, m, :], dbank[s % 2][:], ADD)\
                        .then_inc(bank_free[s % 2], 1)

            with chain.loop(DEPTH, PER["layer"]) as L:
                pl = place1(L)
                projections(L, pl)
                latent(L, pl)
                attention(L)
                recurrence_inputs(L, pl)
                with dve.Fori(0, 2) as i:
                    for half in range(2):
                        recurrence_block(L * 4 + i * 2 + half, half)
                group_norm(L)
                with dve.Fori(0, 4) as i:
                    for j in range(2):
                        done(pl, C_WO + j, i)
                        residual(pl, C_WO + j, i, i * 2 + j, True)
                norm_scale(L * 2, True, LN_EPS)
                norm_tiles(True, L * 16 + 8, lambda m: x[:, m, :])
                for g, tiles in enumerate(GROUPS1):
                    up, down = C_FFN[g]

                    def mod_times_cond(off, i, j):
                        if g == 2:
                            return
                        pairs = L * MODS + (g * MODS + off) // 2 + i
                        dve.wait_ge(mod_landed[j], (pairs + 1) * 16)
                        tt(mraw[:, j], mraw[:, j], cond[:].unsqueeze(2)
                           .to_broadcast([P, KT, P]), MUL).then_inc(mod_mul, 1)

                    with chain.loop(tiles, 2) as i:
                        t = L * 22 + 8 * g + i
                        mod_times_cond(0, i, 0)
                        done(pl, up, i)
                        dve.wait_ge(bank_free[0], pl.use(up, i) + 1)
                        dve.wait_ge(gel_ready, t)
                        m = i + 8 * g
                        chain(ts(cv[:], ua[:, 2:S + 2], vec("conv2", m), None, MUL))
                        chain(stt(cv[:], ua[:, 1:S + 1], vec("conv1", m), cv[:], MUL, ADD))
                        stt(cv[:], ua[:, 0:S], vec("conv0", m), cv[:], MUL, ADD)\
                            .then_inc(conv_done, 1)
                        mod_times_cond(0, i, 1)
                        done(pl, up + 1, i)
                        dve.wait_ge(gel_ready, t + 1)
                        tt(hf[:, 0, :], gel[:], dbank[1][:], MUL).then_inc(bank_free[1], 1)
                        dve.wait_ge(hidh_ready, t + 1)
                        low(hidl[:, i, :], hf[:, 0, :], hidh[:, i, :], hidl_ready)
                    with dve.Fori(0, 4) as i:
                        for j in range(2):
                            mod_times_cond(16, i, j)
                            done(pl, down + j, i)
                            residual(pl, down + j, i, i * 2 + j, g == 0)
                dve.wait_ge(mod_pe, (L + 1) * 2 * MODS)
                tt(mod[:, bass.ds(L, 1), :].rearrange("p l c -> p (l c)"), aux[0][:, 0:48],
                   pv2[:, bass.ds(V2["b_mod"] + L * 48, 48)], ADD).then_inc(mod_out, 1)
                norm_scale(L * 2 + 1, True, LN_EPS)
                norm_tiles(True, L * 16 + 16, lambda m: x[:, m, :])

            pl = PLACE2
            H0 = DEPTH * 22
            dve.wait_ge(mod_out, DEPTH)

            def fold(dst, l, at, gain):
                return stt(small[:, dst, :], mod[:, l, at:at + 8], 1.0, gain, ADD, MUL)

            def gain(name, l):
                return pv2[:, V2[name] + 8 * l:V2[name] + 8 * l + 8]

            fold(4, 0, 8, gain("mix_g", 0))
            fold(5, 0, 32, gain("ffn_g", 0))
            fold(9, 1, 8, gain("mix_g", 1))
            fold(10, 1, 32, gain("ffn_g", 1))
            tt(small[:, 8, :], mod[:, 0, 16:24], gain("b_out", 0), MUL)
            tt(small[:, 11, :], mod[:, 1, 16:24], gain("pool_scale", 0), MUL)\
                .then_inc(fold_ready, 1)

            norm_scale(4, False, RMS_EPS)
            norm_tiles(False, 40, lambda m: nt[:, m % 2, :])
            with dve.Fori(0, 4) as i:
                for j in range(2):
                    done(pl, C_Y + j, i)
            with chain.loop(4, 6) as i:
                for j in range(2):
                    m = i * 2 + j
                    done(pl, C_IN + j, i)
                    dve.wait_ge(bank_free[j], pl.use(C_IN + j, i) + 1)
                    chain(ts(xc[:, m, :], ua[:, 3:S + 3], vec2("conv3", m), vec2("conv_b", m),
                             MUL, ADD))
                    chain(stt(xc[:, m, :], ua[:, 2:S + 2], vec2("conv2", m), xc[:, m, :],
                              MUL, ADD))
                    chain(stt(xc[:, m, :], ua[:, 1:S + 1], vec2("conv1", m), xc[:, m, :],
                              MUL, ADD))
                    stt(xc[:, m, :], ua[:, 0:S], vec2("conv0", m), xc[:, m, :], MUL, ADD)\
                        .then_inc(xc_ready, 1)
                    dve.wait_ge(hidh_ready, H0 + m + 1)
                    low(hidl[:, m, :], xc[:, m, :], hidh[:, m, :], hidl_ready)
            for h in range(4):
                done(pl, C_AX + h)
                dve.wait_ge(ax_read, 4 * h + 4)
                dve.wait_ge(xc_ready, 2 * h + 2)
                buf = (gel[:], cv[:])
                for t in range(2):
                    tt(gx[:, t, :], gx[:, t, :], xc[:, 2 * h + t, :], MUL)
                for t in range(2):
                    dve.wait_ge(th_ready, 2 * h + t + 1)
                    chain(ts(nt[:, t, :], buf[t], 1.0, None, ADD))
                    chain(dve.reciprocal(nt[:, t, :], nt[:, t, :]))
                    tt(buf[t], buf[t], nt[:, t, :], MUL).then_inc(m2_ready, 1)
                for t in range(2):
                    dve.wait_ge(m_ready, 2 * h + t + 1)
                    dve.wait_ge(a_ready, 2 * h + t + 1)
                    m = 2 * h + t
                    chain(tt(gx[:, t, :], gx[:, t, :], buf[t], MUL))
                    chain(dve.tensor_tensor_scan(xc[:, m, :], ga[:, t, :], gx[:, t, :], 0.0,
                                                 MUL, ADD))
                    tt(xc[:, m, :], xc[:, m, :], gate[:, m, :], MUL).then_inc(h_ready, 1)
                for t in range(2):
                    m = 2 * h + t
                    dve.wait_ge(xh_ready, 48 + m + 1)
                    low(xl[:, m, :], xc[:, m, :], xh[:, m, :], xl_ready)
            with dve.Fori(0, 4) as i:
                for j in range(2):
                    m = i * 2 + j
                    done(pl, C_OUT + j, i)
                    dve.wait_ge(bank_free[j], pl.use(C_OUT + j, i) + 1)
                    tt(x[:, m, :], x[:, m, :], nt[:, j, :], ADD).then_inc(y_add, 1)

            def ffn2(c0, k, lay, xh_at, hid0, hidh0, last):
                norm_scale(k, False, RMS_EPS)
                norm_tiles(False, xh_at, lambda m: nt[:, m % 2, :])

                def group(pg, h0, end):
                    with dve.Fori(0, 4) as i:
                        for j in range(2):
                            t = h0 + i * 2 + j
                            done(pg, c0 + j, i)
                            dve.wait_ge(bank_free[j], pg.use(c0 + j, i) + 1)
                            tt(hf[:, j, :], gel[:], gel[:], MUL).then_inc(hf_ready, 1)
                            dve.wait_ge(hidh_ready, t + hidh0 + 1)
                            low(hidl[:, i * 2 + j, :], hf[:, j, :], hidh[:, i * 2 + j, :],
                                hidl_ready)

                    def down(i, more):
                        for j in range(2):
                            m = i * 2 + j
                            done(pg, c0 + 8 + j, i, more)
                            stt(x[:, m, :], dbank[j][:], mod[:, lay, bass.ds(40 + m, 1)],
                                x[:, m, :], MUL, ADD).then_inc(bank_free[j], 1)

                    with dve.Fori(0, 3) as i:
                        down(i, True)
                    down(3, not end)

                with dve.Fori(0, GROUPS2 - 1) as g:
                    group(Place(pl.pair0 + g * 8, [pl.use0[0] + g * 8, pl.use0[1] + g * 8],
                                pl.special), hid0 + g * 8, False)
                g = GROUPS2 - 1
                group(Place(pl.pair0 + g * 8, [u + g * 8 for u in pl.use0], pl.special),
                      hid0 + g * 8, last)

            ffn2(C_F0, 5, 0, 56, 0, H0 + 8, False)
            norm_scale(6, False, RMS_EPS)
            chain(dve.memset(cs[:, 0:16], 0.0))
            normal(0, False)
            for m in range(KT):
                win = POOL_WINDOWS[m // 2]
                if m + 1 < KT:
                    normal(m + 1, False)
                dve.wait_ge(n_aff, 8 * 6 + m + 1)
                h = nt[:, m % 2, :]
                chain(dve.tensor_tensor_scan(cs[:, 16:S + 16],
                                             const("ones", n=1).to_broadcast([P, S]), h, 0.0,
                                             MUL, ADD))
                chain(tt(hp[:, 0:S], cs[:, 16:S + 16], cs[:, 16 - win:S + 16 - win], SUB))
                chain(tt(hp[:, 0:16], hp[:, 0:16],
                         const("pool_fix", n=16, off=16 * (m // 2)), MUL))
                stt(hp[:, 0:S], hp[:, 0:S], 1.0 / win, h, MUL, SUB).then_inc(pooled_ready, 1)
                dve.wait_ge(xh_ready, 64 + m + 1)
                low(xl[:, m, :], hp[:, 0:S], xh[:, m, :], xl_ready)
            for c in range(2):
                done(pl, C_POOL + c)
                for o in range(4):
                    m = 4 * c + o
                    dve.wait_ge(ax_read, 16 + m + 1)
                    tt(x[:, m, :], x[:, m, :], nt[:, o % 2, :], ADD).then_inc(y_add, 1)
            ffn2(C_F1, 7, 1, 72, 32, H0 + 8, True)
            norm_scale(8, False, RMS_EPS)
            for m in range(KT):
                if m >= 2:
                    dve.wait_ge(out_tile, m - 1)
                normal(m, False)

        @block.gpsimd
        def _(pool):
            chain = Chain(pool, pool_chain, wait_apart)
            for n, s in enumerate((mod_red, mod_red, sums_tile, sums_tile)):
                pool.memset(small[:, 14, n:n + 1], 0.0).then_inc(s, 1)
            pool.wait_ge(in_landed, 48)

            def clear_sums(k, ready, value):
                pool.wait_ge(sums_pe, k)
                wait_apart(pool, ready, value)
                pool.memset(norm_sum[:], 0.0)
                chain(pool.memset(norm_sq[:], 0.0))

            def sum_tile(k, m, j):
                pool.wait_ge(sq_ready, 8 * k + m + 1)
                pool.wait_ge(sums_tile, 8 * k + m + 2)
                pool.tensor_tensor(norm_sum[:], norm_sum[:], x[:, m, :], ALU.add)
                pool.tensor_tensor(norm_sq[:], norm_sq[:], sq[:, j, :], ALU.add)\
                    .then_inc(sums_tile, 1)

            def sum_tiles(k):
                with pool.Fori(0, 4) as i:
                    for j in range(2):
                        sum_tile(k, i * 2 + j, j)

            with chain.loop(DEPTH, PER["pool"]) as L:
                pool.wait_ge(vecs_landed, 16 * (L + 1))
                wait_apart(pool, n_aff, L * 16)
                chain(pool.tensor_copy(pv[:], pv_next[:]))
                pool.tensor_scalar(one_minus[:, 0:14], pv[:, V1["mu"]:V1["mu"] + 14], -1.0, 1.0,
                                   ALU.mult, ALU.add)
                pool.tensor_scalar(one_minus[:, 14:18], pv[:, V1["k_a"]:V1["k_a"] + 4], -1.0, 1.0,
                                   ALU.mult, ALU.add).then_inc(vecs_ready, 1)
                wait_apart(pool, krot_ready, L + 1)
                for h in range(4):
                    t = pool.tensor_copy(kh[64:96, h, :], krot[64:96, :])
                t.then_inc(kh_rope, 1)
                wait_apart(pool, hats_ready, L + 1)
                pool.memset(st[:, 0], 0.0).then_inc(zero_ready, 1)
                with pool.Fori(0, BLOCKS) as b:
                    B = L * 4 + b
                    eye = heads4(const("ident"))
                    wait_apart(pool, p_pe, B * 10)
                    for g in range(2):
                        pool.tensor_copy(xi[:, 4 * g:4 * g + 4, :], eye)
                    wait_apart(pool, u_pe, B * 2)
                    for g in range(2):
                        t = pool.tensor_copy(xiT[:, 4 * g:4 * g + 4, :], eye)
                    t.then_inc(eye_ready, 1)
                    pool.wait_ge(state_ready, B * 2)
                    for c in range(2):
                        t = pool.tensor_tensor(mcc[:, c], heads4(const("heads")),
                                               cc[:, :, bass.ds(b * 2 + c, 1)]
                                               .to_broadcast([P, 4, P]), ALU.mult)
                    t.then_inc(mcc_ready, 1)
                clear_sums(L * 2, mixl_ready, L * 8 + 8)
                pool.memset(ua[:, 0:3], 0.0).then_inc(ua_zero, 1)
                sum_tiles(L * 2)
                with chain.loop(MODS, 4) as i:
                    for j in range(2):
                        m = L * 2 * MODS + i * 2 + j
                        pool.wait_ge(mod_mul, m + 1)
                        w = mraw[:, j]
                        chain(pool.tensor_tensor(w[:, 0:4], w[:, 0:4], w[:, 4:8], ALU.add))
                        chain(pool.tensor_tensor(w[:, 0:2], w[:, 0:2], w[:, 2:4], ALU.add))
                        pool.wait_ge(mod_pe, m)
                        pool.tensor_tensor(mred[:, j, :], w[:, 0], w[:, 1], ALU.add)\
                            .then_inc(mod_red, 1)
                clear_sums(L * 2 + 1, n_aff, L * 16 + 8)
                sum_tiles(L * 2 + 1)
            for k, ready, value in ((4, n_aff, 32), (5, xc_ready, 8), (6, n_aff, 48),
                                    (7, n_aff, 56), (8, n_aff, 64)):
                clear_sums(k, ready, value)
                if k == 4:
                    pool.memset(ua[:, 0:3], 0.0).then_inc(ua_zero, 1)
                sum_tiles(k)


def rows(a, k0, n=P):
    r = np.zeros((n, a.shape[1]), np.float32)
    part = a[k0:k0 + n]
    r[:part.shape[0]] = part
    return r


def chunk_of(w, cols, k0=0, tiles=KT):
    c = np.zeros((P, KT, P), np.float32)
    for k in range(tiles):
        c[:, k, :] = w[k0 + k * P:k0 + (k + 1) * P, cols]
    return c.reshape(P, CHUNK)


def weight_stream(a):
    out = np.zeros((CHUNKS, P, CHUNK), np.float32)
    R0 = 768 + 352
    for l in range(DEPTH):
        o = out[l * LC:(l + 1) * LC]
        w = a["w_in"][l]
        cols = np.arange(w.shape[1])
        tiles = [cols[R0 + 1536:R0 + 1664], cols[R0 + 1664:R0 + 1792]]
        for base in (R0 + 512, R0, R0 + 1024):
            tiles += [cols[base + P * t:base + P * (t + 1)] for t in range(4)]
        tiles += [cols[P * t:P * (t + 1)] for t in range(6)]
        rope = cols[768 + 320:768 + 352]
        swapped = np.concatenate([rope[16:], rope[:16]])
        tiles += [cols[768:896], np.concatenate([cols[896:960], rope, swapped]),
                  cols[960:1088]]
        for s, c in enumerate(tiles):
            o[s] = chunk_of(w, c)
        uq, ukv = a["mla_w_uq"][l], a["mla_w_ukv"][l]
        q_cols = []
        for h in range(4):
            c = np.arange(96 * h, 96 * h + 96)
            q_cols += [c, np.concatenate([c[80:96], c[64:80]])]
        q_cols = np.concatenate(q_cols)
        kv_cols = np.concatenate([np.arange(128 * h, 128 * h + 64) for h in range(4)]
                                 + [np.arange(128 * h + 64, 128 * h + 128) for h in range(4)])
        o[C_UP, :, 0:512] = uq[0:128][:, q_cols]
        o[C_UP, :, 512:1024] = ukv[:, kv_cols]
        o[C_UP + 1, 0:64, 0:512] = uq[128:192][:, q_cols]
        o[C_LORA, 0:64, 0:512] = a["rwkv_w2"][l]
        o[C_LORA, 64:128, 0:512] = a["rwkv_a2"][l]
        o[C_LORA, :, 512:1024] = a["rwkv_g2"][l]
        for m in range(KT):
            o[C_WO + m] = chunk_of(a["w_o"][l], slice(m * P, (m + 1) * P))
        up_w, down_w = a["ffn_w_up"][l], a["ffn_w_down"][l]
        for g, n in enumerate(GROUPS1):
            up, down = C_FFN[g]
            for t in range(n):
                f = (8 * g + t) * P
                o[up + 2 * t] = chunk_of(up_w, slice(f, f + P))
                o[up + 2 * t + 1] = chunk_of(up_w, slice(F1 + f, F1 + f + P))
            for m in range(KT):
                o[down + m] = chunk_of(down_w, slice(m * P, (m + 1) * P), 8 * g * P, n)
    o = out[DEPTH * LC:]
    for m in range(KT):
        c = slice(m * P, (m + 1) * P)
        o[C_Y + m] = chunk_of(a["lru_w_y_2"][0], c)
        o[C_IN + m] = chunk_of(a["lru_w_in_2"][0], c)
        o[C_OUT + m] = chunk_of(a["lru_w_out_2"][0], c)

    def square(w):
        return w.reshape(2, P, 2, P).transpose(1, 2, 0, 3).reshape(P, 512)

    for h in range(4):
        o[C_AX + h] = np.concatenate([square(a["lru_w_a_2"][0, h]), square(a["lru_w_x_2"][0, h])], 1)
    for c in range(2):
        o[C_POOL + c] = np.concatenate([square(a["pool_w_2"][0, 2 * c + g]) for g in range(2)], 1)
    for l, c0 in enumerate((C_F0, C_F1)):
        w1, w2 = a["ffn_w1_2"][l], a["ffn_w2_2"][l]
        for g in range(GROUPS2):
            for t in range(8):
                f = (8 * g + t) * P
                o[c0 + 16 * g + t] = chunk_of(w1, slice(f, f + P))
                o[c0 + 16 * g + 8 + t] = chunk_of(w2, slice(t * P, (t + 1) * P), 8 * g * P)
    return out


def feature_columns(vecs, total, values):
    out = np.zeros((P, total), np.float32)
    at = 0
    for name, n in vecs:
        v = np.zeros(n * P, np.float32)
        flat = np.ravel(values[name])
        v[:flat.size] = flat
        out[:, at:at + n] = v.reshape(n, P).T
        at += n
    return out


def kernel(**inputs):
    import concourse.bacc as bacc
    from concourse.bass_utils import run_bass_kernel_spmd

    a = {k: np.asarray(v) for k, v in inputs.items()}
    vecs1 = []
    for l in range(DEPTH):
        mu = a["rwkv_mu"][l]
        mu = np.concatenate([mu[1536:], mu[512:1024], mu[0:512], mu[1024:1536]])
        v = {"mu": mu, "w0": a["rwkv_w0"][l], "a0": a["rwkv_a0"][l], "k_k": a["rwkv_k_k"][l],
             "k_a": a["rwkv_k_a"][l], "r_k": a["rwkv_r_k"][l], "gn_g": a["rwkv_gn_g"][l],
             "gn_b": a["rwkv_gn_b"][l], "q_norm": a["mla_q_norm"][l],
             "kv_norm": a["mla_kv_norm"][l], "ln1_g": a["ln1_g"][l], "ln1_b": a["ln1_b"][l],
             "conv_b": a["ffn_conv_b"][l], "ln2_g": a["ln2_g"][l], "ln2_b": a["ln2_b"][l]}
        for t in range(3):
            v[f"conv{t}"] = a["ffn_conv_w"][l, t]
        vecs1.append(feature_columns(LAYER_VECS, NV1, v))
    v = {"c": a["c_2"], "b_mod": a["b_mod_2"], "mix_g": a["norm_mix_g_2"],
         "ffn_g": a["norm_ffn_g_2"], "b_y": a["lru_b_y_2"], "b_in": a["lru_b_in_2"],
         "conv_b": a["lru_conv_b_2"], "b_a": a["lru_b_a_2"], "b_x": a["lru_b_x_2"],
         "lam": a["lru_lambda_2"], "b_out": a["lru_b_out_2"], "pool_scale": a["pool_scale_2"],
         "final_g": a["final_norm_g_2"]}
    for t in range(4):
        v[f"conv{t}"] = a["lru_conv_w_2"][0, t]
    w_mod = a["w_mod_2"].reshape(DEPTH, KT, P, 48, P).transpose(0, 3, 2, 1, 4)
    arrays = {
        "x_t": np.ascontiguousarray(a["x"][0].T.reshape(KT, P, S).transpose(1, 0, 2)),
        "stream": weight_stream(a),
        "mod_stream": np.ascontiguousarray(w_mod.reshape(DEPTH * 48, P, KT, P)),
        "vecs1": np.stack(vecs1),
        "vecs2": feature_columns(VECS2, NV2, v),
        "consts": constants(),
    }
    nc = bacc.Bacc("TRN2", target_bir_lowering=False, num_devices=1)
    args = [nc.dram_tensor(n, v.shape, F32, kind="ExternalInput").ap() for n, v in arrays.items()]
    out = nc.dram_tensor("y_t", (KT, P, S), F32, kind="ExternalOutput").ap()
    build(nc, *args, out)
    r = run_bass_kernel_spmd(nc, [arrays], core_ids=[0])
    y = r.results[0]["y_t"]
    return np.ascontiguousarray(y.reshape(D, S).T[None])
```

```python
from contextlib import ExitStack, contextmanager

import numpy as np

import concourse.bass as bass
from concourse import mybir

F32 = mybir.dt.float32
F32R = mybir.dt.float32r
I32 = mybir.dt.int32
ALU = mybir.AluOpType
ACT = mybir.ActivationFunctionType
AX_X = mybir.AxisListType.X

P = 128
S = 512
D = 1024
KT = D // P
CHUNK = KT * P
BLOCKS = S // P
DEPTH = 2
HD = 64
F1, F2 = 2816, 4096
GROUPS1 = (8, 8, 6)
GROUPS2 = F2 // P // 8
POOL_WINDOWS = (2, 4, 8, 16)
ALPHA = (2 * DEPTH) ** 0.25
SB_SCALE = HD ** -0.5
MLA_SCALE = (64 + 32) ** -0.5
DECAY = float(np.exp(-0.5))
LN_EPS, RMS_EPS, GN_EPS = 1e-5, 1e-6, 64e-5
NEG = -1e30
LEVELS = (1, 2, 4, 8, 16, 32)

C_WAG, C_KRV = 0, 2
C_SB, C_MLA = 14, 20
C_UP, C_LORA = 23, 25
C_WO = 26
C_FFN = []
_s = C_WO + KT
for _g in GROUPS1:
    C_FFN.append((_s, _s + 2 * _g))
    _s += 2 * _g + KT
LC = _s
SPECIAL1 = (C_UP, C_UP + 1, C_LORA)
C_Y, C_IN, C_AX, C_OUT, C_F0 = 0, 8, 16, 20, 28
C_POOL = C_F0 + 16 * GROUPS2
C_F1 = C_POOL + 2
LC2 = C_F1 + 16 * GROUPS2
SPECIAL2 = (16, 17, 18, 19, C_POOL, C_POOL + 1)
CHUNKS = DEPTH * LC + LC2


def uses_before(s, special):
    return sum(1 for c in range(s % 2, s, 2) if c not in special)


USES1 = [uses_before(LC + p, SPECIAL1) for p in range(2)]


class Place:

    def __init__(self, pair0, use0, special):
        self.pair0, self.use0, self.special = pair0, use0, special

    def chunk(self, s, i=0):
        return self.pair0 * 2 + s + i * 2

    def landed(self, s, i=0):
        return (self.pair0 + s // 2 + i + 1) * 16

    def use(self, s, i=0):
        return self.use0[s % 2] + uses_before(s, self.special) + i


def place1(layer):
    return Place(layer * (LC // 2), [layer * USES1[0], layer * USES1[1]], SPECIAL1)


PLACE2 = Place(DEPTH * LC // 2, [DEPTH * USES1[0], DEPTH * USES1[1]], SPECIAL2)

LAYER_VECS = [("mu", 14), ("w0", 4), ("a0", 4), ("k_k", 4), ("k_a", 4), ("r_k", 4), ("gn_g", 4),
              ("gn_b", 4), ("q_norm", 2), ("kv_norm", 1), ("ln1_g", 8), ("ln1_b", 8),
              ("conv0", 22), ("conv1", 22), ("conv2", 22), ("conv_b", 22), ("ln2_g", 8),
              ("ln2_b", 8)]
VECS2 = [("c", 8), ("b_mod", 96), ("mix_g", 16), ("ffn_g", 16), ("b_y", 8), ("b_in", 8),
         ("conv0", 8), ("conv1", 8), ("conv2", 8), ("conv3", 8), ("conv_b", 8), ("b_a", 8),
         ("b_x", 8), ("lam", 8), ("b_out", 8), ("pool_scale", 8), ("final_g", 8)]


def columns(vecs):
    at, out = 0, {}
    for name, n in vecs:
        out[name] = at
        at += n
    return out, at


V1, NV1 = columns(LAYER_VECS)
V2, NV2 = columns(VECS2)

CONSTS = [("ident", 128), ("neg_sb", 128), ("neg_mla", 128), ("upper", 128), ("lower", 128),
          ("upper_incl", 128), ("heads", 128), ("ones", 128), ("lev_x", 6 * 128),
          ("lev_xt", 6 * 128), ("rope", S), ("chunk_mask", S), ("pool_fix", 64)]
VC, NVC = columns(CONSTS)


def constants():
    c = np.zeros((P, NVC), np.float32)
    i, j = np.arange(P)[:, None], np.arange(P)[None, :]
    same = (i // HD) == (j // HD)

    def put(name, a, n=0):
        c[:, VC[name] + n:VC[name] + n + a.shape[1]] = a

    put("ident", (i == j))
    put("neg_sb", np.where(j >= i, NEG, 0.0))
    put("neg_mla", np.where(j > i, NEG, 0.0))
    put("upper", same & (i < j))
    put("lower", same & (j < i))
    put("upper_incl", same & (i <= j))
    put("heads", same)
    put("ones", np.ones((P, P)))
    for n, b in enumerate(LEVELS):
        low = (i // (2 * b) == j // (2 * b)) & (i // b % 2 == 1) & (j // b % 2 == 0)
        put("lev_x", low, n * P)
        put("lev_xt", low.T, n * P)
    inv = 1.0 / (np.float32(10000.0) ** (np.arange(0, 32, 2, dtype=np.float32) / np.float32(32)))
    ang = np.arange(S, dtype=np.float32)[:, None] * inv[None].astype(np.float32)
    cos, sin = np.cos(ang).T.astype(np.float32), np.sin(ang).T.astype(np.float32)
    rope = np.zeros((P, S), np.float32)
    rope[64:96] = np.concatenate([cos, cos])
    rope[96:128] = np.concatenate([-sin, sin])
    put("rope", rope)
    put("chunk_mask", np.broadcast_to((np.arange(S) % HD != 0), (P, S)))
    for g, win in enumerate(POOL_WINDOWS):
        t = np.arange(16)
        put("pool_fix", np.broadcast_to(win / np.minimum(t + 1.0, win), (P, 16)), 16 * g)
    return c


PER = {"layer": 129, "pool": 111}


class Chain:

    def __init__(self, eng, sem, apart=None):
        self.eng, self.sem, self.base, self.n, self.apart = eng, sem, 0, 0, apart

    def __call__(self, ins):
        ins.then_inc(self.sem, 1)
        self.n += 1
        wait = self.apart or type(self.eng).wait_ge
        wait(self.eng, self.sem, self.base + self.n)

    @contextmanager
    def loop(self, count, calls):
        base, n = self.base, self.n
        with self.eng.Fori(0, count) as i:
            self.base, self.n = base + n + i * calls, 0
            yield i
            assert self.n == calls, f"{self.n} calls in the loop's body, {calls} given"
        self.base, self.n = base, n + count * calls


def build(nc, x_in, stream, mod_stream, vecs1, vecs2, consts, out):
    ctx = ExitStack()
    with ctx:
        top = [nc.sbuf_usable_end - nc.sbuf_bytes_remaining + 63]
        top[0] -= top[0] % 64
        limit = nc.sbuf_usable_end

        def at(name, shape, offset, dt=F32):
            size = 4 * int(np.prod(shape[1:]))
            assert offset + size <= limit, (name, offset, size, limit)
            return nc.alloc_sbuf_tensor_at(name, shape, dt, offset=offset)

        def sb(name, shape, dt=F32):
            t = at(name, shape, top[0], dt)
            top[0] += (4 * int(np.prod(shape[1:])) + 31) // 32 * 32
            return t

        x = sb("x", [P, KT, S])
        xh = sb("xh", [P, KT, S], F32R)
        xl = sb("xl", [P, KT, S], F32R)
        raw = sb("raw", [P, 2, CHUNK])
        wh = sb("wh", [P, 2, KT, P], F32R)
        wl = sb("wl", [P, 2, KT, P], F32R)
        cst = sb("cst", [P, NVC])
        pv_next = sb("pv_next", [P, NV1])
        pv = sb("pv", [P, NV1])
        one_minus = sb("one_minus", [P, 14 + 4])
        pv2 = sb("pv2", [P, NV2])
        cond = sb("cond", [P, KT])
        mod = sb("mod", [P, DEPTH, 48])
        small = sb("small", [P, 16, 8])
        stat = sb("stat", [P, 4, 8])
        krv_at = top[0]
        krv = sb("krv", [P, 12, S])
        norm_sum = at("norm_sum", [P, S], krv_at)
        norm_sq = at("norm_sq", [P, S], krv_at + 2048)
        sq = at("sq", [P, 2, S], krv_at + 4096)
        nt = at("nt", [P, 2, S], krv_at + 12288)
        wag_at = top[0]
        wag = sb("wag", [P, 2, S])
        u0 = at("u0", [P, S], wag_at)
        uu = at("uu", [P, S], wag_at + 2048)
        r0 = top[0]

        class Region:
            def __init__(self, start):
                self.at = start

            def __call__(self, name, shape, dt=F32):
                t = at(name, shape, self.at, dt)
                self.at += (4 * int(np.prod(shape[1:])) + 31) // 32 * 32
                return t

        rg = Region(r0)
        sbq = rg("sbq", [P, 2, S])
        sbk = rg("sbk", [P, 2, S])
        cq_at = rg.at
        cq = rg("cq", [P, 2, S])
        ckv = rg("ckv", [P, S])
        krot = rg("krot", [P, S])
        vsb_at = rg.at
        vsb = rg("vsb", [P, BLOCKS, 256])
        vmla = rg("vmla", [P, BLOCKS, 256])
        qh_at = rg.at
        qh = rg("qh", [P, 4, S])
        kh = rg("kh", [P, 4, S])
        at0 = rg.at
        sbvT = rg("sbvT", [P, 2, S])
        csq = rg("csq", [P, 3, S])
        crs = rg("crs", [P, 2, S])
        rope_t = rg("rope_t", [P, 2, S])
        rg = Region(at0)
        keep = rg("keep", [P, 2, S])
        sig = rg("sig", [P, 2, S])
        later = rg("later", [P, 2, S])
        wts = rg("wts", [P, 2, S])
        wT = rg("wT", [P, 2, S])
        wts_end = rg.at
        rg = Region(wts_end)
        gg = rg("gg", [P, 4, S])
        aa = rg("aa", [P, 4, S])
        cum_at = rg.at
        cum = rg("cum", [P, 4, S])
        decay = rg("decay", [P, 2, S])
        kk = at("kk", [P, 4, S], cq_at)
        bv = at("bv", [P, 4, S], r0)
        e1 = at("e1", [P, 4, S], vsb_at)
        tmp4 = at("tmp4", [P, 4, S], qh_at)
        rg = Region(vsb_at)
        mt = rg("mt", [P, 8, P])
        nT = rg("nT", [P, 8, P])
        rg = Region(qh_at)
        lbT = rg("lbT", [P, 8, P])
        lkT = rg("lkT", [P, 8, P])
        xi = rg("xi", [P, 8, P])
        px = rg("px", [P, 8, P])
        xiT = rg("xiT", [P, 8, P])
        stage_at = rg.at
        stage = rg("stage", [P, 5, 4, P])
        mcc = rg("mcc", [P, 2, 4, P])
        cc = rg("cc", [P, 4, 8])
        assert rg.at <= wts_end
        rg = Region(cum_at)
        tok = rg("tok", [P, 3, 4 * P])
        st = rg("st", [P, 4, 4, P])
        yy = at("yy", [P, 4, S], krv_at)
        rg = Region(stage_at)
        yc = rg("yc", [P, 2, S])
        ysq = rg("ysq", [P, 2, S])
        rg = Region(r0)
        hidh = rg("hidh", [P, 8, S], F32R)
        hidl = rg("hidl", [P, 8, S], F32R)
        hf = rg("hf", [P, 2, S])
        ua = rg("ua", [P, S + 4])
        cv = rg("cv", [P, S])
        gel = rg("gel", [P, S])
        mraw_at = rg.at
        mraw = rg("mraw", [P, 2, KT, P])
        mred = rg("mred", [P, 2, P])
        blk2_at = rg.at
        gate = rg("gate", [P, 8, S])
        ga = at("ga", [P, 4, S], krv_at + 16384)
        gx = at("gx", [P, 4, S], mraw_at)
        xc = rg("xc", [P, 8, S])
        rg = Region(blk2_at)
        hp = rg("hp", [P, 2, S])
        cs = rg("cs", [P, 2, S + 16])

        tb = [hf[:, 0, :], hf[:, 1, :], gel[:], cv[:]]

        dbank = [ctx.enter_context(nc.psum_tensor(f"dense{i}", [P, S], F32)) for i in range(2)]
        aux = [ctx.enter_context(nc.psum_tensor(f"aux{i}", [P, S], F32)) for i in range(6)]

        def sem(name):
            return ctx.enter_context(nc.semaphore(name))

        def const(name, rows=slice(0, P), n=None, off=0):
            n = n if n is not None else dict(CONSTS)[name]
            return cst[rows, VC[name] + off:VC[name] + off + n]

        def vec(name, t, rows=slice(0, P)):
            return pv[rows, bass.ds(V1[name] + t, 1)]

        def vec2(name, t):
            return pv2[:, bass.ds(V2[name] + t, 1)]

        x_landed = [sem(f"x_landed{n}") for n in range(4)]
        in_landed = sem("in_landed")
        vecs_landed = sem("vecs_landed")
        vecs_ready = sem("vecs_ready")
        w_landed = [sem("w_landed0"), sem("w_landed1")]
        hi_done = sem("hi_done")
        lo_done = sem("lo_done")
        pe_chunk = sem("pe_chunk")
        bank_free = [sem("bank0_read"), sem("bank1_read")]
        mod_landed = [sem("mod_landed0"), sem("mod_landed1")]
        mod_mul, mod_red, mod_pe, mod_out = (sem("mod_mul"), sem("mod_red"), sem("mod_pe"),
                                             sem("mod_out"))
        cond_sig, cond_ready, vecs2_ready = sem("cond_sig"), sem("cond_ready"), sem("vecs2_ready")
        xh_ready, xl_ready = sem("xh_ready"), sem("xl_ready")
        dve_chain, act_chain, pool_chain = sem("dve_chain"), sem("act_chain"), sem("pool_chain")
        sq_ready, sums_tile, sums_pe = sem("sq_ready"), sem("sums_tile"), sem("sums_pe")
        var_ready, sd_ready, stat_ready, rows_pe = (sem("var_ready"), sem("sd_ready"),
                                                    sem("stat_ready"), sem("rows_pe"))
        n_mul, n_aff = sem("n_mul"), sem("n_aff")
        shift_a, shift_d = sem("shift_a"), sem("shift_d")
        vtok_pe, vtok_ready = sem("vtok_pe"), sem("vtok_ready")
        csq_ready, c_ms, c_var, c_sd = sem("csq_ready"), sem("c_ms"), sem("c_var"), sem("c_sd")
        c_norm, ch_ready, cl_ready = sem("c_norm"), sem("ch_ready"), sem("cl_ready")
        up_pe, up_act, up_dve = sem("up_pe"), sem("up_act"), sem("up_dve")
        krot_ready, kh_rope = sem("krot_ready"), sem("kh_rope")
        z_ready, w_act, mx_ready, w_ready = (sem("z_ready"), sem("w_act"), sem("mx_ready"),
                                             sem("w_ready"))
        t_ready, wT_ready, av_done = sem("t_ready"), sem("wT_ready"), sem("av_done")
        mixh_ready, mixl_ready = sem("mixh_ready"), sem("mixl_ready")
        wag_ready, lh_ready, ll_ready = sem("wag_ready"), sem("lora_h"), sem("lora_l")
        lora_pe, lora_read = sem("lora_pe"), sem("lora_read")
        cum_ready, e_ready, kk0_ready, kksq_ready = (sem("cum_ready"), sem("e_ready"),
                                                     sem("kk0_ready"), sem("kksq_ready"))
        ss_pe, ss_max, kn_sd = sem("ss_pe"), sem("ss_max"), sem("kn_sd")
        xi_ready, xt_ready = sem("xi_ready"), sem("xt_ready")
        bonus_read, rhat_ready = sem("bonus_read"), sem("rhat_ready")
        rkk_ready, bonus_pe, hats_ready = sem("rkk_ready"), sem("bonus_pe"), sem("hats_ready")
        zero_ready, eye_ready, stage_ready, mcc_ready = (sem("zero_ready"), sem("eye_ready"),
                                                         sem("stage_ready"), sem("mcc_ready"))
        tok_pe, tok_ready, mm5_pe, mm5_read = (sem("tok_pe"), sem("tok_ready"), sem("mm5_pe"),
                                               sem("mm5_read"))
        p_pe, p_read, q_pe, q_read = sem("p_pe"), sem("p_read"), sem("q_pe"), sem("q_read")
        u0_pe, u0_read, u_pe, u_read = sem("u0_pe"), sem("u0_read"), sem("u_pe"), sem("u_read")
        s_pe, st_sum, state_ready = sem("s_pe"), sem("st_sum"), sem("state_ready")
        y_pe, y_read = sem("y_pe"), sem("y_read")
        gm_pe, yc_ready, ysq_ready, gv_pe, gvar_ready, gsd_ready = (
            sem("gm_pe"), sem("yc_ready"), sem("ysq_ready"), sem("gv_pe"), sem("gvar_ready"),
            sem("gsd_ready"))
        gn_mul, gn_aff, yf_ready = sem("gn_mul"), sem("gn_aff"), sem("yf_ready")
        ua_zero, ua_ready, conv_done, gel_ready = (sem("ua_zero"), sem("ua_ready"),
                                                   sem("conv_done"), sem("gel_ready"))
        hf_ready, hidh_ready, hidl_ready = sem("hf_ready"), sem("hidh_ready"), sem("hidl_ready")
        lam_a, lam_d, fold_ready = sem("lam_a"), sem("lam_d"), sem("fold_ready")
        xc_ready, ax_pe, ax_read, a_ready = (sem("xc_ready"), sem("ax_pe"), sem("ax_read"),
                                             sem("a_ready"))
        th_ready, a2_ready, m2_ready, m_ready, h_ready = (
            sem("th_ready"), sem("a2_ready"), sem("m2_ready"), sem("m_ready"), sem("h_ready"))
        window_ready, gx_ready = sem("window_ready"), sem("gx_ready")
        cs_ready = sem("cs_ready")
        y_add, relu_ready, pooled_ready, x_start = (sem("y_add"), sem("relu_ready"),
                                                    sem("pooled_ready"), sem("x_start"))
        out_tile, out_done = sem("out_tile"), sem("out_done")

        UNITS = [(kind, pair, i, e) for kind in ("sb", "mla") for pair in range(2)
                 for i in range(BLOCKS) for e in range(2)]
        NU = len(UNITS)
        zbank = (aux[0], aux[1], aux[3])
        LORA_AT = range(2, 14)
        BONUS_AT = (20, 23, 26, 29)
        MODS = 24
        HATS = {"A": kk, "B": aa, "K": krv[:, 0:4], "R": krv[:, 4:8], "V": krv[:, 8:12]}

        def heads4(a):
            return a.unsqueeze(1).to_broadcast([P, 4, P])

        def mask(name, n=0):
            return heads4(const(name, n=P, off=n * P))

        def bank4(b):
            return b[:].rearrange("q (h t) -> q h t", h=4)

        def wait_apart(eng, sem, value):
            eng.wait_ge(sem, value)
            eng.nop(nofuse=True)

        block = ctx.enter_context(nc.Block())

        @block.sync
        def _(sp):
            def load_x(n):
                t = slice(2 * n, 2 * n + 2)
                sp.dma_start(x[:, t, :], x_in[:, t, :]).then_inc(x_landed[n], 16)

            load_x(0)
            sp.dma_start(raw[:, 0, :], stream[0]).then_inc(w_landed[0], 16)
            load_x(1)
            sp.dma_start(raw[:, 1, :], stream[1]).then_inc(w_landed[1], 16)
            load_x(2)
            load_x(3)
            sp.dma_start(cst[:], consts).then_inc(in_landed, 16)
            sp.dma_start(pv2[:], vecs2).then_inc(in_landed, 16)
            sp.dma_start(pv_next[:], vecs1[0]).then_inc(vecs_landed, 16)

            def load(n, slot):
                sp.wait_ge(lo_done, n - 1)
                sp.dma_start(raw[:, slot, :], stream[n]).then_inc(w_landed[slot], 16)

            def load_mod(m, slot):
                sp.wait_ge(mod_red, m + 1)
                sp.dma_start(mraw[:, slot], mod_stream[m]).then_inc(mod_landed[slot], 16)

            first = C_FFN[0][0]
            with sp.Fori(0, DEPTH) as layer:
                n0 = layer * LC + 2
                with sp.Fori(0, first // 2) as i:
                    for j in range(2):
                        load(n0 + i * 2 + j, j)
                wait_apart(sp, mixl_ready, layer * 8 + 8)
                with sp.Fori(0, MODS) as i:
                    for j in range(2):
                        load(n0 + first + i * 2 + j, j)
                        load_mod(layer * 2 * MODS + i * 2 + j, j)
                sp.wait_ge(vecs_ready, layer + 1)
                sp.dma_start(pv_next[:], vecs1[DEPTH - 1]).then_inc(vecs_landed, 16)
                with sp.Fori(0, (LC - first) // 2 - MODS) as i:
                    for j in range(2):
                        load(n0 + first + 2 * MODS + i * 2 + j, j)
            with sp.Fori(0, LC2 // 2 - 1) as i:
                for j in range(2):
                    load(DEPTH * LC + 2 + i * 2 + j, j)
            for m in range(KT):
                sp.wait_ge(out_tile, m + 1)
                sp.dma_start(out[m], x[:, m, :]).then_inc(out_done, 16)
            sp.wait_ge(out_done, 16 * KT)

        @block.tensor
        def _(pe):
            def split_product(o, w, w_rows, k_rhs, first, last):
                (slot, cols), (h, l) = w, k_rhs
                a = wh[w_rows, slot].rearrange("p k m -> p (k m)")[:, cols:cols + P]
                b = wl[w_rows, slot].rearrange("p k m -> p (k m)")[:, cols:cols + P]
                pe.matmul(o, a, h, start=first, stop=False)
                pe.matmul(o, a, l, start=False, stop=False)
                return pe.matmul(o, b, h, start=False, stop=last)

            def dense(pl, s, i, h, l, tiles=KT, tile_sem=None, tile_at=0):
                slot = s % 2
                pe.wait_ge(lo_done, pl.chunk(s, i) + 1)
                pe.wait_ge(bank_free[slot], pl.use(s, i))
                for k in range(tiles):
                    if tile_sem is not None:
                        pe.wait_ge(tile_sem, tile_at + k + 1)
                    m = split_product(dbank[slot][:], (slot, k * P), slice(0, P),
                                      (h[:, k, :], l[:, k, :]), k == 0, k == tiles - 1)
                m.then_inc(pe_chunk, 1)

            def section(pl, s, count, h, l, tiles=KT, tile_sem=None, tile_at=0, extra=None,
                        late=None):
                for j in range(2):
                    dense(pl, s + j, 0, h, l, tiles, tile_sem if j == 0 else None, tile_at)
                    if late:
                        late(j)
                if count > 2:
                    with pe.Fori(1, count // 2) as i:
                        for j in range(2):
                            dense(pl, s + j, i, h, l, tiles)
                            if extra:
                                extra(i - 1, j)
                return (lambda j: extra(count // 2 - 1, j)) if extra else None

            def norm_sums(k, centred=False):
                pe.wait_ge(sums_tile, 8 * k + 10)
                for n, src in ((0, norm_sum), (1, norm_sq))[0 if centred else 1:]:
                    for t in range(BLOCKS):
                        m = pe.matmul(aux[4][:, 4 * n + t:4 * n + t + 1],
                                      src[:, t * P:(t + 1) * P], const("ones", n=1),
                                      start=True, stop=True)
                m.then_inc(sums_pe, 1)
                pe.wait_ge(stat_ready, k + 1)
                for n in range(2 if centred else 1):
                    for t in range(BLOCKS):
                        m = pe.matmul(aux[4 + n][:, t * P:(t + 1) * P],
                                      stat[:, 2 + n, t:t + 1].to_broadcast([P, P]),
                                      const("ident"), start=True, stop=True)
                m.then_inc(rows_pe, 1)

            def latent(L, pl):
                pe.wait_ge(in_landed, 32)
                pe.wait_ge(csq_ready, L + 1)
                pe.matmul(aux[0][:], const("ones"), csq[:, 0, :], start=True, stop=False)
                pe.matmul(aux[0][:], const("ones", slice(0, 64)), csq[0:64, 1, :],
                          start=False, stop=True)
                pe.matmul(aux[1][:], const("ones"), csq[:, 2, :], start=True, stop=True)\
                  .then_inc(c_ms, 1)
                for tb in range(BLOCKS):
                    for p in range(2):
                        o = aux[2 + tb // 2][:, 256 * (tb % 2) + P * p:256 * (tb % 2) + P * p + P]
                        m = pe.transpose(o, sbvT[:, p, tb * P:(tb + 1) * P], const("ident"))
                m.then_inc(vtok_pe, 1)
                pe.wait_ge(lo_done, pl.chunk(C_UP + 1) + 1)
                pe.wait_ge(cl_ready, L * 3 + 3)
                pe.wait_ge(vtok_ready, L * 2 + 2)
                s0, s1 = C_UP % 2, (C_UP + 1) % 2
                for h in range(4):
                    split_product(aux[h][:], (s0, h * P), slice(0, P), (xh[:, 4, :], xl[:, 4, :]),
                                  True, False)
                    split_product(aux[h][:], (s1, h * P), slice(0, 64),
                                  (xh[0:64, 5, :], xl[0:64, 5, :]), False, True)\
                        .then_inc(up_pe, 1)
                for p in range(2):
                    split_product(aux[4 + p][:], (s0, 512 + p * P), slice(0, P),
                                  (xh[:, 6, :], xl[:, 6, :]), True, True).then_inc(up_pe, 1)
                ukv_h = wh[:, s0].rearrange("p k m -> p (k m)")[:, 768:1024]
                ukv_l = wl[:, s0].rearrange("p k m -> p (k m)")[:, 768:1024]
                for tb in range(BLOCKS):
                    if tb % 2 == 0:
                        pe.wait_ge(up_act, L * 8 + 1 + tb // 2)
                        pe.wait_ge(up_dve, L * 4 + 1 + tb // 2)
                    o = aux[tb // 2][:, 256 * (tb % 2):256 * (tb % 2) + 256]
                    th, tl = xh[:, 6, tb * P:(tb + 1) * P], xl[:, 6, tb * P:(tb + 1) * P]
                    pe.matmul(o, th, ukv_h, start=True, stop=False)
                    pe.matmul(o, th, ukv_l, start=False, stop=False)
                    m = pe.matmul(o, tl, ukv_h, start=False, stop=True)
                m.then_inc(pe_chunk, 2)

            def attention(L, pl):
                def scores(u):
                    kind, pair, i, e = UNITS[u]
                    n, q0, z = (i + 1) * P, i * P, zbank[u % 3]
                    if u >= 3:
                        pe.wait_ge(w_act, L * NU + u - 2)
                    if kind == "sb":
                        r = slice(64 * e, 64 * e + 64)
                        pe.matmul(z[:, 0:n], sbq[r, pair, q0:q0 + P], sbk[r, pair, 0:n],
                                  start=True, stop=False)
                    else:
                        h = 2 * pair + e
                        pe.matmul(z[:, 0:n], qh[0:96, h, q0:q0 + P], kh[0:96, h, 0:n],
                                  start=True, stop=False)
                    neg = const("neg_sb" if kind == "sb" else "neg_mla")
                    pe.matmul(z[:, q0:q0 + P], const("ident"), neg, start=False, stop=True)\
                      .then_inc(z_ready, 1)

                def turn(u):
                    i = UNITS[u][2]
                    pe.wait_ge(w_ready, L * NU + u + 1)
                    if u >= 1:
                        pe.wait_ge(wT_ready, L * NU + u)
                    for j in range(i + 1):
                        m = pe.transpose(aux[2][:, j * P:(j + 1) * P],
                                         wts[:, u % 2, j * P:(j + 1) * P], const("ident"))
                    m.then_inc(t_ready, 1)

                def values(u):
                    kind, pair, i, e = UNITS[u]
                    q = (2 if kind == "mla" else 0) + pair
                    pe.wait_ge(wT_ready, L * NU + u + 1)
                    if i == 0 and e == 0 and q >= 2:
                        pe.wait_ge(mixl_ready, L * 8 + q - 1)
                    v = vsb if kind == "sb" else vmla
                    o = aux[4 + q % 2][64 * e:64 * e + 64, i * P:(i + 1) * P]
                    for j in range(i + 1):
                        m = pe.matmul(o, v[:, j, 128 * pair + 64 * e:128 * pair + 64 * e + 64],
                                      wT[:, u % 2, j * P:(j + 1) * P],
                                      start=(j == 0), stop=(j == i))
                    m.then_inc(av_done, 1)

                def lora(n):
                    if n == 0:
                        pe.wait_ge(lo_done, pl.chunk(C_LORA) + 1)
                        pe.wait_ge(ll_ready, L * 2 + 2)
                    if n < 2:
                        pe.wait_ge(bank_free[n], pl.use(C_WO + n))
                    else:
                        pe.wait_ge(lora_read, L * 12 + n - 1)
                    p, what, slot = n // 3, n % 3, C_LORA % 2
                    r, col, t = ((slice(0, 64), p * P, 4), (slice(64, P), p * P, 4),
                                 (slice(0, P), 512 + p * P, 5))[what]
                    split_product(dbank[n % 2][:], (slot, col), r, (xh[r, t, :], xl[r, t, :]),
                                  True, True).then_inc(lora_pe if n < 11 else pe_chunk, 1)

                def bonus(p):
                    pe.wait_ge(rkk_ready, L * 4 + p + 1)
                    if p < 2:
                        pe.wait_ge(lora_read, L * 12 + 12)
                    else:
                        pe.wait_ge(bonus_read, L * 4 + p - 1)
                    pe.matmul(dbank[p % 2][:], const("heads"), decay[:, p % 2, :], start=True,
                              stop=True).then_inc(bonus_pe, 1)

                pe.wait_ge(vtok_ready, L * 2 + 2)
                pe.wait_ge(kh_rope, L + 1)
                pe.wait_ge(up_dve, L * 4 + 4)
                pe.wait_ge(up_act, L * 8 + 8)
                scores(0)
                scores(1)
                for u in range(NU):
                    if u + 2 < NU:
                        scores(u + 2)
                    turn(u)
                    if u >= 1:
                        values(u - 1)
                    if u in LORA_AT:
                        lora(u - LORA_AT[0])
                    if u in BONUS_AT:
                        bonus(BONUS_AT.index(u))
                values(NU - 1)

            def recurrence_inputs(L, pl):
                for p in range(4):
                    pe.wait_ge(kksq_ready, L * 4 + p + 1)
                    pe.matmul(aux[p][:], const("heads"), tmp4[:, p, :], start=True, stop=True)\
                      .then_inc(ss_pe, 1)

            def recurrence_block(B, b, half):
                A, Bh, K, R, V = (stage[:, n] for n in range(5))
                R_now = HATS["R"][:, :, bass.ts(b, P)]
                pe.wait_ge(stage_ready, B * 2 + 1)
                pe.wait_ge(state_ready, B * 2)
                for n, src in enumerate((Bh, K, V)):
                    for p in range(4):
                        m = pe.transpose(aux[n][:, p * P:(p + 1) * P], src[:, p, :],
                                         const("ident"))
                    m.then_inc(tok_pe, 1)
                pe.wait_ge(stage_ready, B * 2 + 2)
                pe.wait_ge(y_read, B * 2)
                q = 0
                for left, right in ((Bh, A), (K, A), (Bh, R), (K, R)):
                    for g in range(2):
                        b = aux[(3 + q) % 6]
                        if 3 <= q < 6:
                            pe.wait_ge(tok_ready, B * 3 + q - 2)
                        if q >= 6:
                            pe.wait_ge(mm5_read, B * 8 + q - 5)
                        r = slice(64 * g, 64 * g + 64)
                        for p in range(4):
                            m = pe.matmul(b[:, p * P:(p + 1) * P], left[r, p, :],
                                          right[r, p, :], start=True, stop=True)
                        m.then_inc(mm5_pe, 1)
                        q += 1
                for n in range(1, 6):
                    for g in range(2):
                        if n == 1:
                            pe.wait_ge(xi_ready, B * 2 + g + 1)
                            pe.wait_ge(mm5_read, B * 8 + 4 + g)
                        else:
                            pe.wait_ge(q_read, B * 10 + 2 * (n - 2) + g + 1)
                        for h4 in range(4):
                            h = 4 * g + h4
                            m = pe.matmul(aux[g][:, h4 * P:(h4 + 1) * P], mt[:, h, :],
                                          xi[:, h, :], start=True, stop=True)
                        m.then_inc(p_pe, 1)
                    for g in range(2):
                        pe.wait_ge(p_read, B * 10 + 2 * (n - 1) + g + 1)
                        if n == 1:
                            pe.wait_ge(mm5_read, B * 8 + 6 + g)
                        else:
                            pe.wait_ge(xt_ready, B * 8 + 2 * (n - 2) + g + 1)
                        for h4 in range(4):
                            h = 4 * g + h4
                            o = aux[(2 if n < 5 else 4) + g][:, h4 * P:(h4 + 1) * P]
                            a, b = (xiT, px) if n < 5 else (px, xiT)
                            m = pe.matmul(o, a[:, h, :], b[:, h, :], start=True, stop=True)
                        m.then_inc(q_pe, 1)
                tB, tK, tV = (tok[:, n, :] for n in range(3))
                pe.wait_ge(mm5_read, B * 8 + 8)
                for h in range(8):
                    pe.matmul(aux[0][:, h * 64:(h + 1) * 64], nT[:, 4 * (h % 2) + h // 2, :],
                              tV[:, h * 64:(h + 1) * 64], start=(h == 0), stop=False,
                              skip_group_check=True)
                for c in range(2):
                    s_in = st[:, (2 * half + c) % 4]
                    rows = slice(64 * c, 64 * c + 64)
                    pe.wait_ge(state_ready, B * 2 + c)
                    for p in range(4):
                        m = pe.matmul(aux[0][rows, p * P:(p + 1) * P], A[:, p, rows],
                                      s_in[:, p, :], start=False, stop=(p == 3),
                                      skip_group_check=True)
                    m.then_inc(u0_pe, 1)
                    for p in range(4):
                        cols = slice(p * P, (p + 1) * P)
                        pe.matmul(aux[2][:, cols], tK[rows, cols], tV[rows, cols],
                                  start=(p == 0), stop=False, skip_group_check=True)
                    pe.wait_ge(q_read, B * 10 + 10)
                    wait_apart(pe, u0_read, B * 2 + c + 1)
                    for h in range(8):
                        m = pe.matmul(aux[1][rows, h * 64:(h + 1) * 64],
                                      xiT[rows, 4 * (h % 2) + h // 2, rows],
                                      u0[rows, h * 64:(h + 1) * 64], start=True, stop=True)
                    m.then_inc(u_pe, 1)
                    pe.wait_ge(u_read, B * 2 + c + 1)
                    for p in range(4):
                        cols = slice(p * P, (p + 1) * P)
                        m = pe.matmul(aux[2][:, cols], tB[rows, cols], uu[rows, cols],
                                      start=False, stop=(p == 3), skip_group_check=True)
                    m.then_inc(s_pe, 1)
                for p in range(4):
                    o = aux[3 + p // 2][:, (p % 2) * 256:(p % 2) * 256 + 256]\
                        .rearrange("q (g t) -> q g t", g=2)
                    cols = slice(p * P, (p + 1) * P)
                    pe.matmul(o, uu[:, cols], lbT[:, p:p + 5:4, :], start=(p % 2 == 0),
                              stop=False, skip_group_check=True)
                    pe.matmul(o, tV[:, cols], lkT[:, p:p + 5:4, :], start=False, stop=False,
                              skip_group_check=True)
                    for c in range(2):
                        t = slice(64 * c, 64 * c + 64)
                        m = pe.matmul(o[:, :, t], st[:, (2 * half + c) % 4, p, :],
                                      R_now[:, p, t].unsqueeze(1).to_broadcast([P, 2, 64]),
                                      start=False, stop=(p % 2 == 1 and c == 1),
                                      skip_group_check=True)
                    if p % 2:
                        m.then_inc(y_pe, 1)

            def group_norm(L):
                for q in range(2):
                    for r in range(2):
                        if q == 0:
                            pe.wait_ge(y_read, (L + 1) * 8)
                        pe.matmul(aux[r][:], const("heads"), yy[:, 2 * q + r, :], start=True,
                                  stop=True).then_inc(gm_pe, 1)
                    for r in range(2):
                        pe.wait_ge(ysq_ready, L * 4 + 2 * q + r + 1)
                        if q:
                            pe.wait_ge(gvar_ready, L * 4 + r + 1)
                        pe.matmul(aux[2 + r][:], const("heads"), ysq[:, r, :], start=True,
                                  stop=True).then_inc(gv_pe, 1)

            with pe.Fori(0, DEPTH) as L:
                pl = place1(L)
                section(pl, 0, C_UP - 1, xh, xl, tile_sem=xl_ready, tile_at=L * 16)
                dense(pl, C_UP - 1, 0, xh, xl)
                latent(L, pl)
                attention(L, pl)
                recurrence_inputs(L, pl)
                wait_apart(pe, zero_ready, L + 1)
                with pe.Fori(0, 2) as i:
                    for half in range(2):
                        recurrence_block(L * 4 + i * 2 + half, i * 2 + half, half)
                group_norm(L)
                section(pl, C_WO, KT, xh, xl, tile_sem=mixl_ready, tile_at=L * 8)
                norm_sums(L * 2, True)
                def mod_sum(m0):
                    def one(i, j):
                        m = m0 + i * 2 + j
                        pe.wait_ge(mod_red, L * 2 * MODS + m + 3)
                        pe.matmul(aux[0][:, bass.ds(m, 1)], mred[:, j, :], const("ones", n=1),
                                  start=True, stop=True).then_inc(mod_pe, 1)
                    return one

                late = None
                for g, tiles in enumerate(GROUPS1):
                    up, down = C_FFN[g]
                    late = section(pl, up, 2 * tiles, xh, xl,
                                   tile_sem=xl_ready if g == 0 else None, tile_at=L * 16 + 8,
                                   extra=mod_sum(g * MODS) if g < 2 else None, late=late)
                    late = section(pl, down, KT, hidh, hidl, tiles, tile_sem=hidl_ready,
                                   tile_at=L * 22 + 8 * g,
                                   extra=mod_sum(g * MODS + 16) if g < 2 else None, late=late)
                norm_sums(L * 2 + 1, True)

            pl = PLACE2
            H0 = DEPTH * 22
            norm_sums(4)
            section(pl, C_Y, 16, xh, xl, tile_sem=xl_ready, tile_at=40)
            for h in range(4):
                pe.wait_ge(lo_done, pl.chunk(C_AX + h) + 1)
                pe.wait_ge(hidl_ready, H0 + 2 * h + 2)
                if h:
                    pe.wait_ge(ax_read, 4 * h)
                for o in range(4):
                    for k in range(2):
                        m = split_product(aux[o][:], (h % 2, (2 * o + k) * P), slice(0, P),
                                          (hidh[:, 2 * h + k, :], hidl[:, 2 * h + k, :]),
                                          k == 0, k == 1)
                m.then_inc(pe_chunk, 1)
            section(pl, C_OUT, KT, xh, xl, tile_sem=xl_ready, tile_at=48)
            norm_sums(5)
            H1 = H0 + 8

            def ffn2(c0, xl_at, hid_at):
                section(pl, c0, 8, xh, xl, tile_sem=xl_ready, tile_at=xl_at)
                section(pl, c0 + 8, 8, hidh, hidl, tile_sem=hidl_ready, tile_at=hid_at)
                with pe.Fori(1, GROUPS2) as g:
                    pg = Place(pl.pair0 + g * 8, [pl.use0[0] + g * 8, pl.use0[1] + g * 8],
                               pl.special)
                    with pe.Fori(0, 4) as i:
                        for j in range(2):
                            dense(pg, c0 + j, i, xh, xl)
                    for j in range(2):
                        dense(pg, c0 + 8 + j, 0, hidh, hidl, 8,
                              hidl_ready if j == 0 else None, hid_at + g * 8)
                    with pe.Fori(1, 4) as i:
                        for j in range(2):
                            dense(pg, c0 + 8 + j, i, hidh, hidl)

            ffn2(C_F0, 56, H1)
            norm_sums(6)
            for c in range(2):
                pe.wait_ge(lo_done, pl.chunk(C_POOL + c) + 1)
                pe.wait_ge(xl_ready, 64 + 4 * c + 4)
                if c:
                    pe.wait_ge(y_add, 8 + 4)
                for o in range(4):
                    for k in range(2):
                        t = 4 * c + 2 * (o // 2) + k
                        m = split_product(aux[o][:], (c, (2 * o + k) * P), slice(0, P),
                                          (xh[:, t, :], xl[:, t, :]), k == 0, k == 1)
                m.then_inc(pe_chunk, 1)
            norm_sums(7)
            ffn2(C_F1, 72, H1 + 32)
            norm_sums(8)

        @block.scalar
        def _(act):
            chain = Chain(act, act_chain)

            def prepare(pl, s, i=0, lead=False):
                slot = s % 2
                act.wait_ge(w_landed[slot], pl.landed(s, i))
                if not lead:
                    act.wait_ge(pe_chunk, pl.chunk(s, i) - 1)
                act.activation(wh[:, slot].rearrange("p k m -> p (k m)"), raw[:, slot, :],
                               ACT.Copy).then_inc(hi_done, 1)

            def done(pl, s, i=0, more=True):
                if more:
                    prepare(pl, s + 2, i)
                else:
                    act.wait_ge(pe_chunk, pl.chunk(s, i) + 1)

            def squares(pl, k, s, m, i=0, j=0):
                act.wait_ge(bank_free[s % 2], pl.use(s, i) + 1)
                act.wait_ge(sums_tile, 8 * k + m + 1)
                act.activation(sq[:, j, :], x[:, m, :], ACT.Square).then_inc(sq_ready, 1)

            def norm_stats(k):
                act.wait_ge(var_ready, k + 1)
                act.activation(stat[:, 2, 0:4], stat[:, 2, 0:4], ACT.Sqrt).then_inc(sd_ready, 1)

            def split_hi(dst, src):
                act.activation(dst, src, ACT.Copy).then_inc(xh_ready, 1)

            def layer_norm(k, g, b, xk):
                norm_stats(k)
                for m in range(KT):
                    act.wait_ge(n_mul, 8 * k + m + 1)
                    act.activation(x[:, m, :], nt[:, m % 2, :], ACT.Identity,
                                   scale=vec(g, m), bias=vec(b, m)).then_inc(n_aff, 1)
                    act.wait_ge(n_aff, 8 * k + m + 1)
                    split_hi(xh[:, m, :], x[:, m, :])

            for m in range(KT):
                act.wait_ge(x_landed[m // 2], 16)
                split_hi(xh[:, m, :], x[:, m, :])
                if m in (0, 3):
                    prepare(place1(0), m % 2, 0, True)
            act.wait_ge(in_landed, 32)
            act.activation(cond[:], pv2[:, V2["c"]:V2["c"] + 8], ACT.Sigmoid)\
               .then_inc(cond_sig, 1)
            lam = pv2[:, V2["lam"]:V2["lam"] + 8]
            chain(act.activation(small[:, 0, :], lam, ACT.Abs))
            chain(act.activation(small[:, 0, :], small[:, 0, :], ACT.Exp, scale=-1.0))
            act.activation(small[:, 1, :], small[:, 0, :], ACT.Ln, bias=1.0).then_inc(lam_a, 1)

            def projections(L, pl):
                act.wait_ge(vecs_ready, L + 1)

                def keep_own(s, i, dst, col):
                    done(pl, s, i)
                    act.activation(dst, dbank[s % 2][:], ACT.Copy,
                                   scale=one_minus[:, bass.ds(col, 1)]).then_inc(shift_a, 1)

                for j in range(2):
                    keep_own(C_WAG + j, 0, wag[:, j, :], j)
                with act.Fori(0, 6) as i:
                    for j in range(2):
                        keep_own(C_KRV + j, i, krv[:, i * 2 + j, :], i * 2 + j + 2)
                act.wait_ge(n_aff, L * 16)
                for s, dst in zip(range(C_SB, C_UP), (sbq[:, 0, :], sbq[:, 1, :], sbk[:, 0, :],
                                                      sbk[:, 1, :], sbvT[:, 0, :], sbvT[:, 1, :],
                                                      cq[:, 0, :], cq[:, 1, :], ckv[:])):
                    done(pl, s)
                    act.activation(dst, dbank[s % 2][:], ACT.Copy)\
                       .then_inc(bank_free[s % 2], 1)

            def latent(L, pl):
                for s in (C_UP - 1, C_UP - 2):
                    act.wait_ge(bank_free[s % 2], pl.use(s) + 1)
                act.activation(csq[:, 0, :], cq[:, 0, :], ACT.Square)
                act.activation(csq[0:64, 1, :], cq[0:64, 1, :], ACT.Square)
                act.activation(csq[:, 2, :], ckv[:], ACT.Square).then_inc(csq_ready, 1)
                act.wait_ge(c_var, L + 1)
                act.activation(crs[:], crs[:], ACT.Ln).then_inc(c_sd, 1)
                act.wait_ge(c_sd, L * 2 + 1)
                act.activation(crs[:], crs[:], ACT.Exp, scale=-0.5).then_inc(c_sd, 1)
                act.wait_ge(vtok_pe, L + 1)
                for t in range(2):
                    act.activation(vsb[:, 2 * t:2 * t + 2, :].rearrange("p a b -> p (a b)"),
                                   aux[2 + t][:], ACT.Copy).then_inc(vtok_ready, 1)
                for n, (dst, src) in enumerate(((xh[:, 4, :], cq[:, 0, :]),
                                                (xh[0:64, 5, :], cq[0:64, 1, :]),
                                                (xh[:, 6, :], ckv[:]))):
                    act.wait_ge(c_norm, L * 3 + n + 1)
                    act.activation(dst, src, ACT.Copy).then_inc(ch_ready, 1)
                for h in range(4):
                    act.wait_ge(up_pe, L * 6 + h + 1)
                    act.activation(qh[0:64, h, :], aux[h][0:64, :], ACT.Copy).then_inc(up_act, 1)
                for p in range(2):
                    act.wait_ge(up_pe, L * 6 + 5 + p)
                    act.activation(kh[0:64, 2 * p, :], aux[4 + p][0:64, :], ACT.Copy)
                    act.activation(kh[0:64, 2 * p + 1, :], aux[4 + p][64:P, :], ACT.Copy)\
                       .then_inc(up_act, 1)
                for s in (C_UP, C_UP + 1):
                    done(pl, s)
                for t in range(2):
                    act.activation(vmla[:, 2 * t:2 * t + 2, :].rearrange("p a b -> p (a b)"),
                                   aux[t][:], ACT.Copy).then_inc(up_act, 1)

            def attention(L, pl):
                def weights(u):
                    kind, pair, i, e = UNITS[u]
                    n, z, b = (i + 1) * P, zbank[u % 3], u % 2
                    act.wait_ge(z_ready, L * NU + u + 1)
                    if u >= 2:
                        act.wait_ge(w_ready, L * NU + u - 1)
                    if kind == "sb":
                        act.activation(keep[:, b, 0:n], z[:, 0:n], ACT.Sigmoid, scale=-SB_SCALE)
                        act.activation(sig[:, b, 0:n], z[:, 0:n], ACT.Sigmoid, scale=SB_SCALE)\
                           .then_inc(w_act, 1)
                    else:
                        act.wait_ge(mx_ready, L * (NU // 2) + u - NU // 2 + 1)
                        act.activation(keep[:, b, 0:n], z[:, 0:n], ACT.Exp, scale=MLA_SCALE,
                                       bias=small[:, 2, b:b + 1],
                                       accum_out=small[:, 3, b:b + 1]).then_inc(w_act, 1)

                def turned(u):
                    n = (UNITS[u][2] + 1) * P
                    act.wait_ge(t_ready, L * NU + u + 1)
                    if u >= 2:
                        act.wait_ge(av_done, L * NU + u - 1)
                    act.activation(wT[:, u % 2, 0:n], aux[2][:, 0:n], ACT.Copy)\
                       .then_inc(wT_ready, 1)

                def pair_out(q):
                    act.wait_ge(av_done, L * NU + 8 * q + 8)
                    act.activation(xh[:, q, :], aux[4 + q % 2][:], ACT.Copy)\
                       .then_inc(mixh_ready, 1)

                for j in range(2):
                    act.wait_ge(bank_free[j], pl.use(C_WAG + j) + 1)
                act.activation(wag[0:64, 0, :], wag[0:64, 0, :], ACT.Tanh)
                act.activation(wag[:, 1, :], wag[:, 1, :], ACT.Sigmoid).then_inc(wag_ready, 1)
                act.wait_ge(wag_ready, L + 1)
                for j in range(2):
                    act.activation(xh[:, 4 + j, :], wag[:, j, :], ACT.Copy).then_inc(lh_ready, 1)

                def lora_out(n):
                    p, src = n // 3, dbank[n % 2][:]
                    if n < 11:
                        act.wait_ge(lora_pe, L * 11 + n + 1)
                    else:
                        act.wait_ge(pe_chunk, pl.chunk(C_LORA) + 1)
                    if n % 3 == 0:
                        if p >= 2:
                            act.wait_ge(cum_ready, L * 4 + p - 1)
                        a = act.activation(decay[:, p % 2, :], src, ACT.Sigmoid,
                                           bias=vec("w0", p))
                    elif n % 3 == 1:
                        a = act.activation(aa[:, p, :], src, ACT.Sigmoid, bias=vec("a0", p))
                    else:
                        a = act.activation(gg[:, p, :], src, ACT.Copy)
                    a.then_inc(lora_read, 1)

                weights(0)
                for u in range(NU):
                    if u + 1 < NU:
                        weights(u + 1)
                    turned(u)
                    if u - 1 in LORA_AT:
                        lora_out(u - 1 - LORA_AT[0])
                    if u == LORA_AT[-1] + 2:
                        done(pl, C_LORA)
                    if u >= 8 and u % 8 == 1:
                        pair_out(u // 8 - 1)
                pair_out(3)

            def recurrence_inputs(L, pl):
                act.wait_ge(mixl_ready, L * 8 + 4)
                for p in range(4):
                    act.wait_ge(kk0_ready, L * 4 + p + 1)
                    act.activation(tmp4[:, p, :], kk[:, p, :], ACT.Square)\
                       .then_inc(kksq_ready, 1)
                act.wait_ge(cum_ready, L * 4 + 4)
                act.activation(e1[:], cum[:], ACT.Exp, scale=-DECAY)
                act.activation(cum[:], cum[:], ACT.Exp, scale=DECAY).then_inc(e_ready, 1)
                for p in range(4):
                    act.wait_ge(ss_max, L * 4 + p + 1)
                    act.activation(tmp4[:, p, :], tmp4[:, p, :], ACT.Ln).then_inc(kn_sd, 1)
                act.wait_ge(kn_sd, L * 5 + 4)
                act.activation(tmp4[:], tmp4[:], ACT.Exp, scale=-0.5).then_inc(kn_sd, 1)

            def stage_block(b, names):
                for name in names:
                    a = act.activation(stage[:, "ABKRV".index(name)],
                                       HATS[name][:, :, bass.ts(b, P)], ACT.Copy)
                a.then_inc(stage_ready, 1)

            def recurrence_block(B, b, last):
                for n in range(3):
                    act.wait_ge(tok_pe, B * 3 + n + 1)
                    act.activation(tok[:, n, :], aux[n][:], ACT.Copy).then_inc(tok_ready, 1)
                for n in range(1, 6):
                    for g in range(2):
                        k = B * 10 + 2 * (n - 1) + g
                        act.wait_ge(p_pe, k + 1)
                        if n > 1:
                            act.wait_ge(q_pe, k - 1)
                        act.activation(px[:, 4 * g:4 * g + 4, :], bank4(aux[g]), ACT.Copy)\
                           .then_inc(p_read, 1)
                if not last:
                    stage_block(b + 1, "BKRV")
                for c in range(2):
                    rows = slice(64 * c, 64 * c + 64)
                    act.wait_ge(u0_pe, B * 2 + c + 1)
                    act.activation(u0[rows, :], aux[0][rows, :], ACT.Copy).then_inc(u0_read, 1)
                if not last:
                    stage_block(b + 1, "A")
                for q in range(2):
                    act.wait_ge(y_pe, B * 2 + q + 1)
                    for g in range(2):
                        r = slice(64 * g, 64 * g + 64)
                        src = aux[3 + q][r, :].rearrange("q (p g t) -> q p g t", p=2, g=2)
                        a = act.activation(yy[r, 2 * q:2 * q + 2, bass.ts(b, P)],
                                           src[:, :, g, :], ACT.Copy)
                    a.then_inc(y_read, 1)

            def group_norm(L):
                for q in range(2):
                    for r in range(2):
                        k = L * 4 + 2 * q + r + 1
                        act.wait_ge(yc_ready, k)
                        act.activation(ysq[:, r, :], yc[:, r, :], ACT.Square)\
                           .then_inc(ysq_ready, 1)
                    for r in range(2):
                        k = L * 4 + 2 * q + r + 1
                        act.wait_ge(gvar_ready, k)
                        act.activation(ysq[:, r, :], ysq[:, r, :], ACT.Ln)\
                           .then_inc(gsd_ready, 1)
                    act.wait_ge(gsd_ready, L * 6 + 3 * q + 2)
                    act.activation(ysq[:], ysq[:], ACT.Exp, scale=-0.5).then_inc(gsd_ready, 1)
                    for r in range(2):
                        p = 2 * q + r
                        act.wait_ge(gn_mul, L * 4 + p + 1)
                        act.activation(yc[:, r, :], yc[:, r, :], ACT.Identity,
                                       scale=vec("gn_g", p), bias=vec("gn_b", p))\
                           .then_inc(gn_aff, 1)
                    for r in range(2):
                        p = 2 * q + r
                        act.wait_ge(yf_ready, L * 4 + p + 1)
                        act.activation(xh[:, 4 + p, :], yc[:, r, :], ACT.Copy)\
                           .then_inc(mixh_ready, 1)

            def hidden_hi(ready, value, slot_i, j):
                act.wait_ge(ready, value)
                act.activation(hidh[:, slot_i, :], hf[:, j, :], ACT.Copy).then_inc(hidh_ready, 1)

            with act.Fori(0, DEPTH) as L:
                pl = place1(L)
                projections(L, pl)
                latent(L, pl)
                attention(L, pl)
                recurrence_inputs(L, pl)
                act.wait_ge(hats_ready, L + 1)
                act.wait_ge(rhat_ready, L + 1)
                stage_block(0, "BKRV")
                stage_block(0, "A")
                with act.Fori(0, BLOCKS - 1) as b:
                    recurrence_block(L * 4 + b, b, False)
                recurrence_block(L * 4 + BLOCKS - 1, BLOCKS - 1, True)
                group_norm(L)
                with act.Fori(0, KT // 2) as i:
                    for j in range(2):
                        done(pl, C_WO + j, i)
                        squares(pl, L * 2, C_WO + j, i * 2 + j, i, j)
                layer_norm(L * 2, "ln1_g", "ln1_b", 1)
                for g, tiles in enumerate(GROUPS1):
                    up, down = C_FFN[g]
                    with act.Fori(0, tiles) as i:
                        t = L * 22 + 8 * g + i
                        done(pl, up, i)
                        act.wait_ge(ua_zero, L + 1)
                        act.wait_ge(conv_done, t)
                        act.activation(ua[:, 2:S + 2], dbank[0][:], ACT.Copy)\
                           .then_inc(bank_free[0], 1)
                        act.wait_ge(conv_done, t + 1)
                        act.activation(gel[:], cv[:], ACT.Gelu, bias=vec("conv_b", 8 * g + i))\
                           .then_inc(gel_ready, 1)
                        done(pl, up + 1, i)
                        hidden_hi(bank_free[1], pl.use(up + 1, i) + 1, i, 0)
                    with act.Fori(0, KT // 2) as i:
                        for j in range(2):
                            done(pl, down + j, i)
                            if g == 2:
                                squares(pl, L * 2 + 1, down + j, i * 2 + j, i, j)
                layer_norm(L * 2 + 1, "ln2_g", "ln2_b", 2)

            pl = PLACE2
            H0 = DEPTH * 22
            act.wait_ge(n_aff, 32)

            def squares_now(k):
                for m in range(KT):
                    act.wait_ge(sums_tile, 8 * k + m + 1)
                    act.activation(sq[:, m % 2, :], x[:, m, :], ACT.Square).then_inc(sq_ready, 1)

            def modulated(k, scale, bias, hi=True):
                act.wait_ge(fold_ready, 1)
                norm_stats(k)
                for m in range(KT):
                    act.wait_ge(n_mul, 8 * k + m + 1)
                    act.activation(nt[:, m % 2, :], nt[:, m % 2, :], ACT.Identity,
                                   scale=scale(m), bias=bias(m)).then_inc(n_aff, 1)
                    if hi:
                        act.wait_ge(n_aff, 8 * k + m + 1)
                        split_hi(xh[:, m, :], nt[:, m % 2, :])

            squares_now(4)
            modulated(4, lambda m: small[:, 4, m:m + 1], lambda m: mod[:, 0, m:m + 1])
            with act.Fori(0, 4) as i:
                for j in range(2):
                    m = i * 2 + j
                    done(pl, C_Y + j, i)
                    act.activation(gate[:, m, :], dbank[j][:], ACT.Gelu_apprx_tanh,
                                   bias=vec2("b_y", m)).then_inc(bank_free[j], 1)
            with act.Fori(0, 4) as i:
                for j in range(2):
                    m = i * 2 + j
                    done(pl, C_IN + j, i)
                    act.wait_ge(xc_ready, m)
                    act.wait_ge(ua_zero, DEPTH + 1)
                    act.activation(ua[:, 3:S + 3], dbank[j][:], ACT.Identity,
                                   bias=vec2("b_in", m)).then_inc(bank_free[j], 1)
                    act.wait_ge(xc_ready, m + 1)
                    act.activation(hidh[:, m, :], xc[:, m, :], ACT.Copy).then_inc(hidh_ready, 1)
            def gates(h):
                done(pl, C_AX + h)
                o = 2 * (h % 2)
                if h >= 2:
                    act.wait_ge(h_ready, 2 * h - 2)
                for t in range(2):
                    act.activation(ga[:, o + t, :], aux[t][:], ACT.Sigmoid,
                                   bias=vec2("b_a", 2 * h + t)).then_inc(ax_read, 1)
                for t in range(2):
                    act.activation(gx[:, o + t, :], aux[2 + t][:], ACT.Sigmoid,
                                   bias=vec2("b_x", 2 * h + t)).then_inc(ax_read, 1)
                act.wait_ge(ax_read, 4 * h + 4)
                for t in range(2):
                    act.activation(tb[o + t], ga[:, o + t, :], ACT.Tanh,
                                   scale=small[:, 7, 2 * h + t:2 * h + t + 1])\
                       .then_inc(th_ready, 1)
                for t in range(2):
                    act.activation(ga[:, o + t, :], ga[:, o + t, :], ACT.Exp,
                                   scale=small[:, 6, 2 * h + t:2 * h + t + 1])\
                       .then_inc(a_ready, 1)
                for t in range(2):
                    act.wait_ge(a_ready, 2 * h + t + 1)
                    act.wait_ge(m2_ready, 2 * h)
                    act.activation(nt[:, t, :], ga[:, o + t, :], ACT.Square)\
                       .then_inc(a2_ready, 1)

            def roots(h):
                o = 2 * (h % 2)
                for t in range(2):
                    act.wait_ge(m2_ready, 2 * h + t + 1)
                    act.activation(tb[o + t], tb[o + t], ACT.Sqrt).then_inc(m_ready, 1)
                for t in range(2):
                    act.wait_ge(h_ready, 2 * h + t + 1)
                    split_hi(xh[:, 2 * h + t, :], xc[:, 2 * h + t, :])

            gates(0)
            for h in range(1, 4):
                gates(h)
                roots(h - 1)
            roots(3)

            def gated_add(s, i, m, j, scale, bias, k):
                done(pl, s, i)
                act.activation(nt[:, j, :], dbank[j][:], ACT.Identity, scale=scale(m),
                               bias=bias(m)).then_inc(bank_free[j], 1)

            with act.Fori(0, 4) as i:
                for j in range(2):
                    m = i * 2 + j
                    gated_add(C_OUT + j, i, m, j, lambda m: mod[:, 0, bass.ds(16 + m, 1)],
                              lambda m: small[:, 8, bass.ds(m, 1)], 5)
                    act.wait_ge(y_add, m + 1)
                    act.wait_ge(sums_tile, 8 * 5 + m + 1)
                    act.activation(sq[:, j, :], x[:, m, :], ACT.Square).then_inc(sq_ready, 1)

            def ffn2(c0, k, lay, hid0, last):
                modulated(k, lambda m: small[:, 5 if lay == 0 else 10, m:m + 1],
                          lambda m: mod[:, lay, 24 + m:25 + m])

                def group(pg, h0, stats, end):
                    with act.Fori(0, 4) as i:
                        for j in range(2):
                            done(pg, c0 + j, i)
                            t = h0 + i * 2 + j
                            act.wait_ge(hf_ready, t)
                            act.activation(gel[:], dbank[j][:], ACT.Relu)\
                               .then_inc(bank_free[j], 1)
                            hidden_hi(hf_ready, t + 1, i * 2 + j, j)

                    def down(i, more):
                        for j in range(2):
                            done(pg, c0 + 8 + j, i, more)
                            if stats:
                                squares(pg, k + 1, c0 + 8 + j, i * 2 + j, i, j)

                    with act.Fori(0, 3) as i:
                        down(i, True)
                    down(3, not end)

                with act.Fori(0, GROUPS2 - 1) as g:
                    group(Place(pl.pair0 + g * 8, [pl.use0[0] + g * 8, pl.use0[1] + g * 8],
                                pl.special), hid0 + g * 8, False, False)
                g = GROUPS2 - 1
                group(Place(pl.pair0 + g * 8, [u + g * 8 for u in pl.use0], pl.special),
                      hid0 + g * 8, True, last)

            ffn2(C_F0, 5, 0, 0, False)
            norm_stats(6)
            def modulate(m):
                act.wait_ge(n_mul, 8 * 6 + m + 1)
                act.activation(nt[:, m % 2, :], nt[:, m % 2, :], ACT.Identity,
                               scale=small[:, 9, m:m + 1], bias=mod[:, 1, m:m + 1])\
                   .then_inc(n_aff, 1)

            modulate(0)
            for m in range(KT):
                if m + 1 < KT:
                    modulate(m + 1)
                act.wait_ge(pooled_ready, m + 1)
                split_hi(xh[:, m, :], hp[:, m % 2, :])
            for c in range(2):
                done(pl, C_POOL + c)
                for o in range(4):
                    m = 4 * c + o
                    if m >= 2:
                        act.wait_ge(y_add, 8 + m - 1)
                    act.activation(nt[:, o % 2, :], aux[o][:], ACT.Copy,
                                   scale=small[:, 11, m:m + 1]).then_inc(ax_read, 1)
                    act.wait_ge(y_add, 8 + m + 1)
                    act.wait_ge(sums_tile, 8 * 7 + m + 1)
                    act.activation(sq[:, o % 2, :], x[:, m, :], ACT.Square).then_inc(sq_ready, 1)
            ffn2(C_F1, 7, 1, 32, True)
            norm_stats(8)
            for m in range(KT):
                act.wait_ge(n_mul, 8 * 8 + m + 1)
                act.activation(x[:, m, :], nt[:, m % 2, :], ACT.Copy,
                               scale=vec2("final_g", m)).then_inc(out_tile, 1)

        @block.vector
        def _(dve):
            chain = Chain(dve, dve_chain)
            tt, stt, ts = dve.tensor_tensor, dve.scalar_tensor_tensor, dve.tensor_scalar
            MUL, ADD, SUB = ALU.mult, ALU.add, ALU.subtract

            def prepare(n, slot):
                dve.wait_ge(hi_done, n + 1)
                tt(wl[:, slot].rearrange("p k m -> p (k m)"), raw[:, slot, :],
                   wh[:, slot].rearrange("p k m -> p (k m)").bitcast(F32), SUB)\
                    .then_inc(lo_done, 1)

            def done(pl, s, i=0, more=True):
                n = pl.chunk(s, i)
                if more:
                    prepare(n + 2, s % 2)
                dve.wait_ge(pe_chunk, n + 1)

            def low(dst, src, hi, ready):
                tt(dst, src, hi.bitcast(F32), SUB).then_inc(ready, 1)

            def norm_scale(k, centred, eps):
                dve.wait_ge(sums_pe, k + 1)
                mean, ex2, var, inv = stat[:, 0, 0:4], stat[:, 0, 4:8], stat[:, 1, 0:4], \
                    stat[:, 2, 0:4]
                if centred:
                    chain(ts(stat[:, 0, :], aux[4][:, 0:8], 1.0 / D, None, MUL))
                    chain(stt(var, mean, -1.0, mean, MUL, MUL))
                    chain(tt(var, var, ex2, ADD))
                    ts(inv, var, 0.0, eps, ALU.max, ADD).then_inc(var_ready, 1)
                else:
                    ts(inv, aux[4][:, 4:8], 1.0 / D, eps, MUL, ADD).then_inc(var_ready, 1)
                dve.wait_ge(sd_ready, k + 1)
                if centred:
                    chain(dve.reciprocal(inv, inv))
                    stt(stat[:, 3, 0:4], mean, -1.0, inv, MUL, MUL).then_inc(stat_ready, 1)
                else:
                    dve.reciprocal(inv, inv).then_inc(stat_ready, 1)
                dve.wait_ge(rows_pe, k + 1)

            def normal(m, centred):
                if centred:
                    chain(tt(nt[:, m % 2, :], x[:, m, :], aux[4][:], MUL))
                    tt(nt[:, m % 2, :], nt[:, m % 2, :], aux[5][:], ADD).then_inc(n_mul, 1)
                else:
                    tt(nt[:, m % 2, :], x[:, m, :], aux[4][:], MUL).then_inc(n_mul, 1)

            def norm_tiles(centred, xh_at, source):
                normal(0, centred)
                for m in range(KT):
                    if m + 1 < KT:
                        if m and not centred:
                            dve.wait_ge(xl_ready, xh_at + m)
                        normal(m + 1, centred)
                    dve.wait_ge(xh_ready, xh_at + m + 1)
                    low(xl[:, m, :], source(m), xh[:, m, :], xl_ready)

            for m in range(KT):
                dve.wait_ge(xh_ready, m + 1)
                low(xl[:, m, :], x[:, m, :], xh[:, m, :], xl_ready)
                if m in (0, 3):
                    prepare(m % 2, m % 2)
            dve.wait_ge(in_landed, 32)
            dve.wait_ge(cond_sig, 1)
            tt(cond[:], cond[:], pv2[:, V2["c"]:V2["c"] + 8], MUL).then_inc(cond_ready, 1)
            dve.wait_ge(cond_ready, 1)
            dve.wait_ge(lam_a, 1)
            chain(stt(small[:, 6, :], pv2[:, V2["lam"]:V2["lam"] + 8], 0.0, small[:, 1, :],
                      ALU.min, SUB))
            chain(ts(small[:, 6, :], small[:, 6, :], 8.0, None, MUL))
            chain(ts(small[:, 7, :], small[:, 6, :], -1.0, None, MUL))

            def projections(L, pl):
                dve.wait_ge(vecs_ready, L + 1)

                def add_previous(s, i, dst, col, k):
                    prepare(pl.chunk(s, i) + 2, s % 2)
                    dve.wait_ge(shift_a, L * 14 + k + 1)
                    stt(dst[:, 1:S] if not callable(dst) else dst(), dbank[s % 2][:, 0:S - 1],
                        vec("mu", col), dst[:, 1:S] if not callable(dst) else dst(), MUL, ADD)\
                        .then_inc(bank_free[s % 2], 1)

                for j in range(2):
                    add_previous(C_WAG + j, 0, wag[:, j, :], j, j)
                with dve.Fori(0, 6) as i:
                    for j in range(2):
                        k = i * 2 + j + 2
                        add_previous(C_KRV + j, i, lambda: krv[:, i * 2 + j, 1:S], k, k)
                for s in range(C_SB, C_UP):
                    prepare(pl.chunk(s) + 2, s % 2)

            def rope(dst, swapped, plain, c):
                tt(rope_t[64:96, 0, :], swapped, const("rope", slice(96, 128)), MUL)
                c(tt(rope_t[64:96, 1, :], plain, const("rope", slice(64, 96)), MUL))
                return tt(dst, rope_t[64:96, 0, :], rope_t[64:96, 1, :], ADD)

            def latent(L, pl):
                for s in (C_UP - 1, C_UP - 2):
                    dve.wait_ge(bank_free[s % 2], pl.use(s) + 1)
                rope(krot[64:96, :], cq[96:128, 1, :], cq[64:96, 1, :], chain)\
                    .then_inc(krot_ready, 1)
                dve.wait_ge(c_ms, L + 1)
                ts(crs[:, 0, :], aux[0][:], 1.0 / 192, RMS_EPS, MUL, ADD)
                ts(crs[:, 1, :], aux[1][:], 1.0 / 128, RMS_EPS, MUL, ADD).then_inc(c_var, 1)
                dve.wait_ge(c_sd, L * 2 + 2)
                stt(cq[:, 0, :], cq[:, 0, :], vec("q_norm", 0), crs[:, 0, :], MUL, MUL)\
                    .then_inc(c_norm, 1)
                stt(cq[0:64, 1, :], cq[0:64, 1, :], vec("q_norm", 1, slice(0, 64)),
                    crs[0:64, 0, :], MUL, MUL).then_inc(c_norm, 1)
                stt(ckv[:], ckv[:], vec("kv_norm", 0), crs[:, 1, :], MUL, MUL)\
                    .then_inc(c_norm, 1)
                for n, (r, t, src) in enumerate(((slice(0, P), 4, cq[:, 0, :]),
                                                 (slice(0, 64), 5, cq[0:64, 1, :]),
                                                 (slice(0, P), 6, ckv[:]))):
                    dve.wait_ge(ch_ready, L * 3 + n + 1)
                    low(xl[r, t, :], src, xh[r, t, :], cl_ready)
                for h in range(4):
                    dve.wait_ge(up_pe, L * 6 + h + 1)
                    if h:
                        dve.wait_ge(up_dve, L * 4 + h)
                    rope(qh[64:96, h, :], aux[h][96:128, :], aux[h][64:96, :], chain)\
                        .then_inc(up_dve, 1)
                for s in (C_UP, C_UP + 1):
                    prepare(pl.chunk(s) + 2, s % 2)

            def attention(L, pl):
                def row_max(u):
                    kind, pair, i, e = UNITS[u]
                    if kind == "sb":
                        return
                    b = u % 2
                    dve.wait_ge(z_ready, L * NU + u + 1)
                    dve.wait_ge(w_act, L * NU + u - 1)
                    chain(dve.reduce_max(small[:, 12, b:b + 1], zbank[u % 3][:, 0:(i + 1) * P], AX_X))
                    ts(small[:, 2, b:b + 1], small[:, 12, b:b + 1], -MLA_SCALE, None, MUL)\
                        .then_inc(mx_ready, 1)

                def weights(u):
                    kind, pair, i, e = UNITS[u]
                    n, b = (i + 1) * P, u % 2
                    dve.wait_ge(w_act, L * NU + u + 1)
                    if u >= 2:
                        dve.wait_ge(t_ready, L * NU + u - 1)
                    if kind == "sb":
                        k = keep[:, b, 1:n][:, ::-1]
                        chain(dve.tensor_tensor_scan(later[:, b, 0:n - 1][:, ::-1], k, k, 1.0,
                                                     MUL, ALU.min))
                        tt(wts[:, b, 0:n], later[:, b, 0:n], sig[:, b, 0:n], MUL)\
                            .then_inc(w_ready, 1)
                    else:
                        chain(dve.reciprocal(small[:, 13, b:b + 1], small[:, 3, b:b + 1]))
                        ts(wts[:, b, 0:n], keep[:, b, 0:n], small[:, 13, b:b + 1], None, MUL)\
                            .then_inc(w_ready, 1)

                def pair_out(q):
                    dve.wait_ge(mixh_ready, L * 8 + q + 1)
                    low(xl[:, q, :], aux[4 + q % 2][:], xh[:, q, :], mixl_ready)

                dve.wait_ge(up_act, L * 8 + 8)
                chain(dve.memset(later[:], 0.0))
                for j in range(2):
                    dve.wait_ge(lh_ready, L * 2 + j + 1)
                    low(xl[:, 4 + j, :], wag[:, j, :], xh[:, 4 + j, :], ll_ready)
                for u in range(NU):
                    if u + 1 < NU:
                        row_max(u + 1)
                    weights(u)
                    if u - 2 in LORA_AT[::3]:
                        p = (u - 2 - LORA_AT[0]) // 3
                        dve.wait_ge(lora_read, L * 12 + 3 * p + 1)
                        dve.tensor_tensor_scan(cum[:, p, :], const("chunk_mask"),
                                               decay[:, p % 2, :], 0.0, MUL, ADD)\
                            .then_inc(cum_ready, 1)
                    if u - 1 in BONUS_AT:
                        p = BONUS_AT.index(u - 1)
                        dve.wait_ge(bonus_pe, L * 4 + p + 1)
                        tt(bv[:, p, :], dbank[p % 2][:], krv[:, 8 + p, :], MUL)\
                            .then_inc(bonus_read, 1)
                    if u == LORA_AT[-1] + 3:
                        prepare(pl.chunk(C_LORA) + 2, C_LORA % 2)
                    if u >= 8 and u % 8 == 1:
                        pair_out(u // 8 - 1)
                pair_out(3)

            def recurrence_inputs(L, pl):
                k = krv[:, 0:4, :]
                for p in range(4):
                    dve.wait_ge(ss_pe, L * 4 + p + 1)
                    ts(tmp4[:, p, :], aux[p][:], 1e-12, None, ALU.max).then_inc(ss_max, 1)
                dve.wait_ge(e_ready, L + 1)
                tt(k, k, cum[:], MUL)
                chain(tt(aa[:], aa[:], cum[:], MUL))
                dve.wait_ge(kn_sd, L * 5 + 5)
                chain(tt(kk[:], kk[:], tmp4[:], MUL))
                chain(tt(aa[:], kk[:], aa[:], MUL))
                kc = kk[:].rearrange("q p (c t) -> q (p c) t", t=HD)
                ec = e1[:].rearrange("q p (c t) -> q (p c) t", t=HD)
                stt(kc[:, :, 1:HD], kc[:, :, 1:HD], -1.0, ec[:, :, 0:HD - 1], MUL, MUL)
                ts(kc[:, :, 0:1], kc[:, :, 0:1], -1.0, None, MUL)
                dve.tensor_copy(cc[:].rearrange("q p c -> q (p c)").unsqueeze(2),
                                ec[:, :, HD - 1:HD]).then_inc(hats_ready, 1)
                dve.wait_ge(hats_ready, L + 1)
                dve.memset(st[:, 0], 0.0).then_inc(zero_ready, 1)

            def recurrence_block(B, half):
                def turn(dst, src, hs):
                    return dve.transpose(dst[:, hs, :].rearrange("p h t -> p (h t)"),
                                         src[:, hs, :].rearrange("p h t -> p (h t)"))

                dve.wait_ge(eye_ready, B + 1)
                q = 0
                for name in ("mt", "n", "lb", "lk"):
                    for g in range(2):
                        hs = slice(4 * g, 4 * g + 4)
                        b = bank4(aux[(3 + q) % 6])
                        if name == "mt":
                            wait_apart(dve, mm5_pe, B * 8 + q + 1)
                            dve.copy_predicated(xiT[:, hs, :], mask("lev_xt").bitcast(I32), b)
                            tt(mt[:, hs, :], b, mask("upper"), MUL).then_inc(mm5_read, 1)
                            dve.wait_ge(mm5_read, B * 8 + q + 1)
                            turn(xi, xiT, hs).then_inc(xi_ready, 1)
                        else:
                            dve.wait_ge(mm5_pe, B * 8 + q + 1)
                            dst = {"n": nT, "lb": lbT, "lk": lkT}[name]
                            tt(dst[:, hs, :], b, mask("upper" if name == "n" else "upper_incl"),
                               MUL).then_inc(mm5_read, 1)
                        q += 1
                for n in range(1, 6):
                    for g in range(2):
                        hs = slice(4 * g, 4 * g + 4)
                        done_q = B * 10 + 2 * (n - 1) + g + 1
                        wait_apart(dve, q_pe, done_q)
                        dst, lev, b = (xi, "lev_x", 2) if n < 5 else (xiT, "lev_xt", 4)
                        dve.copy_predicated(dst[:, hs, :], mask(lev, n).bitcast(I32),
                                            bank4(aux[b + g])).then_inc(q_read, 1)
                        if n < 5:
                            dve.wait_ge(q_read, done_q)
                            turn(xiT, xi, hs).then_inc(xt_ready, 1)
                for c in range(2):
                    rows = slice(64 * c, 64 * c + 64)
                    s_in, s_out = (2 * half + c) % 4, (2 * half + c + 1) % 4
                    dve.wait_ge(u_pe, B * 2 + c + 1)
                    dve.tensor_copy(uu[rows, :], aux[1][rows, :]).then_inc(u_read, 1)
                    dve.wait_ge(s_pe, B * 2 + c + 1)
                    dve.wait_ge(mcc_ready, B + 1)
                    dve.wait_ge(state_ready, B * 2 + c)
                    tt(st[:, s_out], bank4(aux[2]), st[:, s_in], ADD).then_inc(st_sum, 1)
                    dve.wait_ge(st_sum, B * 2 + c + 1)
                    tt(st[:, s_out], st[:, s_out], mcc[:, c], MUL).then_inc(state_ready, 1)

            def group_norm(L):
                for q in range(2):
                    for r in range(2):
                        p = 2 * q + r
                        dve.wait_ge(gm_pe, L * 4 + p + 1)
                        if q:
                            dve.wait_ge(mixl_ready, L * 8 + 4 + p - 1)
                        stt(yc[:, r, :], aux[r][:], -1.0 / HD, yy[:, p, :], MUL, ADD)\
                            .then_inc(yc_ready, 1)
                    for r in range(2):
                        dve.wait_ge(gv_pe, L * 4 + 2 * q + r + 1)
                        ts(ysq[:, r, :], aux[2 + r][:], 1.0 / HD, GN_EPS, MUL, ADD)\
                            .then_inc(gvar_ready, 1)
                    for r in range(2):
                        dve.wait_ge(gsd_ready, L * 6 + 3 * q + 3)
                        tt(yc[:, r, :], yc[:, r, :], ysq[:, r, :], MUL).then_inc(gn_mul, 1)
                    for r in range(2):
                        p = 2 * q + r
                        dve.wait_ge(gn_aff, L * 4 + p + 1)
                        chain(tt(yc[:, r, :], yc[:, r, :], bv[:, p, :], ADD))
                        tt(yc[:, r, :], yc[:, r, :], gg[:, p, :], MUL).then_inc(yf_ready, 1)
                    for r in range(2):
                        p = 2 * q + r
                        dve.wait_ge(mixh_ready, L * 8 + 4 + p + 1)
                        low(xl[:, 4 + p, :], yc[:, r, :], xh[:, 4 + p, :], mixl_ready)

            def residual(pl, s, i, m, alpha):
                if alpha:
                    stt(x[:, m, :], x[:, m, :], ALPHA, dbank[s % 2][:], MUL, ADD)\
                        .then_inc(bank_free[s % 2], 1)
                else:
                    tt(x[:, m, :], x[:, m, :], dbank[s % 2][:], ADD)\
                        .then_inc(bank_free[s % 2], 1)

            with chain.loop(DEPTH, PER["layer"]) as L:
                pl = place1(L)
                projections(L, pl)
                latent(L, pl)
                attention(L, pl)
                recurrence_inputs(L, pl)
                with dve.Fori(0, 2) as i:
                    for half in range(2):
                        recurrence_block(L * 4 + i * 2 + half, half)
                group_norm(L)
                with dve.Fori(0, 4) as i:
                    for j in range(2):
                        done(pl, C_WO + j, i)
                        residual(pl, C_WO + j, i, i * 2 + j, True)
                norm_scale(L * 2, True, LN_EPS)
                norm_tiles(True, L * 16 + 8, lambda m: x[:, m, :])
                for g, tiles in enumerate(GROUPS1):
                    up, down = C_FFN[g]

                    def mod_times_cond(off, i, j):
                        if g == 2:
                            return
                        pairs = L * MODS + (g * MODS + off) // 2 + i
                        dve.wait_ge(mod_landed[j], (pairs + 1) * 16)
                        tt(mraw[:, j], mraw[:, j], cond[:].unsqueeze(2)
                           .to_broadcast([P, KT, P]), MUL).then_inc(mod_mul, 1)

                    with chain.loop(tiles, 2) as i:
                        t = L * 22 + 8 * g + i
                        mod_times_cond(0, i, 0)
                        done(pl, up, i)
                        dve.wait_ge(bank_free[0], pl.use(up, i) + 1)
                        dve.wait_ge(gel_ready, t)
                        m = i + 8 * g
                        chain(ts(cv[:], ua[:, 2:S + 2], vec("conv2", m), None, MUL))
                        chain(stt(cv[:], ua[:, 1:S + 1], vec("conv1", m), cv[:], MUL, ADD))
                        stt(cv[:], ua[:, 0:S], vec("conv0", m), cv[:], MUL, ADD)\
                            .then_inc(conv_done, 1)
                        mod_times_cond(0, i, 1)
                        done(pl, up + 1, i)
                        dve.wait_ge(gel_ready, t + 1)
                        tt(hf[:, 0, :], gel[:], dbank[1][:], MUL).then_inc(bank_free[1], 1)
                        dve.wait_ge(hidh_ready, t + 1)
                        low(hidl[:, i, :], hf[:, 0, :], hidh[:, i, :], hidl_ready)
                    with dve.Fori(0, 4) as i:
                        for j in range(2):
                            mod_times_cond(16, i, j)
                            done(pl, down + j, i)
                            residual(pl, down + j, i, i * 2 + j, g == 0)
                dve.wait_ge(mod_pe, (L + 1) * 2 * MODS)
                tt(mod[:, bass.ds(L, 1), :].rearrange("p l c -> p (l c)"), aux[0][:, 0:48],
                   pv2[:, bass.ds(V2["b_mod"] + L * 48, 48)], ADD).then_inc(mod_out, 1)
                norm_scale(L * 2 + 1, True, LN_EPS)
                norm_tiles(True, L * 16 + 16, lambda m: x[:, m, :])

            pl = PLACE2
            H0 = DEPTH * 22
            dve.wait_ge(mod_out, DEPTH)

            def fold(dst, l, at, gain):
                return stt(small[:, dst, :], mod[:, l, at:at + 8], 1.0, gain, ADD, MUL)

            def gain(name, l):
                return pv2[:, V2[name] + 8 * l:V2[name] + 8 * l + 8]

            fold(4, 0, 8, gain("mix_g", 0))
            fold(5, 0, 32, gain("ffn_g", 0))
            fold(9, 1, 8, gain("mix_g", 1))
            fold(10, 1, 32, gain("ffn_g", 1))
            tt(small[:, 8, :], mod[:, 0, 16:24], gain("b_out", 0), MUL)
            tt(small[:, 11, :], mod[:, 1, 16:24], gain("pool_scale", 0), MUL)\
                .then_inc(fold_ready, 1)

            norm_scale(4, False, RMS_EPS)
            norm_tiles(False, 40, lambda m: nt[:, m % 2, :])
            with dve.Fori(0, 4) as i:
                for j in range(2):
                    done(pl, C_Y + j, i)
            with chain.loop(4, 6) as i:
                for j in range(2):
                    m = i * 2 + j
                    done(pl, C_IN + j, i)
                    dve.wait_ge(bank_free[j], pl.use(C_IN + j, i) + 1)
                    chain(ts(xc[:, m, :], ua[:, 3:S + 3], vec2("conv3", m), vec2("conv_b", m),
                             MUL, ADD))
                    chain(stt(xc[:, m, :], ua[:, 2:S + 2], vec2("conv2", m), xc[:, m, :],
                              MUL, ADD))
                    chain(stt(xc[:, m, :], ua[:, 1:S + 1], vec2("conv1", m), xc[:, m, :],
                              MUL, ADD))
                    stt(xc[:, m, :], ua[:, 0:S], vec2("conv0", m), xc[:, m, :], MUL, ADD)\
                        .then_inc(xc_ready, 1)
                    dve.wait_ge(hidh_ready, H0 + m + 1)
                    low(hidl[:, m, :], xc[:, m, :], hidh[:, m, :], hidl_ready)
            def one_minus_a2(h):
                done(pl, C_AX + h)
                for t in range(2):
                    dve.wait_ge(th_ready, 2 * h + t + 1)
                    dve.wait_ge(a2_ready, 2 * h + t + 1)
                    b = tb[2 * (h % 2) + t]
                    stt(b, nt[:, t, :], 1.0, b, ADD, MUL).then_inc(m2_ready, 1)

            def scan(h):
                for t in range(2):
                    m, o = 2 * h + t, 2 * (h % 2) + t
                    dve.wait_ge(m_ready, m + 1)
                    dve.wait_ge(gx_ready, m + 1)
                    chain(tt(gx[:, o, :], gx[:, o, :], tb[o], MUL))
                    chain(dve.tensor_tensor_scan(xc[:, m, :], ga[:, o, :], gx[:, o, :], 0.0,
                                                 MUL, ADD))
                    tt(xc[:, m, :], xc[:, m, :], gate[:, m, :], MUL).then_inc(h_ready, 1)
                for t in range(2):
                    m = 2 * h + t
                    dve.wait_ge(xh_ready, 48 + m + 1)
                    low(xl[:, m, :], xc[:, m, :], xh[:, m, :], xl_ready)

            one_minus_a2(0)
            for h in range(1, 4):
                one_minus_a2(h)
                scan(h - 1)
            scan(3)
            with dve.Fori(0, 4) as i:
                for j in range(2):
                    m = i * 2 + j
                    done(pl, C_OUT + j, i)
                    dve.wait_ge(bank_free[j], pl.use(C_OUT + j, i) + 1)
                    tt(x[:, m, :], x[:, m, :], nt[:, j, :], ADD).then_inc(y_add, 1)

            def ffn2(c0, k, lay, xh_at, hid0, hidh0, last):
                norm_scale(k, False, RMS_EPS)
                norm_tiles(False, xh_at, lambda m: nt[:, m % 2, :])

                def group(pg, h0, end):
                    with dve.Fori(0, 4) as i:
                        for j in range(2):
                            t = h0 + i * 2 + j
                            done(pg, c0 + j, i)
                            dve.wait_ge(bank_free[j], pg.use(c0 + j, i) + 1)
                            tt(hf[:, j, :], gel[:], gel[:], MUL).then_inc(hf_ready, 1)
                            dve.wait_ge(hidh_ready, t + hidh0 + 1)
                            low(hidl[:, i * 2 + j, :], hf[:, j, :], hidh[:, i * 2 + j, :],
                                hidl_ready)

                    def down(i, more):
                        for j in range(2):
                            m = i * 2 + j
                            done(pg, c0 + 8 + j, i, more)
                            stt(x[:, m, :], dbank[j][:], mod[:, lay, bass.ds(40 + m, 1)],
                                x[:, m, :], MUL, ADD).then_inc(bank_free[j], 1)

                    with dve.Fori(0, 3) as i:
                        down(i, True)
                    down(3, not end)

                with dve.Fori(0, GROUPS2 - 1) as g:
                    group(Place(pl.pair0 + g * 8, [pl.use0[0] + g * 8, pl.use0[1] + g * 8],
                                pl.special), hid0 + g * 8, False)
                g = GROUPS2 - 1
                group(Place(pl.pair0 + g * 8, [u + g * 8 for u in pl.use0], pl.special),
                      hid0 + g * 8, last)

            ffn2(C_F0, 5, 0, 56, 0, H0 + 8, False)
            norm_scale(6, False, RMS_EPS)
            chain(dve.memset(cs[:, :, 0:16], 0.0))
            normal(0, False)

            def pooled(m):
                dve.wait_ge(window_ready, m + 1)
                stt(hp[:, m % 2, :], hp[:, m % 2, :], 1.0 / POOL_WINDOWS[m // 2],
                    nt[:, m % 2, :], MUL, SUB).then_inc(pooled_ready, 1)
                dve.wait_ge(xh_ready, 64 + m + 1)
                low(xl[:, m, :], hp[:, m % 2, :], xh[:, m, :], xl_ready)

            for m in range(KT):
                dve.wait_ge(n_aff, 8 * 6 + m + 1)
                if m >= 2:
                    dve.wait_ge(window_ready, m - 1)
                dve.tensor_tensor_scan(cs[:, m % 2, 16:S + 16],
                                       const("ones", n=1).to_broadcast([P, S]),
                                       nt[:, m % 2, :], 0.0, MUL, ADD).then_inc(cs_ready, 1)
                if m:
                    pooled(m - 1)
                if m + 1 < KT:
                    if m:
                        dve.wait_ge(pooled_ready, m)
                    normal(m + 1, False)
            pooled(KT - 1)
            for c in range(2):
                done(pl, C_POOL + c)
                for o in range(4):
                    m = 4 * c + o
                    dve.wait_ge(ax_read, 16 + m + 1)
                    tt(x[:, m, :], x[:, m, :], nt[:, o % 2, :], ADD).then_inc(y_add, 1)
            ffn2(C_F1, 7, 1, 72, 32, H0 + 8, True)
            norm_scale(8, False, RMS_EPS)
            for m in range(KT):
                if m >= 2:
                    dve.wait_ge(out_tile, m - 1)
                normal(m, False)

        @block.gpsimd
        def _(pool):
            chain = Chain(pool, pool_chain, wait_apart)
            for n, s in enumerate((mod_red, mod_red, sums_tile, sums_tile)):
                pool.memset(small[:, 14, n:n + 1], 0.0).then_inc(s, 1)
            pool.wait_ge(in_landed, 32)

            def clear_sums(k, ready, value, centred=False):
                pool.wait_ge(sums_pe, k)
                wait_apart(pool, ready, value)
                if centred:
                    pool.memset(norm_sum[:], 0.0)
                chain(pool.memset(norm_sq[:], 0.0))

            def sum_tiles(k, centred=False):
                with pool.Fori(0, 4) as i:
                    for j in range(2):
                        m = i * 2 + j
                        pool.wait_ge(sq_ready, 8 * k + m + 1)
                        pool.wait_ge(sums_tile, 8 * k + m + 2)
                        if centred:
                            pool.tensor_tensor(norm_sum[:], norm_sum[:], x[:, m, :], ALU.add)
                        pool.tensor_tensor(norm_sq[:], norm_sq[:], sq[:, j, :], ALU.add)\
                            .then_inc(sums_tile, 1)

            with chain.loop(DEPTH, PER["pool"]) as L:
                pool.wait_ge(vecs_landed, 16 * (L + 1))
                wait_apart(pool, n_aff, L * 16)
                chain(pool.tensor_copy(pv[:], pv_next[:]))
                pool.tensor_scalar(one_minus[:, 0:14], pv[:, V1["mu"]:V1["mu"] + 14], -1.0, 1.0,
                                   ALU.mult, ALU.add)
                pool.tensor_scalar(one_minus[:, 14:18], pv[:, V1["k_a"]:V1["k_a"] + 4], -1.0, 1.0,
                                   ALU.mult, ALU.add).then_inc(vecs_ready, 1)
                wait_apart(pool, krot_ready, L + 1)
                for h in range(4):
                    t = pool.tensor_copy(kh[64:96, h, :], krot[64:96, :])
                t.then_inc(kh_rope, 1)
                pool.wait_ge(up_dve, L * 4 + 4)
                pool.wait_ge(up_act, L * 8 + 8)
                wait_apart(pool, kh_rope, L + 1)
                for p in range(4):
                    pool.tensor_scalar(kk[:, p, :], krv[:, p, :], vec("k_k", p), None, ALU.mult)\
                        .then_inc(kk0_ready, 1)
                pool.wait_ge(cum_ready, L * 4 + 4)
                wait_apart(pool, lora_read, L * 12 + 12)
                for p in range(4):
                    b = decay[:, p % 2, :]
                    if p >= 2:
                        wait_apart(pool, bonus_pe, L * 4 + p - 1)
                    chain(pool.tensor_scalar(b, aa[:, p, :], vec("k_a", p),
                                             one_minus[:, 14 + p:15 + p], ALU.mult, ALU.add))
                    chain(pool.tensor_tensor(krv[:, p, :], krv[:, p, :], b, ALU.mult))
                    chain(pool.tensor_scalar(b, krv[:, 4 + p, :], vec("r_k", p), None, ALU.mult))
                    pool.tensor_tensor(b, b, krv[:, p, :], ALU.mult).then_inc(rkk_ready, 1)
                eye = heads4(const("ident"))

                def start_x(ready, value):
                    wait_apart(pool, ready, value)
                    for g in range(2):
                        c = pool.tensor_copy(xiT[:, 4 * g:4 * g + 4, :], eye)
                    c.then_inc(eye_ready, 1)

                start_x(mixl_ready, L * 8 + 4)
                pool.wait_ge(e_ready, L + 1)
                pool.tensor_tensor(krv[:, 4:8, :], krv[:, 4:8, :], e1[:], ALU.mult)\
                    .then_inc(rhat_ready, 1)
                pool.wait_ge(hats_ready, L + 1)

                def chunk_decays(b):
                    for c in range(2):
                        t = pool.tensor_tensor(mcc[:, c], heads4(const("heads")),
                                               cc[:, :, bass.ds(b * 2 + c, 1)]
                                               .to_broadcast([P, 4, P]), ALU.mult)
                    t.then_inc(mcc_ready, 1)

                chunk_decays(0)
                with pool.Fori(1, BLOCKS) as b:
                    B = L * 4 + b
                    start_x(u_pe, B * 2)
                    pool.wait_ge(state_ready, B * 2)
                    chunk_decays(b)
                clear_sums(L * 2, mixl_ready, L * 8 + 8, True)
                pool.memset(ua[:, 0:3], 0.0).then_inc(ua_zero, 1)
                sum_tiles(L * 2, True)
                with chain.loop(MODS, 4) as i:
                    for j in range(2):
                        m = L * 2 * MODS + i * 2 + j
                        pool.wait_ge(mod_mul, m + 1)
                        w = mraw[:, j]
                        chain(pool.tensor_tensor(w[:, 0:4], w[:, 0:4], w[:, 4:8], ALU.add))
                        chain(pool.tensor_tensor(w[:, 0:2], w[:, 0:2], w[:, 2:4], ALU.add))
                        pool.wait_ge(mod_pe, m)
                        pool.tensor_tensor(mred[:, j, :], w[:, 0], w[:, 1], ALU.add)\
                            .then_inc(mod_red, 1)
                clear_sums(L * 2 + 1, n_aff, L * 16 + 8, True)
                sum_tiles(L * 2 + 1, True)
            def window(m):
                h, win, c = hp[:, m % 2, :], POOL_WINDOWS[m // 2], cs[:, m % 2, :]
                pool.wait_ge(cs_ready, m + 1)
                if m >= 2:
                    pool.wait_ge(xl_ready, 64 + m - 1)
                chain(pool.tensor_tensor(h, c[:, 16:S + 16], c[:, 16 - win:S + 16 - win],
                                         ALU.subtract))
                pool.tensor_tensor(h[:, 0:16], h[:, 0:16],
                                   const("pool_fix", n=16, off=16 * (m // 2)), ALU.mult)\
                    .then_inc(window_ready, 1)

            def gated_inputs():
                for h in range(4):
                    pool.wait_ge(ax_read, 4 * h + 4)
                    for t in range(2):
                        o = 2 * (h % 2) + t
                        pool.tensor_tensor(gx[:, o, :], gx[:, o, :], xc[:, 2 * h + t, :],
                                           ALU.mult).then_inc(gx_ready, 1)

            for k, ready, value in ((4, n_aff, 32), (5, xc_ready, 8), (6, n_aff, 48),
                                    (7, n_aff, 56), (8, n_aff, 64)):
                if k == 5:
                    pool.wait_ge(xc_ready, 8)
                    gated_inputs()
                if k == 7:
                    for m in range(KT):
                        window(m)
                clear_sums(k, ready, value)
                if k == 4:
                    pool.memset(ua[:, 0:3], 0.0).then_inc(ua_zero, 1)
                sum_tiles(k)


def rows(a, k0, n=P):
    r = np.zeros((n, a.shape[1]), np.float32)
    part = a[k0:k0 + n]
    r[:part.shape[0]] = part
    return r


def chunk_of(w, cols, k0=0, tiles=KT):
    c = np.zeros((P, KT, P), np.float32)
    for k in range(tiles):
        c[:, k, :] = w[k0 + k * P:k0 + (k + 1) * P, cols]
    return c.reshape(P, CHUNK)


def weight_stream(a):
    out = np.zeros((CHUNKS, P, CHUNK), np.float32)
    R0 = 768 + 352
    for l in range(DEPTH):
        o = out[l * LC:(l + 1) * LC]
        w = a["w_in"][l]
        cols = np.arange(w.shape[1])
        tiles = [cols[R0 + 1536:R0 + 1664], cols[R0 + 1664:R0 + 1792]]
        for base in (R0 + 512, R0, R0 + 1024):
            tiles += [cols[base + P * t:base + P * (t + 1)] for t in range(4)]
        tiles += [cols[P * t:P * (t + 1)] for t in range(6)]
        rope = cols[768 + 320:768 + 352]
        swapped = np.concatenate([rope[16:], rope[:16]])
        tiles += [cols[768:896], np.concatenate([cols[896:960], rope, swapped]),
                  cols[960:1088]]
        for s, c in enumerate(tiles):
            o[s] = chunk_of(w, c)
        uq, ukv = a["mla_w_uq"][l], a["mla_w_ukv"][l]
        q_cols = []
        for h in range(4):
            c = np.arange(96 * h, 96 * h + 96)
            q_cols += [c, np.concatenate([c[80:96], c[64:80]])]
        q_cols = np.concatenate(q_cols)
        kv_cols = np.concatenate([np.arange(128 * h, 128 * h + 64) for h in range(4)]
                                 + [np.arange(128 * h + 64, 128 * h + 128) for h in range(4)])
        o[C_UP, :, 0:512] = uq[0:128][:, q_cols]
        o[C_UP, :, 512:1024] = ukv[:, kv_cols]
        o[C_UP + 1, 0:64, 0:512] = uq[128:192][:, q_cols]
        o[C_LORA, 0:64, 0:512] = a["rwkv_w2"][l]
        o[C_LORA, 64:128, 0:512] = a["rwkv_a2"][l]
        o[C_LORA, :, 512:1024] = a["rwkv_g2"][l]
        for m in range(KT):
            o[C_WO + m] = chunk_of(a["w_o"][l], slice(m * P, (m + 1) * P))
        up_w, down_w = a["ffn_w_up"][l], a["ffn_w_down"][l]
        for g, n in enumerate(GROUPS1):
            up, down = C_FFN[g]
            for t in range(n):
                f = (8 * g + t) * P
                o[up + 2 * t] = chunk_of(up_w, slice(f, f + P))
                o[up + 2 * t + 1] = chunk_of(up_w, slice(F1 + f, F1 + f + P))
            for m in range(KT):
                o[down + m] = chunk_of(down_w, slice(m * P, (m + 1) * P), 8 * g * P, n)
    o = out[DEPTH * LC:]
    for m in range(KT):
        c = slice(m * P, (m + 1) * P)
        o[C_Y + m] = chunk_of(a["lru_w_y_2"][0], c)
        o[C_IN + m] = chunk_of(a["lru_w_in_2"][0], c)
        o[C_OUT + m] = chunk_of(a["lru_w_out_2"][0], c)

    def square(w):
        return w.reshape(2, P, 2, P).transpose(1, 2, 0, 3).reshape(P, 512)

    for h in range(4):
        o[C_AX + h] = np.concatenate([square(a["lru_w_a_2"][0, h]), square(a["lru_w_x_2"][0, h])], 1)
    for c in range(2):
        o[C_POOL + c] = np.concatenate([square(a["pool_w_2"][0, 2 * c + g]) for g in range(2)], 1)
    for l, c0 in enumerate((C_F0, C_F1)):
        w1, w2 = a["ffn_w1_2"][l], a["ffn_w2_2"][l]
        for g in range(GROUPS2):
            for t in range(8):
                f = (8 * g + t) * P
                o[c0 + 16 * g + t] = chunk_of(w1, slice(f, f + P))
                o[c0 + 16 * g + 8 + t] = chunk_of(w2, slice(t * P, (t + 1) * P), 8 * g * P)
    return out


def feature_columns(vecs, total, values):
    out = np.zeros((P, total), np.float32)
    at = 0
    for name, n in vecs:
        v = np.zeros(n * P, np.float32)
        flat = np.ravel(values[name])
        v[:flat.size] = flat
        out[:, at:at + n] = v.reshape(n, P).T
        at += n
    return out


def kernel(**inputs):
    import concourse.bacc as bacc
    from concourse.bass_utils import run_bass_kernel_spmd

    a = {k: np.asarray(v) for k, v in inputs.items()}
    vecs1 = []
    for l in range(DEPTH):
        mu = a["rwkv_mu"][l]
        mu = np.concatenate([mu[1536:], mu[512:1024], mu[0:512], mu[1024:1536]])
        v = {"mu": mu, "w0": a["rwkv_w0"][l], "a0": a["rwkv_a0"][l], "k_k": a["rwkv_k_k"][l],
             "k_a": a["rwkv_k_a"][l], "r_k": a["rwkv_r_k"][l], "gn_g": a["rwkv_gn_g"][l],
             "gn_b": a["rwkv_gn_b"][l], "q_norm": a["mla_q_norm"][l],
             "kv_norm": a["mla_kv_norm"][l], "ln1_g": a["ln1_g"][l], "ln1_b": a["ln1_b"][l],
             "conv_b": a["ffn_conv_b"][l], "ln2_g": a["ln2_g"][l], "ln2_b": a["ln2_b"][l]}
        for t in range(3):
            v[f"conv{t}"] = a["ffn_conv_w"][l, t]
        vecs1.append(feature_columns(LAYER_VECS, NV1, v))
    v = {"c": a["c_2"], "b_mod": a["b_mod_2"], "mix_g": a["norm_mix_g_2"],
         "ffn_g": a["norm_ffn_g_2"], "b_y": a["lru_b_y_2"], "b_in": a["lru_b_in_2"],
         "conv_b": a["lru_conv_b_2"], "b_a": a["lru_b_a_2"], "b_x": a["lru_b_x_2"],
         "lam": a["lru_lambda_2"], "b_out": a["lru_b_out_2"], "pool_scale": a["pool_scale_2"],
         "final_g": a["final_norm_g_2"]}
    for t in range(4):
        v[f"conv{t}"] = a["lru_conv_w_2"][0, t]
    w_mod = a["w_mod_2"].reshape(DEPTH, KT, P, 48, P).transpose(0, 3, 2, 1, 4)
    arrays = {
        "x_t": np.ascontiguousarray(a["x"][0].T.reshape(KT, P, S).transpose(1, 0, 2)),
        "stream": weight_stream(a),
        "mod_stream": np.ascontiguousarray(w_mod.reshape(DEPTH * 48, P, KT, P)),
        "vecs1": np.stack(vecs1),
        "vecs2": feature_columns(VECS2, NV2, v),
        "consts": constants(),
    }
    nc = bacc.Bacc("TRN2", target_bir_lowering=False, num_devices=1)
    args = [nc.dram_tensor(n, v.shape, F32, kind="ExternalInput").ap() for n, v in arrays.items()]
    out = nc.dram_tensor("y_t", (KT, P, S), F32, kind="ExternalOutput").ap()
    build(nc, *args, out)
    r = run_bass_kernel_spmd(nc, [arrays], core_ids=[0])
    y = r.results[0]["y_t"]
    return np.ascontiguousarray(y.reshape(D, S).T[None])
```
